# Optimizing a Trainium2 kernel written in Bass

```python
import jax
import jax.numpy as jnp
from jax import lax
import numpy as np

D_MODEL = 1024
BATCH = 1
SEQ = 128
DEPTH = 1
DEC_BATCH = 1
DEC_SEQ = 1024
PAST_LEN = 128

GRID_W = 64
N_DIR = 2
A_GROUPS = 4
A_GC = 64
A_W = A_GROUPS * A_GC
CHUNK = 128
ROWS_PER_CHUNK = CHUNK // GRID_W
B_H = 6
B_DK = 64
B_DV = 64
B_W = B_H * B_DV
MLSTM_CHUNK = 64
C_H = 6
C_N = 64
C_W = C_H * C_N
DECAY_RANK = 64
ICLR_RANK = 64
GATE_RANK = 128
MIX_W = A_W + B_W + C_W
D_FF = 4 * D_MODEL
N_MOD = 6
EPS = 1e-6
HEAD_EPS = 1e-5
OFF_A = 0
OFF_QK = OFF_A + 2 * A_W
OFF_V = OFF_QK + 2 * B_H * B_DK
OFF_O = OFF_V + B_W
OFF_G = OFF_O + B_W
OFF_C = OFF_G + N_DIR * 2 * B_H
C_COLS = 3 * C_W + N_DIR * DECAY_RANK + N_DIR * ICLR_RANK + GATE_RANK
IN_COLS = OFF_C + C_COLS
C_SPLITS = [C_W, 2 * C_W, 3 * C_W, 3 * C_W + N_DIR * DECAY_RANK, 3 * C_W + N_DIR * (DECAY_RANK + ICLR_RANK)]

kernel_name = 'hybrid_gmlp_mlstm_rwkv7_diffusion_step'

def _rmsnorm(x, g):
    xf = x.astype(jnp.float32)
    y = xf * lax.rsqrt(jnp.mean(xf * xf, axis=-1, keepdims=True) + EPS)
    return (y * g.astype(jnp.float32)).astype(x.dtype)

def _head_norm(x, g, n_heads):
    shp = x.shape
    xf = x.astype(jnp.float32).reshape(shp[:-1] + (n_heads, shp[-1] // n_heads))
    mu = jnp.mean(xf, axis=-1, keepdims=True)
    var = jnp.mean(jnp.square(xf - mu), axis=-1, keepdims=True)
    y = ((xf - mu) * lax.rsqrt(var + HEAD_EPS)).reshape(shp)
    return y * g.astype(jnp.float32)

def _shift_prev(x):
    return jnp.pad(x, ((0, 0), (1, 0), (0, 0)))[:, :-1]

def _shift_next(x):
    return jnp.pad(x, ((0, 0), (0, 1), (0, 0)))[:, 1:]

def _orient(a, axis):
    return jnp.stack([a[0], jnp.flip(a[1], axis=axis - 1)])

def _chunk_gmlp(z, ln_g, w_s, b_s, n_chunks):
    bsz, t, _ = z.shape
    u, v = jnp.split(jax.nn.gelu(z), 2, axis=-1)
    v = _head_norm(v, ln_g, A_GROUPS).reshape(bsz, n_chunks, CHUNK, A_GROUPS, A_GC)
    sv = jnp.einsum('gts,bnsgc->bntgc', w_s, v) + b_s.T[:, :, None]
    y = u.reshape(sv.shape) * sv
    return y.reshape(bsz, t, A_W).astype(z.dtype)

def _mlstm_scan(q, k, v, log_i, log_f, C0, n0, m0):
    r_, b_, h_, t, _ = q.shape
    nc = t // MLSTM_CHUNK

    def chunks(a):
        a = a.reshape(a.shape[:3] + (nc, MLSTM_CHUNK) + a.shape[4:])
        return jnp.moveaxis(a, 3, 0)

    tri = jnp.tril(jnp.ones((MLSTM_CHUNK, MLSTM_CHUNK), dtype=bool))

    def step(carry, inp):
        C, n, m = carry
        qc, kc, vc, ic, fc = inp
        b = jnp.cumsum(fc, axis=-1)
        logw = jnp.where(tri, b[..., :, None] - b[..., None, :] + ic[..., None, :], -jnp.inf)
        log_inter = b + m[..., None]
        m_t = jnp.maximum(jnp.max(logw, axis=-1), log_inter)
        s = jnp.einsum('rbhtd,rbhsd->rbhts', qc, kc) * jnp.exp(logw - m_t[..., None])
        g_inter = jnp.exp(log_inter - m_t)
        num = jnp.einsum('rbhts,rbhsv->rbhtv', s, vc) + g_inter[..., None] * jnp.einsum('rbhtk,rbhkv->rbhtv', qc, C)
        den = jnp.sum(s, axis=-1) + g_inter * jnp.einsum('rbhtk,rbhk->rbht', qc, n)
        h = num / jnp.maximum(jnp.abs(den), jnp.exp(-m_t))[..., None]
        m_new = m_t[..., -1]
        w_end = jnp.exp(b[..., -1:] - b + ic - m_new[..., None])
        carry_decay = jnp.exp(b[..., -1] + m - m_new)
        C = carry_decay[..., None, None] * C + jnp.einsum('rbhs,rbhsk,rbhsv->rbhkv', w_end, kc, vc)
        n = carry_decay[..., None] * n + jnp.einsum('rbhs,rbhsk->rbhk', w_end, kc)
        return (C, n, m_new), h

    (C, n, m), hs = lax.scan(step, (C0, n0, m0), tuple(chunks(a) for a in (q, k, v, log_i, log_f)))
    hs = jnp.moveaxis(hs, 0, 3).reshape(r_, b_, h_, t, -1)
    return hs, C, n, m

def _mlstm_branch(z, conv, gate_b, out_g, C0, n0, m0):
    f32 = jnp.float32
    bsz, t, _ = z.shape
    qk = z[..., OFF_QK:OFF_V]
    qk = jax.nn.silu(_shift_prev(qk) * conv[0] + qk * conv[1] + _shift_next(qk) * conv[2])
    q, k = jnp.split(qk, 2, axis=-1)
    k = k * (B_DK ** -0.5)
    v = z[..., OFF_V:OFF_O]
    o = jax.nn.sigmoid(z[..., OFF_O:OFF_G].astype(f32))
    gates = z[..., OFF_G:OFF_C].astype(f32).reshape(bsz, t, N_DIR, 2, B_H) + gate_b.astype(f32)
    gates = _orient(jnp.moveaxis(gates, 2, 0), 2)
    log_i = jnp.swapaxes(gates[..., 0, :], 2, 3)
    log_f = jnp.swapaxes(jax.nn.log_sigmoid(gates[..., 1, :]), 2, 3)

    def heads(a, d):
        a = a.astype(f32).reshape(bsz, t, B_H, d).transpose(0, 2, 1, 3)
        return jnp.stack([a, jnp.flip(a, axis=2)])

    hs, C, n, m = _mlstm_scan(heads(q, B_DK), heads(k, B_DK), heads(v, B_DV), log_i, log_f,
                              C0.astype(f32), n0.astype(f32), m0.astype(f32))
    hs = _orient(hs, 3)
    h = (hs[0] + hs[1]).transpose(0, 2, 1, 3).reshape(bsz, t, B_W)
    return (_head_norm(h, out_g, B_H) * o).astype(z.dtype), C, n, m

def _rwkv7_scan(r, w, k, v, kk, a, S0):
    xs = tuple(jnp.moveaxis(x_, 2, 0) for x_ in (r, w, k, v, kk, a))

    def step(S, inp):
        rt, wt, kt, vt, kkt, at = inp
        sa = jnp.einsum('rbhvk,rbhk->rbhv', S, -kkt)
        S = S * wt[..., None, :] + sa[..., None] * (kkt * at)[..., None, :] + vt[..., None] * kt[..., None, :]
        return S, jnp.einsum('rbhvk,rbhk->rbhv', S, rt)

    S, ys = lax.scan(step, S0, xs)
    return jnp.moveaxis(ys, 0, 2), S

def _rwkv_branch(z, mu, w0, w2, a0, a2, g2, k_k, k_a, r_k, ln_g, S0):
    f32 = jnp.float32
    bsz, t, _ = z.shape
    zc = z[..., OFF_C:]
    zc = zc + mu * (0.5 * (_shift_prev(zc) + _shift_next(zc)) - zc)
    r, k, v, dw, da, dg = jnp.split(zc, C_SPLITS, axis=-1)
    dw = jnp.tanh(dw.reshape(bsz, t, N_DIR, DECAY_RANK))
    w_log = -jax.nn.softplus(-(w0 + jnp.einsum('btrj,rjc->btrc', dw, w2))) - 0.5
    decay = jnp.exp(-jnp.exp(w_log.astype(f32)))
    a = jax.nn.sigmoid(a0 + jnp.einsum('btrj,rjc->btrc', da.reshape(bsz, t, N_DIR, ICLR_RANK), a2))
    g = jax.nn.sigmoid(dg) @ g2
    kk = (k * k_k).astype(f32).reshape(bsz, t, C_H, C_N)
    kk = kk / jnp.maximum(jnp.linalg.norm(kk, axis=-1, keepdims=True), 1e-12)
    k_dir = k[:, :, None, :] * (1 + (a - 1) * k_a)

    def shared(x_):
        x_ = x_.astype(f32).reshape(bsz, t, C_H, C_N)
        return jnp.stack([x_, jnp.flip(x_, axis=1)])

    def per_dir(x_):
        x_ = jnp.moveaxis(x_.astype(f32), 2, 0).reshape(N_DIR, bsz, t, C_H, C_N)
        return _orient(x_, 2)

    ys, S = _rwkv7_scan(shared(r), per_dir(decay), per_dir(k_dir), shared(v), shared(kk), per_dir(a), S0.astype(f32))
    ys = _orient(ys, 2)
    y = _head_norm((ys[0] + ys[1]).reshape(bsz, t, C_W), ln_g, C_H)
    bonus = jnp.sum((r[:, :, None, :] * k_dir * r_k).astype(f32).reshape(bsz, t, N_DIR, C_H, C_N), axis=(2, 4))
    y = y + (bonus[..., None] * v.astype(f32).reshape(bsz, t, C_H, C_N)).reshape(bsz, t, C_W)
    return (y * g.astype(f32)).astype(z.dtype), S

def _layer(x, cond, n_chunks, lp, C0, n0, m0, S0):
    mod = jax.nn.silu(cond) @ lp['w_mod'] + lp['b_mod']
    sh1, sc1, g1, sh2, sc2, g2 = jnp.split(mod[:, None, :], N_MOD, axis=-1)
    h = _rmsnorm(x, lp['norm1_g']) * (1 + sc1) + sh1
    z = h @ lp['w_in']
    y_a = _chunk_gmlp(z[..., OFF_A:OFF_QK], lp['gmlp_ln_g'], lp['gmlp_w_s'], lp['gmlp_b_s'], n_chunks)
    y_b, C, n, m = _mlstm_branch(z, lp['mlstm_conv'], lp['mlstm_gate_b'], lp['mlstm_out_g'], C0, n0, m0)
    y_c, S = _rwkv_branch(z, lp['rwkv_mu'], lp['rwkv_w0'], lp['rwkv_w2'], lp['rwkv_a0'], lp['rwkv_a2'],
                          lp['rwkv_g2'], lp['rwkv_k_k'], lp['rwkv_k_a'], lp['rwkv_r_k'], lp['rwkv_ln_g'], S0)
    x = x + g1 * (jnp.concatenate([y_a, y_b, y_c], axis=-1) @ lp['w_out'])
    h = _rmsnorm(x, lp['norm2_g']) * (1 + sc2) + sh2
    x = x + g2 * (jnp.square(jax.nn.relu(h @ lp['mlp_w1'])) @ lp['mlp_w2'])
    return x, C, n, m, S

def setup_inputs(seed: int = 0) -> dict:
    key = jax.random.key(seed)
    ks = iter(jax.random.split(key, 48))

    def nrm(shape, s):
        return jax.random.normal(next(ks), shape, jnp.float32) * s

    def uni(shape, lo, hi):
        return jax.random.uniform(next(ks), shape, jnp.float32, lo, hi)

    f_bias = jnp.broadcast_to(jnp.linspace(3.0, 6.0, B_H), (DEPTH, N_DIR, B_H))
    gate_b = jnp.stack([nrm((DEPTH, N_DIR, B_H), 0.1), f_bias + nrm((DEPTH, N_DIR, B_H), 0.1)], axis=2)
    conv_center = jnp.array([0.0, 1.0, 0.0], jnp.float32)[None, :, None]
    return {
        'x_prompt': nrm((BATCH, SEQ, D_MODEL), 1.0),
        'x_sample': nrm((DEC_BATCH, DEC_SEQ, D_MODEL), 1.0),
        'c': nrm((DEC_BATCH, D_MODEL), 1.0),
        'state_mlstm_C': nrm((DEC_BATCH, DEPTH, N_DIR, B_H, B_DK, B_DV), 0.3),
        'state_mlstm_n': nrm((DEC_BATCH, DEPTH, N_DIR, B_H, B_DK), 0.3),
        'state_mlstm_m': 2.0 + nrm((DEC_BATCH, DEPTH, N_DIR, B_H), 0.5),
        'state_rwkv_S': nrm((DEC_BATCH, DEPTH, N_DIR, C_H, C_N, C_N), 0.3),
        'c_ctx': nrm((D_MODEL,), 1.0),
        'norm1_g': 1.0 + nrm((DEPTH, D_MODEL), 0.05),
        'norm2_g': 1.0 + nrm((DEPTH, D_MODEL), 0.05),
        'w_mod': nrm((DEPTH, D_MODEL, N_MOD * D_MODEL), 0.5 * D_MODEL ** -0.5),
        'b_mod': nrm((DEPTH, N_MOD * D_MODEL), 0.02),
        'w_in': nrm((DEPTH, D_MODEL, IN_COLS), D_MODEL ** -0.5),
        'w_out': nrm((DEPTH, MIX_W, D_MODEL), MIX_W ** -0.5),
        'gmlp_ln_g': 1.0 + nrm((DEPTH, A_W), 0.05),
        'gmlp_w_s': nrm((DEPTH, A_GROUPS, CHUNK, CHUNK), CHUNK ** -0.5),
        'gmlp_b_s': 1.0 + nrm((DEPTH, A_GROUPS, CHUNK), 0.1),
        'mlstm_conv': conv_center + nrm((DEPTH, 3, 2 * B_H * B_DK), 0.3),
        'mlstm_gate_b': gate_b,
        'mlstm_out_g': 1.0 + nrm((DEPTH, B_W), 0.05),
        'rwkv_mu': uni((DEPTH, C_COLS), 0.0, 1.0),
        'rwkv_w0': uni((DEPTH, N_DIR, C_W), -4.0, 1.0),
        'rwkv_w2': nrm((DEPTH, N_DIR, DECAY_RANK, C_W), 0.1),
        'rwkv_a0': nrm((DEPTH, N_DIR, C_W), 0.5),
        'rwkv_a2': nrm((DEPTH, N_DIR, ICLR_RANK, C_W), 0.1),
        'rwkv_g2': nrm((DEPTH, GATE_RANK, C_W), GATE_RANK ** -0.5),
        'rwkv_k_k': 0.85 + nrm((DEPTH, C_W), 0.05),
        'rwkv_k_a': 1.0 + nrm((DEPTH, C_W), 0.05),
        'rwkv_r_k': nrm((DEPTH, C_W), 0.1),
        'rwkv_ln_g': 1.0 + nrm((DEPTH, C_W), 0.05),
        'mlp_w1': nrm((DEPTH, D_MODEL, D_FF), D_MODEL ** -0.5),
        'mlp_w2': nrm((DEPTH, D_FF, D_MODEL), D_FF ** -0.5),
        'final_g': 1.0 + nrm((D_MODEL,), 0.05),
    }

def reference(x_prompt, x_sample, c, state_mlstm_C, state_mlstm_n, state_mlstm_m, state_rwkv_S, c_ctx,
              norm1_g, norm2_g, w_mod, b_mod, w_in, w_out, gmlp_ln_g, gmlp_w_s, gmlp_b_s,
              mlstm_conv, mlstm_gate_b, mlstm_out_g, rwkv_mu, rwkv_w0, rwkv_w2, rwkv_a0, rwkv_a2,
              rwkv_g2, rwkv_k_k, rwkv_k_a, rwkv_r_k, rwkv_ln_g, mlp_w1, mlp_w2, final_g):
    f32 = jnp.float32
    n_prompt = x_prompt.shape[0]
    ctx_chunks = x_prompt.shape[1] // CHUNK
    rows = x_sample.shape[1] // GRID_W
    lat_chunks = rows // ROWS_PER_CHUNK
    cond_ctx = c_ctx[None, :]
    xp, xs = x_prompt, x_sample
    new_C, new_n, new_m, new_S = [], [], [], []
    for l in range(DEPTH):
        lp = {
            'norm1_g': norm1_g[l], 'norm2_g': norm2_g[l], 'w_mod': w_mod[l], 'b_mod': b_mod[l],
            'w_in': w_in[l], 'w_out': w_out[l], 'gmlp_ln_g': gmlp_ln_g[l], 'gmlp_w_s': gmlp_w_s[l],
            'gmlp_b_s': gmlp_b_s[l], 'mlstm_conv': mlstm_conv[l], 'mlstm_gate_b': mlstm_gate_b[l],
            'mlstm_out_g': mlstm_out_g[l], 'rwkv_mu': rwkv_mu[l], 'rwkv_w0': rwkv_w0[l],
            'rwkv_w2': rwkv_w2[l], 'rwkv_a0': rwkv_a0[l], 'rwkv_a2': rwkv_a2[l], 'rwkv_g2': rwkv_g2[l],
            'rwkv_k_k': rwkv_k_k[l], 'rwkv_k_a': rwkv_k_a[l], 'rwkv_r_k': rwkv_r_k[l],
            'rwkv_ln_g': rwkv_ln_g[l], 'mlp_w1': mlp_w1[l], 'mlp_w2': mlp_w2[l],
        }
        xp, C, n, m, S = _layer(
            xp, cond_ctx, ctx_chunks, lp,
            jnp.zeros((N_DIR, n_prompt, B_H, B_DK, B_DV), f32),
            jnp.zeros((N_DIR, n_prompt, B_H, B_DK), f32),
            jnp.zeros((N_DIR, n_prompt, B_H), f32),
            jnp.zeros((N_DIR, n_prompt, C_H, C_N, C_N), f32))
        new_C.append(jnp.swapaxes(C, 0, 1))
        new_n.append(jnp.swapaxes(n, 0, 1))
        new_m.append(jnp.swapaxes(m, 0, 1))
        new_S.append(jnp.swapaxes(S, 0, 1))
        xs, _, _, _, _ = _layer(
            xs, c, lat_chunks, lp,
            jnp.swapaxes(state_mlstm_C[:, l], 0, 1),
            jnp.swapaxes(state_mlstm_n[:, l], 0, 1),
            jnp.swapaxes(state_mlstm_m[:, l], 0, 1),
            jnp.swapaxes(state_rwkv_S[:, l], 0, 1))
    y_prompt = _rmsnorm(xp, final_g)
    y_sample = _rmsnorm(xs, final_g)
    return (y_prompt, y_sample, jnp.stack(new_C, axis=1), jnp.stack(new_n, axis=1),
            jnp.stack(new_m, axis=1), jnp.stack(new_S, axis=1))


_drawn_inputs = setup_inputs


def setup_inputs(seed=0):
    import zlib

    import numpy as np

    out = dict(_drawn_inputs(seed))
    spreads = {}
    factors = {'state_mlstm_C': 2.869,
     'state_mlstm_n': 8.0,
     'state_mlstm_m': 8.0,
     'state_rwkv_S': 8.0,
     'gmlp_ln_g': 8.0,
     'gmlp_b_s': 5.715,
     'mlstm_out_g': 8.0,
     'rwkv_ln_g': 8.0,
     'norm2_g': 4.082,
     'rwkv_r_k': 2.791}
    for name, (base, spread) in spreads.items():
        noise = np.random.default_rng([zlib.crc32(name.encode()), seed]).standard_normal(out[name].shape)
        drawn = base * np.exp(spread * noise) if base else spread * noise
        out[name] = jnp.asarray(drawn.astype(out[name].dtype))
    for name, factor in factors.items():
        out[name] = (out[name] * factor).astype(out[name].dtype)
    return out
```

```python
import concourse.bass as bass
from concourse import mybir
from contextlib import ExitStack
import math

F32 = mybir.dt.float32
F32R = mybir.dt.float32r
ALU = mybir.AluOpType
ACT = mybir.ActivationFunctionType
AX = mybir.AxisListType
ds = bass.ds

P = 128
D = 1024
KB = D // P
N_CTX, N_LAT = 128, 1024
T = N_CTX + N_LAT
NT = T // P
GRP = 384
NG = T // GRP
H, N = 6, 64
NP = H // 2
A_W, A_G = 256, 4
B_W = C_W = H * N
OFF_QK, OFF_V, OFF_O, OFF_G = 512, 1280, 1664, 2048
OFF_C = OFF_G + 24
IN_COLS = OFF_C + 3 * C_W + 384
D_FF = 4 * D
N_MOD = 6
EPS, HEAD_EPS = 1e-6, 1e-5
LEVELS = 7
DECAY = math.exp(-0.5)
GELU = 2.0 * math.sqrt(2.0 / math.pi)
NEG = -1e30
CTX0, LAT0, PADW = 1, N_CTX + 2, T + 4

PROWS = {}
_at = 0
for _name, _n in (("b_mod", 48), ("norm1_g", 8), ("norm2_g", 8), ("final_g", 8), ("mlstm_conv", 18),
                  ("rwkv_mu", 12), ("rwkv_w0", 6), ("rwkv_a0", 6), ("rwkv_k_k", 3), ("rwkv_k_a", 3),
                  ("rwkv_r_k", 3), ("rwkv_ln_g", 3), ("gmlp_ln_g", 2), ("mlstm_out_g", 3),
                  ("c", 8), ("c_ctx", 8)):
    PROWS[_name] = (_at, _n)
    _at += _n
N_PROWS = _at


class Flag:

    def __init__(self, sem, q=1, in_hand=0):
        self.sem, self.q, self.in_hand = sem, q, in_hand

    def at(self, j=0, k=None):
        return j * self.q + (self.q if k is None else k) + self.in_hand

    def last(self, j, k=None):
        return j * self.q - self.q + (self.q if k is None else k) + self.in_hand

    def front(self, j, k):
        return j * self.q + k - 1 + self.in_hand


def later(j, k=1):
    return not isinstance(j, int) or j > 0 or k > 1


def plain(x):
    return x.bitcast(F32)


class Store:

    def __init__(self, nc, ctx, io, out):
        self.nc, self.ctx, self.io, self.out = nc, ctx, io, out
        self.sems = []

    def sb(self, name, *shape):
        return self.ctx.enter_context(self.nc.sbuf_tensor(name, list(shape), F32))

    def sb2(self, name, *shape):
        with self.nc.sbuf_tensor(name + "_r", list(shape), F32R) as r:
            pass
        x = self.sb(name, *shape)
        return x, r

    def half(self, name, *shape):
        return self.ctx.enter_context(self.nc.sbuf_tensor(name, list(shape), mybir.dt.bfloat16))

    def sem(self, name):
        self.sems.append(self.nc.alloc_semaphore(name=name))
        return self.sems[-1]

    def release(self):
        self.nc.clear_and_free_semaphores(self.sems)
        self.nc.all_engine_barrier()
        self.sems = []

    def apart(self, eng):
        eng.wait_ge(self.always, 1)

    def flag(self, name, q=1, in_hand=0):
        return Flag(self.sem(name), q, in_hand)

    def param(self, name, i=0, n=None):
        at, count = PROWS[name]
        return self.PT[:, at + i:at + i + (count - i if n is None else n)]


def allocate(S):
    S.XT, S.XTr = S.sb2("XT", P, KB, T)
    S.HT, S.HTr = S.sb2("HT", P, KB, T)
    S.YT, S.YTr = S.sb2("YT", P, KB, T)
    S.Z, S.Zr = S.sb2("Z", P, 12, T)
    slabs = [S.sb2(f"W{i}", P, KB, P) for i in range(2)]
    S.W, S.Wr = [x[0] for x in slabs], [x[1] for x in slabs]
    S.PAD = [S.sb(f"PAD{i}", P, PADW) for i in range(4)]
    S.PT = S.sb("PT", P, N_PROWS)
    S.MOD = S.sb("MOD", P, 48, 2)
    S.GS = S.sb("GSC", P, 2, KB, 2)
    S.ident = S.sb("ident", P, P)
    S.ones = S.sb("ones", P, P)
    S.halves = S.sb("halves", P, P)
    S.tri = {k: S.sb(f"tri_{k}", P, P) for k in ("UPS", "UPI", "LOS", "LOI")}
    S.level = S.half("level", P, 2, LEVELS, P)
    S.neg = [S.sb(f"neg{d}", P, P) for d in range(2)]
    S.eps = S.sb("eps", P, 4)
    S.PS = [S.ctx.enter_context(S.nc.psum_tensor(f"bank{i}", [P, 512], F32)) for i in range(8)]


def setup(S):
    nc, io = S.nc, S.io
    rows = [S.Z[:, 0, 0:P], S.Z[:, 0, P:2 * P]]
    loaded, turned, done = S.flag("params_loaded"), S.flag("params_turned"), S.flag("params_done")
    made, copied = S.flag("constants_made"), S.flag("constants_copied")
    lead = S.flag("rows_cleared")

    with nc.Block() as block:
        @block.vector
        def _(dve):
            dve.sem_inc(S.always, 1)
            nc.vector.memset(S.Z[:, 0, 0:2 * P], 0.0).then_inc(lead.sem, 1)
            nc.vector.memset(S.ones[:, :], 1.0)
            nc.vector.memset(S.eps[:, 0:1], EPS)
            nc.vector.memset(S.eps[:, 1:2], HEAD_EPS)
            nc.vector.memset(S.eps[:, 2:3], 1.0)
            nc.vector.memset(S.halves[0:N, 0:N], 1.0)
            nc.vector.memset(S.halves[N:P, N:P], 1.0)
            nc.vector.memset(S.halves[0:N, N:P], 0.0)
            nc.vector.memset(S.halves[N:P, 0:N], 0.0)
            dve.wait_ge(turned.sem, turned.at())
            nc.vector.tensor_copy(S.PT[:, 0:P], S.PS[0][:, 0:P])
            nc.vector.tensor_copy(S.PT[:, P:N_PROWS], S.PS[0][:, P:N_PROWS])

        @block.sync
        def _(sp):
            sp.wait_ge(lead.sem, lead.at())
            n = 0
            for name, (at, count) in PROWS.items():
                src = io[name].rearrange(SHAPES[name][1], p=P)
                for r in (0, 1):
                    a, b = max(at, r * P), min(at + count, r * P + P)
                    if a < b:
                        sp.dma_start(rows[r][a - r * P:b - r * P, :], src[a - at:b - at, :]).then_inc(loaded.sem, 16)
                        n += 1
            S.n_param_loads = n

        @block.gpsimd
        def _(pool):
            n = 0

            def done_one(ins):
                nonlocal n
                ins.then_inc(made.sem, 1)
                n += 1
                pool.wait_ge(made.sem, made.at(0, n))

            def keep(view, pattern, base, mult, op=ALU.is_ge, fill=0.0):
                done_one(nc.gpsimd.affine_select(out=view, in_=view, compare_op=op, fill=fill, base=base,
                                                 pattern=pattern, channel_multiplier=mult))

            done_one(nc.gpsimd.memset(S.ident[:, :], 0.0))
            keep(S.ident[:, :], [[-1, P]], 0, 1, ALU.not_equal, 1.0)
            for k, (base, mult, step) in {"UPS": (-1, -1, 1), "UPI": (0, -1, 1),
                                          "LOS": (-1, 1, -1), "LOI": (0, 1, -1)}.items():
                done_one(nc.gpsimd.memset(S.tri[k][:, :], 1.0))
                keep(S.tri[k][:, :], [[step, P]], base, mult)
            for d, (mult, step) in enumerate(((-1, 1), (1, -1))):
                done_one(nc.gpsimd.memset(S.neg[d][:, :], 0.0))
                keep(S.neg[d][:, :], [[step, P]], 0, mult, fill=NEG)

        @block.tensor
        def _(pe):
            pe.wait_ge(loaded.sem, loaded.at(0, 16 * S.n_param_loads))
            pe.wait_ge(made.sem, made.at(0, 2))
            nc.tensor.transpose(S.PS[0][:, 0:P], rows[0], S.ident[:, :])
            nc.tensor.transpose(S.PS[0][:, P:2 * P], rows[1], S.ident[:, :]).then_inc(turned.sem, 1)


SHAPES = {
    "x_prompt": ((1, N_CTX, D), None), "x_sample": ((1, N_LAT, D), None), "c": ((1, D), "a (k p) -> (a k) p"),
    "state_mlstm_C": ((1, 1, 2, H, N, N), None), "state_mlstm_n": ((1, 1, 2, H, N), None),
    "state_mlstm_m": ((1, 1, 2, H), None), "state_rwkv_S": ((1, 1, 2, H, N, N), None),
    "c_ctx": ((D,), "(k p) -> k p"), "norm1_g": ((1, D), "a (k p) -> (a k) p"),
    "norm2_g": ((1, D), "a (k p) -> (a k) p"), "w_mod": ((1, D, N_MOD * D), None),
    "b_mod": ((1, N_MOD * D), "a (k p) -> (a k) p"), "w_in": ((1, D, IN_COLS), None), "w_out": ((1, D, D), None),
    "gmlp_ln_g": ((1, A_W), "a (k p) -> (a k) p"), "gmlp_w_s": ((1, A_G, P, P), None),
    "gmlp_b_s": ((1, A_G, P), None), "mlstm_conv": ((1, 3, 2 * B_W), "a c (k p) -> (a c k) p"),
    "mlstm_gate_b": ((1, 2, 2, H), None), "mlstm_out_g": ((1, B_W), "a (k p) -> (a k) p"),
    "rwkv_mu": ((1, 3 * C_W + 384), "a (k p) -> (a k) p"), "rwkv_w0": ((1, 2, C_W), "a r (k p) -> (a r k) p"),
    "rwkv_w2": ((1, 2, 64, C_W), None), "rwkv_a0": ((1, 2, C_W), "a r (k p) -> (a r k) p"),
    "rwkv_a2": ((1, 2, 64, C_W), None), "rwkv_g2": ((1, 128, C_W), None),
    "rwkv_k_k": ((1, C_W), "a (k p) -> (a k) p"), "rwkv_k_a": ((1, C_W), "a (k p) -> (a k) p"),
    "rwkv_r_k": ((1, C_W), "a (k p) -> (a k) p"), "rwkv_ln_g": ((1, C_W), "a (k p) -> (a k) p"),
    "mlp_w1": ((1, D, D_FF), None), "mlp_w2": ((1, D_FF, D), None), "final_g": ((D,), "(k p) -> k p"),
}
OUTS = [(1, N_CTX, D), (1, N_LAT, D), (1, 1, 2, H, N, N), (1, 1, 2, H, N), (1, 1, 2, H), (1, 1, 2, H, N, N)]


EXP_LN, EXP_TANH = "natural_log_exp_and_others", "exp_and_others"


class Area:

    def __init__(self, flat):
        self.flat, self.at = flat, 0

    def cut(self, *shape, rows=P):
        n = math.prod(shape)
        a = self.flat[0:rows, self.at:self.at + n]
        self.at += n
        assert self.at <= self.flat.shape[1], "the region is full"
        if len(shape) > 1:
            names = "abcde"[:len(shape)]
            a = a.rearrange(f"p ({' '.join(names)}) -> p {' '.join(names)}", **dict(zip(names, shape)))
        return a


def square_sums(S, tag):
    nc = S.nc
    squared, summed = S.flag(f"{tag}_squared", KB), S.flag(f"{tag}_summed", KB)
    logged = S.flag(f"{tag}_logged", NG)
    SQ = [S.YT[:, i, :] for i in range(2)] if tag != "fin" else [S.YT[:, i, :] for i in range(2)]
    with nc.Block() as block:
        @block.scalar
        def _(act):
            for k in range(KB):
                if k >= 2:
                    act.wait_ge(summed.sem, summed.at(0, k - 1))
                nc.scalar.activation(SQ[k % 2], S.XT[:, k, :], ACT.Square).then_inc(squared.sem, 1)
            act.wait_ge(summed.sem, summed.at())
            for g in range(NG):
                nc.scalar.activation(S.RS[:, g * GRP:(g + 1) * GRP], S.PS[g][:, 0:GRP], ACT.Ln,
                                                bias=S.eps[:, 0:1], scale=1.0 / D).then_inc(logged.sem, 1)
            act.wait_ge(logged.sem, logged.at())
            nc.scalar.activation(S.RS[:, :], S.RS[:, :], ACT.Exp, scale=-0.5)

        @block.tensor
        def _(pe):
            for k in range(KB):
                pe.wait_ge(squared.sem, squared.at(0, k + 1))
                for g in range(NG):
                    mm = nc.tensor.matmul(S.PS[g][:, 0:GRP], S.ones[:, :], SQ[k % 2][:, g * GRP:(g + 1) * GRP],
                                          start=(k == 0), stop=(k == KB - 1))
                mm.then_inc(summed.sem, 1)


def modulate(S, tag, which, low, low_r):
    nc = S.nc
    scaled, gained = S.flag(f"{tag}_scaled", KB), S.flag(f"{tag}_gained")
    shifted, split = S.flag(f"{tag}_shifted", KB), S.flag(f"{tag}_rounded", KB)
    left = S.flag(f"{tag}_left", KB)
    with nc.Block() as block:
        @block.vector
        def _(dve):
            sc = S.MOD[:, (3 * which + 1) * KB:(3 * which + 2) * KB, :]
            g = S.param("norm1_g" if which == 0 else "norm2_g")
            for c in range(2):
                ins = nc.vector.scalar_tensor_tensor(out=S.GS[:, which, :, c], in0=sc[:, :, c], scalar=1.0, in1=g,
                                                     op0=ALU.add, op1=ALU.mult)
            ins.then_inc(gained.sem, 1)
            for k in range(KB):
                nc.vector.tensor_tensor(S.HT[:, k, :], S.XT[:, k, :], S.RS[:, :], ALU.mult).then_inc(scaled.sem, 1)
            for k in range(KB):
                dve.wait_ge(split.sem, split.at(0, k + 1))
                nc.vector.tensor_tensor(low_r[:, k, :], low[:, k, :], plain(S.HTr[:, k, :]), ALU.subtract).then_inc(left.sem, 1)

        @block.scalar
        def _(act):
            act.wait_ge(gained.sem, gained.at())
            if which == 0:
                act.wait_ge(S.saved.sem, S.saved.at())
            for k in range(KB):
                act.wait_ge(scaled.sem, scaled.at(0, k + 1))
                for c, (a, b) in enumerate(((0, N_CTX), (N_CTX, T))):
                    ins = nc.scalar.activation(low[:, k, a:b], S.HT[:, k, a:b], ACT.Identity,
                                               bias=S.MOD[:, 3 * which * KB + k, c:c + 1], scale=S.GS[:, which, k, c:c + 1])
                ins.then_inc(shifted.sem, 1)

        @block.gpsimd
        def _(pool):
            for k in range(KB):
                pool.wait_ge(shifted.sem, shifted.at(0, k + 1))
                nc.gpsimd.tensor_copy(S.HTr[:, k, :], low[:, k, :]).then_inc(split.sem, 1)

        @block.sync
        def _(sp):
            if which == 0:
                sp.wait_ge(left.sem, left.at())
                sp.dma_start(S.low_dram, plain(S.XTr[:, :, :])).then_inc(S.low_saved.sem, 16)


def enter(S):
    nc, io = S.nc, S.io
    x_in = [S.YT[:, i, 0:D] for i in range(2)]
    WM = [S.Z[:, 4 * i:4 * i + 4, :].rearrange("p a b -> p (a b)")[:, 0:KB * 512].rearrange("p (k n) -> p k n", k=KB)
          for i in range(3)]
    SC = S.HT[:, 0, 0:16].rearrange("p (k c) -> p k c", c=2)
    SE = S.HT[:, 1, 0:16].rearrange("p (k c) -> p k c", c=2)
    x_loaded = [S.flag(f"x_loaded{i}") for i in range(2)]
    x_turned, x_stored = S.flag("x_turned", 2), S.flag("x_stored", 2)
    S.saved = S.flag("residual_saved", 16)
    mod_loaded = [S.flag(f"w_mod_loaded{i}") for i in range(3)]
    mod_used, mod_turned = S.flag("w_mod_used", 3), S.flag("mod_turned")
    mod_rows = S.flag("mod_rows", 3, in_hand=3)
    MR = S.HT[0:2, 2:8, :].rearrange("p a b -> p (a b)")
    expd, cond = S.flag("cond_exp"), S.flag("cond_ready", 4)
    w_mod = io["w_mod"][0].rearrange("(k p) n -> p k n", p=P)
    n_mod = N_MOD * D // 512 // 3

    with nc.Block() as block:
        @block.sync
        def _(sp):
            sp.dma_start(x_in[0], io["x_prompt"][0]).then_inc(x_loaded[0].sem, 16)
            for i in range(3):
                sp.dma_start(WM[i], w_mod[:, :, i * 512:(i + 1) * 512]).then_inc(mod_loaded[i].sem, 16)
            for t in range(1, NT):
                if t >= 2:
                    sp.wait_ge(x_turned.sem, x_turned.at(0, t - 1))
                sp.dma_start(x_in[t % 2], io["x_sample"][0, (t - 1) * P:t * P, :]).then_inc(x_loaded[t % 2].sem, 16)
            with sp.Fori(1, n_mod) as j:
                for i in range(3):
                    sp.wait_ge(mod_used.sem, mod_used.at(j - 1, i + 1))
                    sp.dma_start(WM[i], w_mod[:, :, ds(j * 1536 + i * 512, 512)]).then_inc(mod_loaded[i].sem, 16)
            sp.wait_ge(x_stored.sem, x_stored.at(0, NT))
            sp.dma_start(S.x_dram, S.XT[:, :, :]).then_inc(S.saved.sem, 16)

        @block.tensor
        def _(pe):
            for t in range(NT):
                pe.wait_ge(x_loaded[t % 2].sem, x_loaded[t % 2].at(0, 16 * (t // 2 + 1)))
                if t >= 2:
                    pe.wait_ge(x_stored.sem, x_stored.at(0, t - 1))
                for k in range(KB):
                    tr = nc.tensor.transpose(S.PS[2 * (t % 2) + k // 4][:, (k % 4) * P:(k % 4 + 1) * P],
                                             x_in[t % 2][:, k * P:(k + 1) * P], S.ident[:, :])
                tr.then_inc(x_turned.sem, 1)
            pe.wait_ge(cond.sem, cond.at())
            with pe.Fori(0, n_mod) as j:
                for i in range(3):
                    pe.wait_ge(mod_loaded[i].sem, mod_loaded[i].at(16 * j, 16))
                    pe.wait_ge(mod_rows.sem, mod_rows.last(j, i + 1))
                    for k in range(KB):
                        mm = nc.tensor.matmul(S.PS[4 + i][0:2, :], SC[:, k, :], WM[i][:, k, :],
                                              start=(k == 0), stop=(k == KB - 1))
                    mm.then_inc(mod_used.sem, 1)
            pe.wait_ge(mod_rows.sem, mod_rows.at(n_mod - 1))
            for b in range(N_MOD * KB):
                tr = nc.tensor.transpose(S.PS[7][:, 2 * b:2 * b + 2], MR[:, b * P:(b + 1) * P], S.ident[0:2, 0:2])
            tr.then_inc(mod_turned.sem, 1)

        @block.scalar
        def _(act):
            for c, name in enumerate(("c_ctx", "c")):
                ins = nc.scalar.activation(SE[:, :, c], S.param(name), ACT.Exp, scale=-1.0)
            ins.then_inc(expd.sem, 1)
            for t in range(NT):
                act.wait_ge(x_turned.sem, x_turned.at(0, t + 1))
                for i in range(2):
                    ins = nc.scalar.copy(S.XT[:, 4 * i:4 * i + 4, t * P:(t + 1) * P],
                                         S.PS[2 * (t % 2) + i][:, :].rearrange("p (k n) -> p k n", k=4))
                ins.then_inc(x_stored.sem, 1)
            with act.Fori(0, n_mod) as j:
                for i in range(3):
                    act.wait_ge(mod_used.sem, mod_used.at(j, i + 1))
                    S.apart(act)
                    nc.scalar.copy(MR[:, ds(j * 1536 + i * 512, 512)], S.PS[4 + i][0:2, :]).then_inc(mod_rows.sem, 1)

        @block.gpsimd
        def _(pool):
            pool.sem_inc(mod_rows.sem, mod_rows.in_hand)

        @block.vector
        def _(dve):
            dve.wait_ge(expd.sem, expd.at())
            nc.vector.tensor_scalar(SE, SE, 1.0, None, ALU.add).then_inc(cond.sem, 1)
            dve.wait_ge(cond.sem, cond.at(0, 1))
            nc.vector.reciprocal(SE, SE).then_inc(cond.sem, 1)
            dve.wait_ge(cond.sem, cond.at(0, 2))
            for c, name in enumerate(("c_ctx", "c")):
                nc.vector.tensor_tensor(SC[:, :, c], SE[:, :, c], S.param(name), ALU.mult).then_inc(cond.sem, 1)
            dve.wait_ge(mod_turned.sem, mod_turned.at())
            for c in range(2):
                nc.vector.tensor_tensor(S.MOD[:, :, c], S.PS[7][:, 0:96].rearrange("p (b c) -> p b c", c=2)[:, :, c],
                                        S.param("b_mod"), ALU.add)


class Dense:

    def __init__(self, S, tag, low, high=None, blocks=KB):
        self.S, self.blocks = S, blocks
        self.high_r = high or [w[:, :, :] for w in S.Wr]
        self.low, self.low_r = low
        self.loaded = [S.flag(f"{tag}_weights_loaded{i}", 16) for i in range(2)]
        self.rounded = S.flag(f"{tag}_weights_rounded", 2)
        self.split = S.flag(f"{tag}_weights_split", 2)
        self.summed = S.flag(f"{tag}_summed", 2 * NG, in_hand=2 * NG)
        self.drained = [S.flag(f"{tag}_drained{g}", 2, in_hand=2) for g in range(NG)]

    def start(self, eng):
        eng.sem_inc(self.summed.sem, self.summed.in_hand)
        for d in self.drained:
            eng.sem_inc(d.sem, d.in_hand)

    def load(self, sp, i, slot, src):
        sp.wait_ge(self.summed.sem, self.summed.last(i, NG * (slot + 1)))
        sp.dma_start(self.low[slot], src).then_inc(self.loaded[slot].sem, 16)

    def divide(self, pool, i, slot):
        nc = self.S.nc
        pool.wait_ge(self.loaded[slot].sem, self.loaded[slot].at(i))
        ones = self.S.ones[:, :].unsqueeze(1).to_broadcast([P, self.blocks, P])
        nc.gpsimd.tensor_tensor(self.high_r[slot], self.low[slot], ones,
                                ALU.mult).then_inc(self.rounded.sem, 1)
        pool.wait_ge(self.rounded.sem, self.rounded.at(i, slot + 1))
        nc.gpsimd.tensor_tensor(self.low_r[slot], self.low[slot], plain(self.high_r[slot]),
                                ALU.subtract).then_inc(self.split.sem, 1)

    def multiply(self, pe, i, slot, high, low):
        nc, S = self.S.nc, self.S
        pe.wait_ge(self.split.sem, self.split.at(i, slot + 1))
        products = ((self.high_r, high), (self.low_r, high), (self.high_r, low))
        for g in range(NG):
            pe.wait_ge(self.drained[g].sem, self.drained[g].last(i, slot + 1))
            for n, (w, x) in enumerate(products):
                for k in range(self.blocks):
                    mm = nc.tensor.matmul(self.bank(slot, g), w[slot][:, k, :], x(k, g),
                                          start=(n == 0 and k == 0), stop=(n == 2 and k == self.blocks - 1))
            mm.then_inc(self.summed.sem, 1)

    def bank(self, slot, g):
        return self.S.PS[3 * slot + g][:, 0:GRP]

    def filled(self, i, slot, g):
        return self.summed.at(i, NG * slot + g + 1)


def slabs(places, views, blocks=KB, skip=0):
    return [[place(x)[:, skip:skip + blocks * P].rearrange("p (k n) -> p k n", k=blocks) for place in places]
            for x in views]


def group(buf, first=0):
    return lambda k, g: buf[:, first + k, g * GRP:(g + 1) * GRP]


def to_padded(S, dense, act, i, slot, ZP):
    nc = S.nc
    for g in range(NG):
        act.wait_ge(dense.summed.sem, dense.filled(i, slot, g))
        a = LAT0 + g * GRP - N_CTX
        if g == 0:
            nc.scalar.copy(ZP[:, CTX0:CTX0 + N_CTX], S.PS[3 * slot][:, 0:N_CTX])
            ins = nc.scalar.copy(ZP[:, LAT0:LAT0 + GRP - N_CTX], S.PS[3 * slot][:, N_CTX:GRP])
        else:
            ins = nc.scalar.copy(ZP[:, a:a + GRP], dense.bank(slot, g))
        ins.then_inc(dense.drained[g].sem, 1)


SEQS = ((0, N_CTX, CTX0), (N_CTX, N_LAT, LAT0))


class HeadNorm:

    def __init__(self, S, tag, heads, dev, q=1):
        self.S, self.heads, self.q, self.dev = S, heads, q, dev
        self.summed = S.flag(f"{tag}_mean", q)
        self.centred = S.flag(f"{tag}_centred", q)
        self.squared = S.flag(f"{tag}_squared_dev", q)
        self.varied = S.flag(f"{tag}_variance", q)
        self.logged = S.flag(f"{tag}_log", q)
        self.rooted = S.flag(f"{tag}_rstd", q)
        self.normed = S.flag(f"{tag}_normed", q)
        self.stat = S.sb(f"{tag}_stat", P, 3, heads)

    def vector(self, dve, j, x, sq, out):
        nc, S, st, dev, h = self.S.nc, self.S, self.stat, self.dev, self.heads
        nc.vector.tensor_reduce(st[:, 0, :], x, AX.X, ALU.add).then_inc(self.summed.sem, 1)
        dve.wait_ge(self.summed.sem, self.summed.at(j))
        nc.vector.scalar_tensor_tensor(
            out=dev, in0=st[:, 0, :].unsqueeze(2).to_broadcast([P, h, N]), scalar=-1.0 / N, in1=x,
            op0=ALU.mult, op1=ALU.add).then_inc(self.centred.sem, 1)
        dve.wait_ge(self.centred.sem, self.centred.at(j))
        nc.vector.tensor_tensor(sq, dev, dev, ALU.mult).then_inc(self.squared.sem, 1)
        dve.wait_ge(self.squared.sem, self.squared.at(j))
        nc.vector.tensor_reduce(st[:, 1, :], sq, AX.X, ALU.add).then_inc(self.varied.sem, 1)
        dve.wait_ge(self.rooted.sem, self.rooted.at(j))
        nc.vector.tensor_tensor(out, dev,
                                                st[:, 2, :].unsqueeze(2).to_broadcast([P, h, N]), ALU.mult).then_inc(self.normed.sem, 1)

    def scalar(self, act, j):
        nc, S, st = self.S.nc, self.S, self.stat
        act.wait_ge(self.varied.sem, self.varied.at(j))
        nc.scalar.activation(st[:, 2, :], st[:, 1, :], ACT.Ln, bias=S.eps[:, 1:2], scale=1.0 / N).then_inc(self.logged.sem, 1)
        act.wait_ge(self.logged.sem, self.logged.at(j))
        nc.scalar.activation(st[:, 2, :], st[:, 2, :], ACT.Exp, scale=-0.5).then_inc(self.rooted.sem, 1)


def project_a(S):
    nc, io = S.nc, S.io
    w_in = io["w_in"][0].rearrange("(k p) n -> p k n", p=P)
    dense = Dense(S, "a", slabs([lambda x: x[:, 5, :], lambda x: x[:, 6, :]], (S.YT, S.YTr)))
    with nc.Block() as block:
        @block.gpsimd
        def _(pool):
            dense.start(pool)
            with pool.Fori(0, 2) as i:
                for slot in range(2):
                    dense.divide(pool, i, slot)

        @block.sync
        def _(sp):
            with sp.Fori(0, 2) as i:
                for slot in range(2):
                    dense.load(sp, i, slot, w_in[:, :, ds(i * 256 + slot * P, P)])
            sp.wait_ge(S.low_saved.sem, S.low_saved.at())

        @block.tensor
        def _(pe):
            with pe.Fori(0, 2) as i:
                for slot in range(2):
                    dense.multiply(pe, i, slot, group(S.HTr), group(S.XTr))

        @block.scalar
        def _(act):
            with act.Fori(0, 2) as i:
                for slot in range(2):
                    blk = act.snap(i * 2 + slot, min_val=0, max_val=3)
                    for g in range(NG):
                        act.wait_ge(dense.summed.sem, dense.filled(i, slot, g))
                        S.apart(act)
                        nc.scalar.activation(
                            S.Z[:, ds(blk, 1), g * GRP:(g + 1) * GRP], dense.bank(slot, g), ACT.Gelu_apprx_tanh).then_inc(dense.drained[g].sem, 1)


def branch_a(S):
    nc, io = S.nc, S.io
    WS = S.Z[:, 4, 0:4 * P].rearrange("p (g s) -> p g s", g=4)
    WT = S.Z[:, 5, 0:4 * P].rearrange("p (g t) -> p g t", g=4)
    BS = S.Z[0:A_G, 6, 0:P]
    SEL = S.Z[0:A_G, 7, 0:2 * P].rearrange("g (b c) -> g b c", b=2)
    BB = S.Z[:, 8, 0:2 * P].rearrange("p (b t) -> p b t", b=2)
    VT = S.Z[:, 6, 512:512 + 2 * P].rearrange("p (b t) -> p b t", b=2)
    VN = S.Z[:, 9, 0:A_W].rearrange("p (g c) -> p g c", g=A_G)
    SQ = S.Z[:, 9, A_W:2 * A_W].rearrange("p (g c) -> p g c", g=A_G)
    SV = S.Z[:, 10, 0:2 * P].rearrange("p (b t) -> p b t", b=2)
    loaded, sel, made = S.flag("ws_loaded", 16 * 5), S.flag("a_selector", 2), S.flag("a_constants")
    turned, copied = S.flag("ws_turned"), S.flag("ws_copied", 2)
    staged, v_turned = S.flag("v_staged"), S.flag("v_turned")
    norm = HeadNorm(S, "an", A_G, S.Z[:, 11, 0:A_W].rearrange("p (g c) -> p g c", g=A_G))
    mixed, biased, stored = S.flag("v_mixed"), S.flag("v_biased", 2), S.flag("a_stored")

    def round_pe(pe, t):
        pe.wait_ge(staged.sem, staged.at(t))
        if later(t):
            pe.wait_ge(norm.centred.sem, norm.centred.last(t))
        for b in range(2):
            tr = nc.tensor.transpose(S.PS[1][:, b * P:(b + 1) * P], VT[:, b, :], S.ident[:, :])
        tr.then_inc(v_turned.sem, 1)
        pe.wait_ge(norm.normed.sem, norm.normed.at(t))
        if later(t):
            pe.wait_ge(biased.sem, biased.last(t))
        for b in range(2):
            mm = nc.tensor.matmul(S.PS[2][:, b * 256:(b + 1) * 256], VN[:, 2 * b:2 * b + 2, :],
                                  WT[:, 2 * b:2 * b + 2, :], start=True, stop=True)
        mm.then_inc(mixed.sem, 1)

    def round_act(act, t, tok):
        if later(t):
            act.wait_ge(v_turned.sem, v_turned.last(t))
        S.apart(act)
        nc.scalar.copy(VT[:, :, :], S.Z[:, 2:4, ds(tok, P)]).then_inc(staged.sem, 1)
        norm.scalar(act, t)

    def round_dve(dve, t, tok):
        dve.wait_ge(v_turned.sem, v_turned.at(t))
        if later(t):
            dve.wait_ge(mixed.sem, mixed.last(t))
        norm.vector(dve, t, S.PS[1][:, 0:A_W].rearrange("p (g c) -> p g c", g=A_G), SQ, VN)
        dve.wait_ge(mixed.sem, mixed.at(t))
        for b in range(2):
            for half in range(2):
                rows = slice(N * half, N * half + N)
                ins = nc.vector.scalar_tensor_tensor(
                    out=SV[rows, b, :], in0=S.PS[2][rows, b * 256 + half * P:b * 256 + half * P + P],
                    scalar=S.param("gmlp_ln_g", b, 1)[rows, :], in1=BB[rows, b, :], op0=ALU.mult, op1=ALU.add)
            ins.then_inc(biased.sem, 1)
        dve.wait_ge(biased.sem, biased.at(t))
        nc.vector.tensor_tensor(S.YT[:, 0:2, ds(tok, P)], SV[:, :, :], S.Z[:, 0:2, ds(tok, P)], ALU.mult).then_inc(stored.sem, 1)

    with nc.Block() as block:
        @block.sync
        def _(sp):
            for g in range(A_G):
                sp.dma_start(WS[:, g, :], io["gmlp_w_s"][0, g]).then_inc(loaded.sem, 16)
            sp.dma_start(BS, io["gmlp_b_s"][0]).then_inc(loaded.sem, 16)

        @block.gpsimd
        def _(pool):
            nc.gpsimd.memset(SEL, 0.0).then_inc(sel.sem, 1)
            pool.wait_ge(sel.sem, sel.at(0, 1))
            nc.gpsimd.affine_select(out=SEL.rearrange("g b (h c) -> g b h c", h=2),
                                            in_=SEL.rearrange("g b (h c) -> g b h c", h=2),
                                            compare_op=ALU.not_equal, fill=1.0, base=0,
                                            pattern=[[-2, 2], [-1, 2], [0, N]], channel_multiplier=1).then_inc(sel.sem, 1)

        @block.tensor
        def _(pe):
            pe.wait_ge(loaded.sem, loaded.at())
            pe.wait_ge(sel.sem, sel.at())
            for g in range(A_G):
                nc.tensor.transpose(S.PS[0][:, g * P:(g + 1) * P], WS[:, g, :], S.ident[:, :])
            for b in range(2):
                mm = nc.tensor.matmul(S.PS[3][:, b * P:(b + 1) * P], SEL[:, b, :], BS, start=True, stop=True)
            mm.then_inc(turned.sem, 1)
            pe.wait_ge(copied.sem, copied.at())
            round_pe(pe, 0)
            with pe.Fori(1, NT) as t:
                round_pe(pe, t)

        @block.scalar
        def _(act):
            act.preload_act_table_set(EXP_LN)
            round_act(act, 0, 0)
            with act.Fori(1, NT) as t:
                round_act(act, t, act.snap(t * P, min_val=0, max_val=T - P))

        @block.vector
        def _(dve):
            dve.wait_ge(turned.sem, turned.at())
            nc.vector.tensor_copy(WT, S.PS[0][:, :].rearrange("p (g t) -> p g t", g=4)).then_inc(copied.sem, 1)
            nc.vector.tensor_copy(BB, S.PS[3][:, 0:2 * P].rearrange("p (b t) -> p b t", b=2)).then_inc(copied.sem, 1)
            dve.wait_ge(copied.sem, copied.at())
            round_dve(dve, 0, 0)
            with dve.Fori(1, NT) as t:
                round_dve(dve, t, dve.snap(t * P, min_val=0, max_val=T - P))

def project_b(S):
    nc, io = S.nc, S.io
    w_in = io["w_in"][0].rearrange("(k p) n -> p k n", p=P)
    dense = Dense(S, "b", slabs([lambda x: x[:, 6, :], lambda x: x[:, 7, :]], (S.YT, S.YTr)))
    ZP, CV = S.PAD[0:2], S.PAD[2:4]
    cleared = S.flag("b_pads_cleared", 2)
    centre, left, right = S.flag("conv_centre", 2), S.flag("conv_left", 2), S.flag("conv_right", 2, in_hand=2)
    silued = S.flag("qk_silued", 2, in_hand=2)
    at = PROWS["mlstm_conv"][0]
    with nc.Block() as block:
        @block.gpsimd
        def _(pool):
            dense.start(pool)
            pool.sem_inc(right.sem, right.in_hand)
            pool.sem_inc(silued.sem, silued.in_hand)
            for z in ZP:
                nc.gpsimd.memset(z[:, :], 0.0).then_inc(cleared.sem, 1)
            with pool.Fori(0, 6) as i:
                for slot in range(2):
                    dense.divide(pool, i, slot)

        @block.sync
        def _(sp):
            with sp.Fori(0, 6) as i:
                for slot in range(2):
                    dense.load(sp, i, slot, w_in[:, :, ds(i * 256 + OFF_QK + slot * P, P)])

        @block.tensor
        def _(pe):
            with pe.Fori(0, 6) as i:
                for slot in range(2):
                    dense.multiply(pe, i, slot, group(S.HTr), group(S.XTr))

        @block.scalar
        def _(act):
            act.wait_ge(cleared.sem, cleared.at())
            with act.Fori(0, 3) as i:
                for slot in range(2):
                    blk = act.snap(i * 2 + slot, min_val=0, max_val=5)
                    act.wait_ge(right.sem, right.last(i, slot + 1))
                    to_padded(S, dense, act, i, slot, ZP[slot])
                    act.wait_ge(right.sem, right.at(i, slot + 1))
                    S.apart(act)
                    for a, n, p in SEQS:
                        ins = nc.scalar.activation(S.Z[:, ds(blk, 1), a:a + n], CV[slot][:, p:p + n], ACT.Silu)
                    ins.then_inc(silued.sem, 1)
            with act.Fori(3, 6) as i:
                for slot in range(2):
                    blk = act.snap(i * 2 + slot, min_val=6, max_val=11)
                    for g in range(NG):
                        act.wait_ge(dense.summed.sem, dense.filled(i, slot, g))
                        S.apart(act)
                        nc.scalar.copy(S.Z[:, ds(blk, 1), g * GRP:(g + 1) * GRP], dense.bank(slot, g)).then_inc(dense.drained[g].sem, 1)
            act.wait_ge(dense.drained[NG - 1].sem, dense.drained[NG - 1].at(5))
            nc.scalar.activation(S.Z[:, 9:12, :], S.Z[:, 9:12, :], ACT.Sigmoid)

        @block.vector
        def _(dve):
            with dve.Fori(0, 3) as i:
                for slot in range(2):
                    tap = [dve.snap(i * 2 + (at + 6 * c + slot), min_val=0, max_val=N_PROWS - 1) for c in range(3)]
                    tap = [S.PT[:, ds(c, 1)] for c in tap]
                    z, cv = ZP[slot], CV[slot]
                    dve.wait_ge(dense.drained[NG - 1].sem, dense.drained[NG - 1].at(i, slot + 1))
                    dve.wait_ge(silued.sem, silued.last(i, slot + 1))
                    nc.vector.tensor_scalar(cv[:, 1:LAT0 + N_LAT], z[:, 1:LAT0 + N_LAT], tap[1], None, ALU.mult).then_inc(centre.sem, 1)
                    dve.wait_ge(centre.sem, centre.at(i, slot + 1))
                    nc.vector.scalar_tensor_tensor(
                        out=cv[:, 1:LAT0 + N_LAT], in0=z[:, 0:LAT0 + N_LAT - 1], scalar=tap[0],
                        in1=cv[:, 1:LAT0 + N_LAT], op0=ALU.mult, op1=ALU.add).then_inc(left.sem, 1)
                    dve.wait_ge(left.sem, left.at(i, slot + 1))
                    nc.vector.scalar_tensor_tensor(
                        out=cv[:, 1:LAT0 + N_LAT], in0=z[:, 2:LAT0 + N_LAT + 1], scalar=tap[2],
                        in1=cv[:, 1:LAT0 + N_LAT], op0=ALU.mult, op1=ALU.add).then_inc(right.sem, 1)


DIR_ROW = 32
ROWS = DIR_ROW + H


def last_in_time(x, d):
    return x[:, P - 1::P] if d == 0 else x[:, 0::P]


def gates_b(S, B):
    nc, io = S.nc, S.io
    WG = S.W[0]
    weights = S.flag("gate_weights", 2)
    I, F = B.I, B.F
    loaded, cleared = S.flag("gate_loads", 16 * 12), S.flag("gate_cleared", 10)
    summed, biased = S.flag("gates_summed", NG), S.flag("gates_biased", 2 * NG)
    folded, soft = S.flag("gates_folded"), S.flag("gates_soft", 2)
    rows, turned, spread = S.flag("gate_rows", 40), S.flag("gates_turned"), S.flag("gates_spread")
    prepared, out_m = S.flag("gates_prepared", 40), S.flag("m_out", 32)
    n_rows = [0]

    with nc.Block() as block:
        @block.gpsimd
        def _(pool):
            for x in (WG[:, :, :], B.VAL[:, :, :], B.gate_bias[:, :], B.m0[:, :]):
                nc.gpsimd.memset(x, 0.0).then_inc(cleared.sem, 1)
            nc.gpsimd.memset(B.reset[:, :], 1.0).then_inc(cleared.sem, 1)
            nc.gpsimd.memset(B.SEL[:, :, :], 0.0).then_inc(cleared.sem, 1)
            pool.wait_ge(cleared.sem, cleared.at(0, 6))
            nc.gpsimd.memset(B.reset[0:DIR_ROW, 0::P], 0.0).then_inc(cleared.sem, 1)
            pool.wait_ge(cleared.sem, cleared.at(0, 7))
            nc.gpsimd.memset(B.reset[DIR_ROW:2 * DIR_ROW, P - 1::P], 0.0).then_inc(cleared.sem, 1)
            pool.wait_ge(cleared.sem, cleared.at(0, 8))
            for d in range(2):
                v = B.SEL[:, d * H:(d + 1) * H, :]
                ins = nc.gpsimd.affine_select(out=v, in_=v, compare_op=ALU.not_equal, fill=1.0, base=-DIR_ROW * d,
                                              pattern=[[-1, H], [0, P]], channel_multiplier=1)
            pool.wait_ge(loaded.sem, loaded.at(0, 16 * 10))
            nc.gpsimd.tensor_copy(S.Wr[1][:, :, :], WG[:, :, :]).then_inc(weights.sem, 1)
            pool.wait_ge(weights.sem, weights.at(0, 1))
            nc.gpsimd.tensor_tensor(S.Wr[0][:, :, :], WG[:, :, :], plain(S.Wr[1][:, :, :]), ALU.subtract).then_inc(weights.sem, 1)
            pool.wait_ge(summed.sem, summed.at())
            nc.gpsimd.memset(B.M[:, :], 0.0).then_inc(cleared.sem, 1)
            nc.gpsimd.memset(B.C[:, :], 0.0).then_inc(cleared.sem, 1)

        @block.sync
        def _(sp):
            sp.wait_ge(cleared.sem, cleared.at(0, 4))
            w = io["w_in"][0].rearrange("(k p) n -> p k n", p=P)
            for d in range(2):
                for f in range(2):
                    a, c = OFF_G + 2 * H * d + H * f, 2 * DIR_ROW * f + DIR_ROW * d
                    sp.dma_start(WG[:, :, c:c + H], w[:, :, a:a + H]).then_inc(loaded.sem, 16)
                    sp.dma_start(B.gate_bias[DIR_ROW * d:DIR_ROW * d + H, f:f + 1],
                                 io["mlstm_gate_b"][0, d, f].unsqueeze(1)).then_inc(loaded.sem, 16)
                sp.dma_start(B.m0[DIR_ROW * d:DIR_ROW * d + H, :],
                             io["state_mlstm_m"][0, 0, d].unsqueeze(1)).then_inc(loaded.sem, 16)
            sp.wait_ge(rows.sem, rows.at(0, B.scans_done))
            for d in range(2):
                c = P - 1 if d == 0 else 0
                sp.dma_start(S.out[4][0, 0, d].unsqueeze(1), B.M[DIR_ROW * d:DIR_ROW * d + H, c:c + 1]).then_inc(out_m.sem, 16)
            sp.wait_ge(out_m.sem, out_m.at())

        @block.tensor
        def _(pe):
            pe.wait_ge(weights.sem, weights.at())
            for g in range(NG):
                for n, (w, x) in enumerate(((S.Wr[1], S.HTr), (S.Wr[0], S.HTr), (S.Wr[1], S.XTr))):
                    for k in range(KB):
                        mm = nc.tensor.matmul(S.PS[g][:, 0:GRP], w[:, k, :], x[:, k, g * GRP:(g + 1) * GRP],
                                              start=(n == 0 and k == 0), stop=(n == 2 and k == KB - 1))
                mm.then_inc(summed.sem, 1)
            pe.wait_ge(rows.sem, rows.at(0, B.rows_done))
            for q, x in enumerate((B.I, B.X2, B.M)):
                for t in range(NT):
                    c = t * ROWS
                    tr = nc.tensor.transpose(S.PS[3 + q][:, c:c + ROWS], x[0:ROWS, t * P:(t + 1) * P],
                                             S.ident[0:ROWS, 0:ROWS])
            tr.then_inc(turned.sem, 1)
            for d in range(2):
                r = slice(DIR_ROW * d, DIR_ROW * d + H)
                mm = nc.tensor.matmul(S.PS[6 + d][:, 0:3 * NT * H], S.ones[r, :],
                                      B.diag[r, :, :, :], start=True, stop=True)
            mm.then_inc(spread.sem, 1)

        @block.scalar
        def _(act):
            act.preload_act_table_set(EXP_LN)
            act.wait_ge(summed.sem, summed.at())
            for g in range(NG):
                for f, x in enumerate((I, F)):
                    nc.scalar.activation(x[0:2 * DIR_ROW, g * GRP:(g + 1) * GRP],
                                                    S.PS[g][2 * DIR_ROW * f:2 * DIR_ROW * (f + 1), 0:GRP],
                                                    ACT.Identity, bias=B.gate_bias[:, f:f + 1]).then_inc(biased.sem, 1)
            act.wait_ge(folded.sem, folded.at())
            nc.scalar.activation(B.X2[:, :], B.X2[:, :], ACT.Exp).then_inc(soft.sem, 1)
            act.wait_ge(soft.sem, soft.at(0, 1))
            nc.scalar.activation(B.X2[:, :], B.X2[:, :], ACT.Ln, bias=S.eps[0:2 * DIR_ROW, 2:3]).then_inc(soft.sem, 1)
            act.wait_ge(prepared.sem, prepared.at(0, B.logs_done))
            nc.scalar.activation(B.tok[:, :, :, 0:3, :], B.tok[:, :, :, 0:3, :], ACT.Exp)
            for half in range(2):
                r = slice(N * half, N * half + N)
                for d in range(2):
                    nc.scalar.activation(B.decay[r, d, :, :], B.spread[r, d, 2, :, half::2], ACT.Exp)

        @block.vector
        def _(dve):
            def row_op(ins):
                ins.then_inc(rows.sem, 1)
                n_rows[0] += 1
                dve.wait_ge(rows.sem, rows.at(0, n_rows[0]))

            dve.wait_ge(biased.sem, biased.at())
            dve.wait_ge(cleared.sem, cleared.at())
            nc.vector.scalar_tensor_tensor(out=B.X2[:, :], in0=F[:, :], scalar=-1.0, in1=F[:, :],
                                                      op0=ALU.mult, op1=ALU.min).then_inc(folded.sem, 1)
            dve.wait_ge(soft.sem, soft.at())
            row_op(nc.vector.scalar_tensor_tensor(out=F[:, :], in0=F[:, :], scalar=0.0, in1=B.X2[:, :],
                                                  op0=ALU.min, op1=ALU.subtract))
            for d in range(2):
                r = slice(DIR_ROW * d, DIR_ROW * d + H)

                def time(x, a, b, d=d, r=r):
                    return x[r, a:b] if d == 0 else x[r, a:b][:, ::-1]
                row_op(nc.vector.tensor_tensor_scan(time(B.C, 0, T), time(B.reset, 0, T), time(F, 0, T), 0.0,
                                                    ALU.mult, ALU.add))
                for a, b, first in ((0, N_CTX, 0.0), (N_CTX, T, B.m0[r, :])):
                    row_op(nc.vector.tensor_tensor_scan(time(B.M, a, b), time(F, a, b), time(I, a, b), first,
                                                        ALU.add, ALU.max))
            B_scans = n_rows[0]
            assert B_scans == B.scans_done
            row_op(nc.vector.tensor_tensor(I[:, :], I[:, :], B.C[:, :], ALU.subtract))
            row_op(nc.vector.tensor_tensor(B.X2[:, :], B.C[:, :], B.M[:, :], ALU.subtract))
            for d in range(2):
                r = slice(DIR_ROW * d, DIR_ROW * d + H)
                V, M, C = B.VAL[r, :, :], B.M[r, :], B.C[r, :]
                if d == 0:
                    nc.vector.tensor_copy(V[:, 0, 1:2], B.m0[r, :])
                    nc.vector.tensor_copy(V[:, 0, 2:NT], M[:, 2 * P - 1:T - P:P])
                else:
                    nc.vector.tensor_copy(V[:, 0, NT - 1:NT], B.m0[r, :])
                    nc.vector.tensor_copy(V[:, 0, 1:NT - 1], M[:, 2 * P::P])
                row_op(nc.vector.tensor_tensor(V[:, 1, :], last_in_time(C, d), last_in_time(M, d), ALU.subtract))
                row_op(nc.vector.tensor_tensor(V[:, 2, :], V[:, 1, :], V[:, 0, :], ALU.add))
                for h in range(H):
                    row_op(nc.vector.tensor_scalar(B.diag[r, :, :, h], V, S.ident[r, DIR_ROW * d + h:DIR_ROW * d + h + 1],
                                                   None, ALU.mult))
            assert n_rows[0] == B.rows_done
            dve.wait_ge(turned.sem, turned.at())
            dve.wait_ge(spread.sem, spread.at())
            n = 0

            def prepare(ins):
                nonlocal n
                ins.then_inc(prepared.sem, 1)
                n += 1

            def per_token(q, d):
                return S.PS[3 + q][:, 0:NT * ROWS].rearrange("p (t r) -> p t r", r=ROWS)[:, :, DIR_ROW * d:DIR_ROW * d + H]
            for d in range(2):
                prepare(nc.vector.tensor_copy(B.spread[:, d, :, :, :],
                                              S.PS[6 + d][:, 0:3 * NT * H].rearrange("p (q t h) -> p q t h", q=3, t=NT)))
            dve.wait_ge(prepared.sem, prepared.at(0, n))
            for d in range(2):
                tok = B.tok[:, d, :, :, :]
                prepare(nc.vector.tensor_tensor(tok[:, :, 0, :], per_token(1, d), B.spread[:, d, 0, :, :], ALU.add))
                prepare(nc.vector.tensor_tensor(tok[:, :, 1, :], per_token(0, d), B.spread[:, d, 1, :, :], ALU.add))
                prepare(nc.vector.tensor_scalar(tok[:, :, 2, :], per_token(2, d), -1.0, None, ALU.mult))
                prepare(nc.vector.tensor_copy(tok[:, :, 3, :], per_token(0, d)))
            assert n == B.logs_done


class StoreB:
    scans_done = 1 + 2 * 3
    rows_done = scans_done + 2 + 2 * (2 + H)
    logs_done = 2 + 2 * 4

    def __init__(self, S):
        area = Area(S.XT[:, :, :].rearrange("p k t -> p (k t)"))
        self.Hs = area.cut(NT, B_W)
        R = 2 * DIR_ROW
        self.I, self.F = area.cut(T, rows=R), area.cut(T, rows=R)
        self.C, self.M = area.cut(T, rows=R), area.cut(T, rows=R)
        self.X2 = S.RS[0:R, :]
        self.reset = S.PAD[0][0:R, 0:T]
        self.tok = area.cut(2, NT, 4, H)
        pads = Area(S.PAD[1][:, :])
        self.spread = pads.cut(2, 3, NT, H)
        self.VAL = pads.cut(3, NT, rows=R)
        self.diag = pads.cut(3, NT, H, rows=R)
        self.gate_bias = S.sb("gate_bias", R, 2)
        self.m0 = S.sb("m0", R, 1)
        self.decay = area.cut(2, NT, NP)
        self.SEL = Area(S.YT[:, 5:8, :].rearrange("p k t -> p (k t)")).cut(2 * H, P, rows=R)

def slot_of(h):
    return NP * (h % 2) + h // 2


def direction_tiles(eng, t):
    if isinstance(t, int):
        f, b = t, (NT - t) % NT
        return [f * P, b * P], [f, b]
    f = eng.snap(t * P, min_val=0, max_val=T - P)
    b = eng.snap(t * (-P) + T, min_val=0, max_val=T - P)
    return [f, b], [t, eng.snap(t * (-1) + NT, min_val=0, max_val=NT - 1)]


def recur_b(S, B):
    nc, io = S.nc, S.io
    pads = Area(S.PAD[2][:, :])
    QS, KS = pads.cut(NP, P), pads.cut(NP, P)
    VS = pads.cut(NP, P)
    pads = Area(S.PAD[3][:, :])
    KW, V1 = pads.cut(H, N), pads.cut(H, N + 1)
    DEN = pads.cut(2, H)
    yt = Area(S.YT[:, 2:5, :].rearrange("p k t -> p (k t)"))
    X2S, CUR = yt.cut(P, rows=2 * DIR_ROW), yt.cut(4, H)
    E, PM = yt.cut(H, P), yt.cut(H, P)
    HN, HH = yt.cut(H, N + 1), yt.cut(H, N)
    CS = [yt.cut(NP, 2 * (N + 1)) for _ in range(2)]
    MASK = yt.cut(2 * (N + 1))
    W2 = 2 * (N + 1)

    f = {k: S.flag("mlstm_" + k, 2) for k in (
        "staged_q", "staged_k", "staged_v", "staged_rows", "turned", "weighted_k", "copied_v", "scored",
        "exponents", "exped", "weighted_scores", "numerator", "inter", "update", "decayed", "updated",
        "gated", "summed", "den_abs", "den_max", "den_inv", "quotient", "h_added")}
    ready, loads, stores = S.flag("b_ready", 4), S.flag("b_state_loads", 16 * 24), S.flag("b_state_stores", 16 * 24)
    zeroed = S.flag("b_states_zeroed", 2)
    bK, bV, bS, bE, bN, bI = S.PS[0], S.PS[1], S.PS[2:4], S.PS[4:6], S.PS[6], S.PS[7]

    def head_rows(h):
        return slice(N * (h % 2), N * (h % 2) + N)

    def state_io(sp, flag, C, n, store):
        for d in range(2):
            for h in range(H):
                c = (N + 1) * (h % 2)
                for on_chip, dram in ((CS[d][head_rows(h), h // 2, c:c + N], C[0, 0, d, h]),
                                      (CS[d][head_rows(h), h // 2, c + N:c + N + 1], n[0, 0, d, h].unsqueeze(1))):
                    a, b = (dram, on_chip) if store else (on_chip, dram)
                    sp.dma_start(a, b).then_inc(flag.sem, 16)

    def round_pool(pool, t):
        tok, tile = direction_tiles(pool, t)
        for d in range(2):
            k = d + 1
            if later(t, k):
                pool.wait_ge(f["inter"].sem, f["inter"].front(t, k))
            S.apart(pool)
            nc.gpsimd.tensor_copy(QS, S.Z[:, 0:3, ds(tok[d], P)]).then_inc(f["staged_q"].sem, 1)
            if later(t, k):
                pool.wait_ge(f["turned"].sem, f["turned"].front(t, k))
            S.apart(pool)
            nc.gpsimd.tensor_copy(VS, S.Z[:, 6:9, ds(tok[d], P)]).then_inc(f["staged_v"].sem, 1)

    def round_pe(pe, t):
        for d in range(2):
            k = d + 1
            pe.wait_ge(f["staged_k"].sem, f["staged_k"].at(t, k))
            pe.wait_ge(f["staged_v"].sem, f["staged_v"].at(t, k))
            if later(t, k):
                pe.wait_ge(f["updated"].sem, f["updated"].front(t, k))
            if later(t, k):
                pe.wait_ge(f["copied_v"].sem, f["copied_v"].front(t, k))
            for p in range(NP):
                nc.tensor.transpose(bK[:, p * P:(p + 1) * P], KS[:, p, :], S.ident[:, :])
            for p in range(NP):
                tr = nc.tensor.transpose(bV[:, p * P:(p + 1) * P], VS[:, p, :], S.ident[:, :])
            tr.then_inc(f["turned"].sem, 1)
            pe.wait_ge(f["staged_q"].sem, f["staged_q"].at(t, k))
            if later(t, k):
                pe.wait_ge(f["weighted_scores"].sem, f["weighted_scores"].front(t, k))
            for h in range(H):
                mm = nc.tensor.matmul(bS[h % 2][:, (h // 2) * P:(h // 2 + 1) * P], KS[head_rows(h), h // 2, :],
                                      QS[head_rows(h), h // 2, :], start=True, stop=True)
            mm.then_inc(f["scored"].sem, 1)
            pe.wait_ge(f["staged_rows"].sem, f["staged_rows"].at(t, k))
            if later(t, k):
                pe.wait_ge(f["exped"].sem, f["exped"].front(t, k))
            for b in range(2):
                for i in range(3):
                    h, o = 2 * i + b, bE[b][:, i * P:(i + 1) * P]
                    nc.tensor.matmul(o, S.ident[:, :], S.neg[d][:, :], start=True, stop=False)
                    mm = nc.tensor.matmul(o, B.SEL[:, d * H + h, :], X2S, start=False, stop=True)
            mm.then_inc(f["exponents"].sem, 1)
            if later(t, k):
                pe.wait_ge(f["gated"].sem, f["gated"].front(t, k))
            if later(t):
                pe.wait_ge(f["updated"].sem, f["updated"].last(t, k))
            for p in range(NP):
                mm = nc.tensor.matmul(bI[:, p * W2:(p + 1) * W2], QS[:, p, :], CS[d][:, p, :], start=True, stop=True)
            mm.then_inc(f["inter"].sem, 1)
            pe.wait_ge(f["weighted_k"].sem, f["weighted_k"].at(t, k))
            pe.wait_ge(f["copied_v"].sem, f["copied_v"].at(t, k))
            for p in range(NP):
                mm = nc.tensor.matmul(bK[:, p * W2:(p + 1) * W2], KW[:, 2 * p:2 * p + 2, :],
                                      V1[:, 2 * p:2 * p + 2, :], start=True, stop=True)
            mm.then_inc(f["update"].sem, 1)
            pe.wait_ge(f["weighted_scores"].sem, f["weighted_scores"].at(t, k))
            if later(t, k):
                pe.wait_ge(f["summed"].sem, f["summed"].front(t, k))
            for h in range(H):
                mm = nc.tensor.matmul(bN[:, h * (N + 1):(h + 1) * (N + 1)], PM[:, slot_of(h), :], V1[:, h, :],
                                      start=True, stop=True)
            mm.then_inc(f["numerator"].sem, 1)

    def round_act(act, t):
        for d in range(2):
            k = d + 1
            act.wait_ge(f["turned"].sem, f["turned"].at(t, k))
            if later(t, k):
                act.wait_ge(f["numerator"].sem, f["numerator"].front(t, k))
            nc.scalar.copy(V1[:, :, 0:N], bV[:, 0:B_W].rearrange("p (h c) -> p h c", h=H)).then_inc(f["copied_v"].sem, 1)
            act.wait_ge(f["exponents"].sem, f["exponents"].at(t, k))
            act.wait_ge(f["staged_rows"].sem, f["staged_rows"].at(t, k))
            if later(t, k):
                act.wait_ge(f["weighted_scores"].sem, f["weighted_scores"].front(t, k))
            for h in range(H):
                ins = nc.scalar.activation(E[:, slot_of(h), :], bE[h % 2][:, (h // 2) * P:(h // 2 + 1) * P], ACT.Exp,
                                           bias=CUR[:, 3, h:h + 1])
            ins.then_inc(f["exped"].sem, 1)

    def round_dve(dve, t):
        tok, tile = direction_tiles(dve, t)
        for d in range(2):
            k = d + 1
            if later(t, k):
                dve.wait_ge(f["scored"].sem, f["scored"].front(t, k))
            nc.vector.tensor_scalar(KS, S.Z[:, 3:6, ds(tok[d], P)], N ** -0.5, None, ALU.mult).then_inc(f["staged_k"].sem, 1)
            if later(t, k):
                dve.wait_ge(f["exped"].sem, f["exped"].front(t, k))
            if later(t, k):
                dve.wait_ge(f["quotient"].sem, f["quotient"].front(t, k))
            S.apart(dve)
            nc.vector.tensor_copy(CUR, B.tok[:, d, ds(tile[d], 1), :, :])
            nc.vector.tensor_copy(X2S, B.X2[:, ds(tok[d], P)]).then_inc(f["staged_rows"].sem, 1)
            dve.wait_ge(f["turned"].sem, f["turned"].at(t, k))
            dve.wait_ge(f["staged_rows"].sem, f["staged_rows"].at(t, k))
            if later(t, k):
                dve.wait_ge(f["update"].sem, f["update"].front(t, k))
            nc.vector.tensor_tensor(
                KW, bK[:, 0:B_W].rearrange("p (h c) -> p h c", h=H),
                CUR[:, 1, :].unsqueeze(2).to_broadcast([P, H, N]), ALU.mult).then_inc(f["weighted_k"].sem, 1)
            dve.wait_ge(f["scored"].sem, f["scored"].at(t, k))
            dve.wait_ge(f["exped"].sem, f["exped"].at(t, k))
            if later(t, k):
                dve.wait_ge(f["numerator"].sem, f["numerator"].front(t, k))
            for b in range(2):
                ins = nc.vector.tensor_tensor(PM[:, 3 * b:3 * b + 3, :], E[:, 3 * b:3 * b + 3, :],
                                              bS[b][:, 0:3 * P].rearrange("p (h t) -> p h t", h=3), ALU.mult)
            ins.then_inc(f["weighted_scores"].sem, 1)
            dve.wait_ge(f["update"].sem, f["update"].at(t, k))
            dve.wait_ge(f["inter"].sem, f["inter"].at(t, k))
            for p in range(NP):
                ins = nc.vector.scalar_tensor_tensor(
                    out=CS[d][:, p, :], in0=CS[d][:, p, :], scalar=B.decay[:, d, ds(tile[d], 1), p:p + 1].rearrange("p a b -> p (a b)"),
                    in1=bK[:, p * W2:(p + 1) * W2], op0=ALU.mult, op1=ALU.add)
            ins.then_inc(f["decayed"].sem, 1)
            dve.wait_ge(f["decayed"].sem, f["decayed"].at(t, k))
            nc.vector.tensor_tensor(CS[d], CS[d], MASK.unsqueeze(1).to_broadcast([P, NP, W2]), ALU.mult).then_inc(f["updated"].sem, 1)
            nc.vector.tensor_tensor(
                HN, bI[:, 0:NP * W2].rearrange("p (h c) -> p h c", h=H),
                CUR[:, 0, :].unsqueeze(2).to_broadcast([P, H, N + 1]), ALU.mult).then_inc(f["gated"].sem, 1)
            dve.wait_ge(f["numerator"].sem, f["numerator"].at(t, k))
            dve.wait_ge(f["gated"].sem, f["gated"].at(t, k))
            nc.vector.tensor_tensor(
                HN, HN, bN[:, 0:NP * W2].rearrange("p (h c) -> p h c", h=H), ALU.add).then_inc(f["summed"].sem, 1)
            dve.wait_ge(f["summed"].sem, f["summed"].at(t, k))
            den = HN[:, :, N]
            nc.vector.scalar_tensor_tensor(out=DEN[:, 0, :], in0=den, scalar=-1.0, in1=den,
                                                            op0=ALU.mult, op1=ALU.max).then_inc(f["den_abs"].sem, 1)
            dve.wait_ge(f["den_abs"].sem, f["den_abs"].at(t, k))
            nc.vector.tensor_tensor(DEN[:, 1, :], DEN[:, 0, :], CUR[:, 2, :], ALU.max).then_inc(f["den_max"].sem, 1)
            dve.wait_ge(f["den_max"].sem, f["den_max"].at(t, k))
            nc.vector.reciprocal(DEN[:, 0, :], DEN[:, 1, :]).then_inc(f["den_inv"].sem, 1)
            dve.wait_ge(f["den_inv"].sem, f["den_inv"].at(t, k))
            nc.vector.tensor_tensor(
                HH, HN[:, :, 0:N], DEN[:, 0, :].unsqueeze(2).to_broadcast([P, H, N]), ALU.mult).then_inc(f["quotient"].sem, 1)
            dve.wait_ge(f["quotient"].sem, f["quotient"].at(t, k))
            hs = B.Hs[:, ds(tile[d], 1), :].rearrange("p a (h c) -> p (a h) c", h=H)
            nc.vector.tensor_tensor(hs, hs, HH, ALU.add).then_inc(f["h_added"].sem, 1)
            dve.wait_ge(f["h_added"].sem, f["h_added"].at(t, k))

    with nc.Block() as block:
        @block.sync
        def _(sp):
            sp.wait_ge(f["updated"].sem, f["updated"].at(0))
            state_io(sp, stores, S.out[2], S.out[3], True)
            sp.wait_ge(stores.sem, stores.at())
            state_io(sp, loads, io["state_mlstm_C"], io["state_mlstm_n"], False)

        @block.gpsimd
        def _(pool):
            round_pool(pool, 0)
            with pool.Fori(1, NT) as t:
                round_pool(pool, t)

        @block.tensor
        def _(pe):
            pe.wait_ge(ready.sem, ready.at())
            round_pe(pe, 0)
            pe.wait_ge(loads.sem, loads.at())
            with pe.Fori(1, NT) as t:
                round_pe(pe, t)

        @block.scalar
        def _(act):
            act.preload_act_table_set(EXP_LN)
            act.wait_ge(ready.sem, ready.at())
            round_act(act, 0)
            with act.Fori(1, NT) as t:
                round_act(act, t)

        @block.vector
        def _(dve):
            nc.vector.memset(B.Hs[:, :, :], 0.0)
            for d in range(2):
                nc.vector.memset(CS[d], 0.0).then_inc(ready.sem, 1)
            nc.vector.memset(V1, 1.0).then_inc(ready.sem, 1)
            nc.vector.memset(MASK, 0.0)
            nc.vector.memset(DEN, 0.0).then_inc(ready.sem, 1)
            dve.wait_ge(ready.sem, ready.at())
            nc.vector.memset(MASK[0:N, 0:N + 1], 1.0)
            nc.vector.memset(MASK[N:P, N + 1:W2], 1.0).then_inc(zeroed.sem, 1)
            dve.wait_ge(zeroed.sem, zeroed.at(0, 1))
            round_dve(dve, 0)
            dve.wait_ge(loads.sem, loads.at())
            with dve.Fori(1, NT) as t:
                round_dve(dve, t)


def finish_b(S, B):
    nc = S.nc
    pads = Area(S.PAD[2][:, :])
    HN, SQ, DEV = pads.cut(H, N), pads.cut(H, N), pads.cut(H, N)
    norm = HeadNorm(S, "bn", H, DEV)
    turned, stored = S.flag("bf_turned"), S.flag("bf_stored")
    at = PROWS["mlstm_out_g"][0]

    def round_pe(pe, t):
        pe.wait_ge(norm.normed.sem, norm.normed.at(t))
        if later(t):
            pe.wait_ge(stored.sem, stored.last(t))
        for p in range(NP):
            tr = nc.tensor.transpose(S.PS[0][:, p * P:(p + 1) * P], HN[:, 2 * p:2 * p + 2, :], S.ident[:, :])
        tr.then_inc(turned.sem, 1)

    def round_dve(dve, t):
        tile = t if isinstance(t, int) else t
        tok = 0 if isinstance(t, int) else dve.snap(t * P, min_val=0, max_val=T - P)
        if later(t):
            dve.wait_ge(turned.sem, turned.last(t))
        S.apart(dve)
        norm.vector(dve, t, B.Hs[:, ds(tile, 1), :].rearrange("p a (h c) -> p (a h) c", h=H), SQ, HN)
        dve.wait_ge(turned.sem, turned.at(t))
        for p in range(NP):
            ins = nc.vector.scalar_tensor_tensor(
                out=S.YT[:, 2 + p, ds(tok, P)], in0=S.PS[0][:, p * P:(p + 1) * P], scalar=S.PT[:, at + p:at + p + 1],
                in1=S.Z[:, 9 + p, ds(tok, P)], op0=ALU.mult, op1=ALU.mult)
        ins.then_inc(stored.sem, 1)

    with nc.Block() as block:
        @block.tensor
        def _(pe):
            round_pe(pe, 0)
            with pe.Fori(1, NT) as t:
                round_pe(pe, t)

        @block.scalar
        def _(act):
            act.preload_act_table_set(EXP_LN)
            norm.scalar(act, 0)
            with act.Fori(1, NT) as t:
                norm.scalar(act, t)

        @block.vector
        def _(dve):
            round_dve(dve, 0)
            with dve.Fori(1, NT) as t:
                round_dve(dve, t)


def project_c(S):
    nc, io = S.nc, S.io
    w_in = io["w_in"][0].rearrange("(k p) n -> p k n", p=P)
    dense = Dense(S, "c", [[Area(yt[:, 5:8, :].rearrange("p k t -> p (k t)")[:, 2 * PADW:]).cut(KB, P),
                            Area(rs[:, 24:]).cut(KB, P)] for yt, rs in ((S.YT, S.RS), (S.YTr, S.RSr))])
    low_loaded, low_back = S.flag("low_part_loaded", 16), S.flag("low_part_back", KB)
    ZP = S.PAD[0:2]
    SM = S.PAD[2:4]
    yt = Area(S.YT[:, 5:8, :].rearrange("p k t -> p (k t)"))
    CV = [yt.cut(PADW) for i in range(2)]
    half_mu, one_mu = S.RS[:, 0:12], S.RS[:, 12:24]
    cleared, coeffs = S.flag("c_pads_cleared", 2), S.flag("c_mu", 2)
    neighbours, own = S.flag("c_neighbours", 2), S.flag("c_own", 2)
    mixed = S.flag("c_mixed", 2, in_hand=2)
    with nc.Block() as block:
        @block.gpsimd
        def _(pool):
            dense.start(pool)
            pool.sem_inc(mixed.sem, mixed.in_hand)
            for z in ZP:
                nc.gpsimd.memset(z[:, :], 0.0).then_inc(cleared.sem, 1)
            with pool.Fori(0, 6) as i:
                for slot in range(2):
                    dense.divide(pool, i, slot)

        @block.sync
        def _(sp):
            for slot in range(2):
                dense.load(sp, 0, slot, w_in[:, :, OFF_C + slot * P:OFF_C + (slot + 1) * P])
            sp.dma_start(S.XT[:, :, :], S.low_dram).then_inc(low_loaded.sem, 16)
            with sp.Fori(1, 6) as i:
                for slot in range(2):
                    dense.load(sp, i, slot, w_in[:, :, ds(i * 256 + OFF_C + slot * P, P)])

        @block.tensor
        def _(pe):
            pe.wait_ge(low_back.sem, low_back.at())
            with pe.Fori(0, 6) as i:
                for slot in range(2):
                    dense.multiply(pe, i, slot, group(S.HTr), group(S.XTr))

        @block.scalar
        def _(act):
            act.wait_ge(low_loaded.sem, low_loaded.at())
            for k in range(KB):
                nc.scalar.copy(S.XTr[:, k, :], S.XT[:, k, :]).then_inc(low_back.sem, 1)
            act.wait_ge(cleared.sem, cleared.at())
            with act.Fori(0, 6) as i:
                for slot in range(2):
                    act.wait_ge(mixed.sem, mixed.last(i, slot + 1))
                    to_padded(S, dense, act, i, slot, ZP[slot])
            act.wait_ge(mixed.sem, mixed.at(5))
            nc.scalar.activation(S.Z[:, 9, :], S.Z[:, 9, :], ACT.Tanh)
            nc.scalar.activation(S.Z[:, 11, :], S.Z[:, 11, :], ACT.Sigmoid)

        @block.vector
        def _(dve):
            nc.vector.tensor_scalar(half_mu, S.param("rwkv_mu"), 0.5, None, ALU.mult).then_inc(coeffs.sem, 1)
            nc.vector.tensor_scalar(one_mu, S.param("rwkv_mu"), -1.0, 1.0, ALU.mult, ALU.add).then_inc(coeffs.sem, 1)
            dve.wait_ge(coeffs.sem, coeffs.at())
            with dve.Fori(0, 6) as i:
                for slot in range(2):
                    blk = dve.snap(i * 2 + slot, min_val=0, max_val=11)
                    dve.wait_ge(dense.drained[NG - 1].sem, dense.drained[NG - 1].at(i, slot + 1))
                    dve.wait_ge(mixed.sem, mixed.last(i, slot + 1))
                    nc.vector.tensor_tensor(SM[slot][:, 1:LAT0 + N_LAT], ZP[slot][:, 0:LAT0 + N_LAT - 1],
                                            ZP[slot][:, 2:LAT0 + N_LAT + 1], ALU.add).then_inc(neighbours.sem, 1)
                    nc.vector.tensor_scalar(CV[slot][:, 1:LAT0 + N_LAT], ZP[slot][:, 1:LAT0 + N_LAT],
                                                    one_mu[:, ds(blk, 1)], None, ALU.mult).then_inc(own.sem, 1)
                    dve.wait_ge(own.sem, own.at(i, slot + 1))
                    dve.wait_ge(neighbours.sem, neighbours.at(i, slot + 1))
                    for a, n, p in SEQS:
                        ins = nc.vector.scalar_tensor_tensor(
                            out=S.Z[:, ds(blk, 1), a:a + n].rearrange("p a n -> p (a n)"), in0=SM[slot][:, p:p + n],
                            scalar=half_mu[:, ds(blk, 1)], in1=CV[slot][:, p:p + n], op0=ALU.mult, op1=ALU.add)
                    ins.then_inc(mixed.sem, 1)


class StoreC:

    def __init__(self, S):
        X = Area(S.XT[:, :, :].rearrange("p k t -> p (k t)"))
        HA = Area(S.HT[:, :, :].rearrange("p k t -> p (k t)"))
        PD = [Area(p[:, :]) for p in S.PAD]
        W = [Area(w[:, :, :].rearrange("p k n -> p (k n)")) for w in S.W]
        self.A = X.cut(2, NP, T)
        self.nkk, self.Y = HA.cut(NP, T), HA.cut(NT, C_W)
        self.TI, self.TT, self.Zm = X.cut(H, P), X.cut(H, P), X.cut(H, P)
        self.LT, self.RB, self.AK = HA.cut(H, P), HA.cut(H, P), HA.cut(H, P)
        self.RK, self.BT = PD[0].cut(H, P), PD[0].cut(NP, P)
        yt = Area(S.YT[:, 5:8, :].rearrange("p k t -> p (k t)"))
        self.AR = [PD[1].cut(2, NP, P), yt.cut(2, NP, P)]
        self.KT = PD[1].cut(NP, P)
        self.Bt, self.Kt, self.Vt = (PD[2].cut(NP, P) for _ in range(3))
        self.U, self.Q, self.Sc = (PD[3].cut(NP, P) for _ in range(3))
        self.W2 = W[0].cut(2, C_W)
        rs = Area(S.RS[:, :])
        self.S = [rs.cut(NP, P) for _ in range(2)]
        self.VS = rs.cut(NP, P)
        self.A2 = W[1].cut(2, C_W)
        z = Area(S.Z[:, 10, :])
        self.EM, self.t1, self.t2 = z.cut(NP, P), z.cut(NP, P), z.cut(NP, P)
        w1 = Area(S.W[1][:, :, :].rearrange("p k n -> p (k n)"))
        self.SW = w1.cut(NP, P)
        self.cs = S.sb("c_sums", P, NP, P + 1)
        self.EP = [S.sb("c_decays", P, NP, P + 1), yt.cut(NP, P + 1)]
        self.half_w0 = yt.cut(2 * NP)
        self.mid = S.sb("c_mid", P, 3, NP)
        self.one_ka = S.sb("c_one_ka", P, NP)


def prepare_c(S, C):
    nc, io = S.nc, S.io
    kkr = [S.YT[:, 5 + p, :] for p in range(NP)]
    sq = [S.PAD[p][:, 0:T] for p in range(NP)]
    loaded, cleared = S.flag("cp_loads", 16 * 4), S.flag("cp_cleared", 2)
    squared, summed, rooted = S.flag("cp_squared", NP), S.flag("cp_summed", NP), S.flag("cp_rooted", NP)
    scaled, clipped, inverted = S.flag("cp_scaled", NP), S.flag("cp_clipped", NP), S.flag("cp_inverted", NP)
    lora, a_done, made = S.flag("cp_lora", 6), S.flag("cp_a", 6), S.flag("cp_levels")
    with nc.Block() as block:
        @block.gpsimd
        def _(pool):
            n = 0

            def one(ins):
                nonlocal n
                ins.then_inc(made.sem, 1)
                n += 1
                pool.wait_ge(made.sem, made.at(0, n))

            for w in (C.W2, C.A2):
                nc.gpsimd.memset(w, 0.0).then_inc(cleared.sem, 1)
            pool.wait_ge(cleared.sem, cleared.at())
            for d in range(2):
                for i in range(LEVELS):
                    b = 1 << i
                    m = S.level[:, d, i, :].rearrange("p (n h x) -> p n h x", h=2, x=b)
                    src = m[:, :, d, :]
                    one(nc.gpsimd.memset(S.level[:, d, i, :], 0.0))
                    one(nc.gpsimd.memset(src, 1.0))
                    first = b if d == 0 else 0
                    for base, mult, step in ((-first, 1, -2 * b), (first + b - 1, -1, 2 * b)):
                        one(nc.gpsimd.affine_select(out=src, in_=src, compare_op=ALU.is_ge, fill=0.0, base=base,
                                                    pattern=[[step, P // (2 * b)], [0, b]], channel_multiplier=mult))

        @block.sync
        def _(sp):
            sp.wait_ge(cleared.sem, cleared.at())
            for d in range(2):
                r = slice(N * d, N * d + N)
                sp.dma_start(C.W2[r, d, :], io["rwkv_w2"][0, d]).then_inc(loaded.sem, 16)
                sp.dma_start(C.A2[r, d, :], io["rwkv_a2"][0, d]).then_inc(loaded.sem, 16)

        @block.tensor
        def _(pe):
            for p in range(NP):
                pe.wait_ge(squared.sem, squared.at(0, p + 1))
                if p:
                    pe.wait_ge(rooted.sem, rooted.at(0, p))
                for g in range(NG):
                    mm = nc.tensor.matmul(S.PS[g][:, 0:GRP], S.halves[:, :], sq[p][:, g * GRP:(g + 1) * GRP],
                                          start=True, stop=True)
                mm.then_inc(summed.sem, 1)
            pe.wait_ge(loaded.sem, loaded.at())
            for d in range(2):
                for p in range(NP):
                    n = d * NP + p
                    if n:
                        pe.wait_ge(a_done.sem, a_done.at(0, n))
                    for g in range(NG):
                        mm = nc.tensor.matmul(S.PS[3 + g][:, 0:GRP], C.A2[:, d, p * P:(p + 1) * P],
                                              S.Z[:, 10, g * GRP:(g + 1) * GRP], start=True, stop=True)
                    mm.then_inc(lora.sem, 1)

        @block.scalar
        def _(act):
            for p in range(NP):
                act.wait_ge(scaled.sem, scaled.at(0, p + 1))
                nc.scalar.activation(sq[p], kkr[p], ACT.Square).then_inc(squared.sem, 1)
            for p in range(NP):
                act.wait_ge(summed.sem, summed.at(0, p + 1))
                for g in range(NG):
                    ins = nc.scalar.activation(sq[p][:, g * GRP:(g + 1) * GRP], S.PS[g][:, 0:GRP], ACT.Sqrt)
                ins.then_inc(rooted.sem, 1)
            for d in range(2):
                for p in range(NP):
                    act.wait_ge(lora.sem, lora.at(0, d * NP + p + 1))
                    for g in range(NG):
                        ins = nc.scalar.activation(C.A[:, d, p, g * GRP:(g + 1) * GRP], S.PS[3 + g][:, 0:GRP],
                                                   ACT.Sigmoid, bias=S.param("rwkv_a0", d * NP + p, 1))
                    ins.then_inc(a_done.sem, 1)

        @block.vector
        def _(dve):
            for p in range(NP):
                nc.vector.tensor_scalar(kkr[p], S.Z[:, 3 + p, :], S.param("rwkv_k_k", p, 1), None, ALU.mult).then_inc(scaled.sem, 1)
            nc.vector.tensor_scalar(C.one_ka[:, :], S.param("rwkv_k_a"), -1.0, 1.0, ALU.mult, ALU.add)
            for p in range(NP):
                dve.wait_ge(rooted.sem, rooted.at(0, p + 1))
                nc.vector.tensor_scalar(sq[p], sq[p], 1e-12, None, ALU.max).then_inc(clipped.sem, 1)
                dve.wait_ge(clipped.sem, clipped.at(0, p + 1))
                nc.vector.reciprocal(sq[p], sq[p]).then_inc(inverted.sem, 1)
                dve.wait_ge(inverted.sem, inverted.at(0, p + 1))
                nc.vector.scalar_tensor_tensor(out=C.nkk[:, p, :], in0=kkr[p], scalar=-1.0, in1=sq[p],
                                               op0=ALU.mult, op1=ALU.mult)


def recur_c(S, C):
    nc, io = S.nc, S.io
    names = ("decay_arg", "tanh", "sw", "summed", "middle", "exped", "staged_v", "a_rows", "r_rows", "b_rows", "k_rows",
             "k_dir", "a_em", "ka", "turned", "copied", "level0", "t_first", "seeded", "moved", "q", "q_copied",
             "u", "u_copied", "state", "y", "added", "new_state", "y_added")
    f = {k: S.flag("rwkv_" + k, 2) for k in names}
    gram, masked = S.flag("rwkv_gram", 2 * 10), S.flag("rwkv_masked", 2 * 10)
    n_lv = LEVELS - 1
    lt, zm = S.flag("rwkv_lt", 4 * n_lv), S.flag("rwkv_zm", 4 * n_lv)
    tz, grown = S.flag("rwkv_tz", 4 * n_lv), S.flag("rwkv_grown", 4 * n_lv)
    ready = S.flag("rwkv_ready", 3)
    s_out, s_in = S.flag("rwkv_state_stores", 16 * 12), S.flag("rwkv_state_loads", 16 * 12)
    s_turned, s_copied, s_cleared = S.flag("rwkv_state_turned", 2), S.flag("rwkv_state_copied", 4), S.flag("rwkv_cleared")
    bank = [S.PS[i][:, 0:3 * P] for i in range(8)]
    b3 = [b.rearrange("p (h t) -> p h t", h=3) for b in bank]
    A_of, R_ = [ar[:, 0, :, :] for ar in C.AR], [ar[:, 1, :, :] for ar in C.AR]
    w0_at, ka_at = PROWS["rwkv_w0"][0], PROWS["rwkv_k_a"][0]

    def rows_of(h):
        return slice(N * (h % 2), N * (h % 2) + N)

    def strict(d, turned):
        return S.tri["UPS" if (d == 0) == turned else "LOS"]

    def products(d):
        A_, R = A_of[d], R_[d]
        return (("L_turned", C.BT, A_, strict(d, True), C.LT),
                ("L", A_, C.BT, None, C.TI),
                ("AK", C.KT, A_, strict(d, True), C.AK),
                ("RB", C.BT, R, S.tri["UPI" if d == 0 else "LOI"], C.RB),
                ("RK", C.KT, R, S.tri["UPI" if d == 0 else "LOI"], C.RK))


    def following(eng, t, d):
        if d == 0:
            return t, 1
        return (t + 1 if isinstance(t, int) else eng.snap(t + 1, min_val=1, max_val=NT)), 0

    def prepare_pool(pool, t, d):
        tok, k = direction_tiles(pool, t)[0][d], d + 1
        if later(t, k):
            pool.wait_ge(f["turned"].sem, f["turned"].front(t, k))
        S.apart(pool)
        nc.gpsimd.tensor_copy(C.VS, S.Z[:, 6:9, ds(tok, P)]).then_inc(f["staged_v"].sem, 1)
        pool.wait_ge(f["exped"].sem, f["exped"].at(t, k))
        if later(t):
            pool.wait_ge(f["y"].sem, f["y"].last(t, k))
        S.apart(pool)
        off = 1 - d
        nc.gpsimd.tensor_tensor(R_[d], S.Z[:, 0:3, ds(tok, P)], C.EP[d][:, :, off:off + P],
                                ALU.mult).then_inc(f["r_rows"].sem, 1)

    def step_pool(pool, t, d, more=True):
        k = d + 1
        pool.wait_ge(masked.sem, masked.at(t, 10 * d + 2))
        nc.gpsimd.tensor_tensor(
            C.TT, C.LT, S.level[:, 1 - d, 0, :].unsqueeze(1).to_broadcast([P, H, P]), ALU.mult).then_inc(f["t_first"].sem, 1)
        pool.wait_ge(f["t_first"].sem, f["t_first"].at(t, k))
        nc.gpsimd.tensor_tensor(
            C.TT, C.TT, S.ident[:, :].unsqueeze(1).to_broadcast([P, H, P]), ALU.add).then_inc(f["seeded"].sem, 1)
        if more:
            prepare_pool(pool, *following(pool, t, d))

    def prepare_pe(pe, t, d):
        tok = direction_tiles(pe, t)[0][d]
        for p in range(NP):
            mm = nc.tensor.matmul(bank[6][:, p * P:(p + 1) * P], C.W2[:, d, p * P:(p + 1) * P],
                                  S.Z[:, 9, ds(tok, P)], start=True, stop=True)
        mm.then_inc(f["decay_arg"].sem, 1)

    def step_pe(pe, t, d, more=True):
        k, A_, R = d + 1, A_of[d], R_[d]
        for x in ("a_rows", "b_rows", "k_rows", "r_rows", "staged_v"):
            pe.wait_ge(f[x].sem, f[x].at(t, k))
        if later(t, k):
            pe.wait_ge(grown.sem, grown.front(t, 2 * n_lv * d + 1))
        for i, x in enumerate((C.BT, C.KT)):
            for p in range(NP):
                tr = nc.tensor.transpose(bank[4 + i][:, p * P:(p + 1) * P], x[:, p, :], S.ident[:, :])
        for i, (_, source, target, _, _) in enumerate(products(d)):
            for half in range(2):
                n = 2 * i + half
                if n >= 4:
                    pe.wait_ge(masked.sem, masked.at(t, 10 * d + n - 3))
                for j in range(NP):
                    h = 2 * j + half
                    mm = nc.tensor.matmul(bank[n % 4][:, j * P:(j + 1) * P], source[rows_of(h), h // 2, :],
                                          target[rows_of(h), h // 2, :], start=True, stop=True)
                mm.then_inc(gram.sem, 1)
        if later(t, k):
            pe.wait_ge(f["new_state"].sem, f["new_state"].front(t, k))
        for p in range(NP):
            tr = nc.tensor.transpose(bank[6][:, p * P:(p + 1) * P], C.VS[:, p, :], S.ident[:, :])
        tr.then_inc(f["turned"].sem, 1)
        pe.wait_ge(f["seeded"].sem, f["seeded"].at(t, k))
        pe.wait_ge(f["level0"].sem, f["level0"].at(t, k))
        pe.wait_ge(masked.sem, masked.at(t, 10 * d + 10))
        for i in range(n_lv):
            m = 2 * n_lv * d + 2 * i
            if i == 1 and more:
                prepare_pe(pe, *following(pe, t, d))
            for half in range(2):
                if i:
                    pe.wait_ge(grown.sem, grown.at(t, m - 2 + half + 1))
                for j in range(3):
                    x = 3 * half + j
                    mm = nc.tensor.matmul(bank[half][:, j * P:(j + 1) * P], C.LT[:, x, :], C.TI[:, x, :],
                                          start=True, stop=True)
                mm.then_inc(lt.sem, 1)
            if i == 0:
                pe.wait_ge(f["copied"].sem, f["copied"].at(t, k))
            for half in range(2):
                pe.wait_ge(zm.sem, zm.at(t, m + half + 1))
                if i < n_lv - 1:
                    for j in range(3):
                        x = 3 * half + j
                        nc.tensor.matmul(bank[2 + half][:, j * P:(j + 1) * P], C.TT[:, x, :], C.Zm[:, x, :],
                                         start=True, stop=True)
                for j in range(3):
                    x = 3 * half + j
                    mm = nc.tensor.matmul(bank[4 + half][:, j * P:(j + 1) * P], C.Zm[:, x, :], C.TT[:, x, :],
                                          start=True, stop=True)
                mm.then_inc(tz.sem, 1)
        pe.wait_ge(f["moved"].sem, f["moved"].at(t, k))
        if more:
            n, e = following(pe, t, d)
            pe.wait_ge(f["sw"].sem, f["sw"].at(n, e + 1))
        for h in range(H):
            if h % 2 == 0:
                nc.tensor.matmul(bank[6][:, h * N:(h + 2) * N], A_[:, h // 2, :], C.Sc[:, h // 2, :],
                                 start=True, stop=False)
            mm = nc.tensor.matmul(bank[6][:, h * N:(h + 1) * N], C.AK[:, slot_of(h), :],
                                  C.Vt[:, h // 2, N * (h % 2):N * (h % 2) + N], start=False, stop=(h % 2 == 1))
        mm.then_inc(f["q"].sem, 1)
        pe.wait_ge(grown.sem, grown.at(t, 2 * n_lv * (d + 1)))
        pe.wait_ge(f["q_copied"].sem, f["q_copied"].at(t, k))
        if later(t, k):
            pe.wait_ge(f["y_added"].sem, f["y_added"].front(t, k))
        for h in range(H):
            mm = nc.tensor.matmul(bank[7][:, h * N:(h + 1) * N], C.TT[:, slot_of(h), :],
                                  C.Q[:, h // 2, N * (h % 2):N * (h % 2) + N], start=True, stop=True)
        mm.then_inc(f["u"].sem, 1)
        pe.wait_ge(f["u_copied"].sem, f["u_copied"].at(t, k))
        for p in range(NP):
            nc.tensor.matmul(bank[6][:, p * P:(p + 1) * P], C.Bt[:, p, :], C.U[:, p, :], start=True, stop=False)
            mm = nc.tensor.matmul(bank[6][:, p * P:(p + 1) * P], C.Kt[:, p, :], C.Vt[:, p, :], start=False, stop=True)
        mm.then_inc(f["state"].sem, 1)
        for h in range(H):
            o, c = bank[7][:, h * N:(h + 1) * N], slice(N * (h % 2), N * (h % 2) + N)
            if h % 2 == 0:
                nc.tensor.matmul(bank[7][:, h * N:(h + 2) * N], R[:, h // 2, :], C.Sc[:, h // 2, :],
                                 start=True, stop=False)
            nc.tensor.matmul(o, C.RB[:, slot_of(h), :], C.U[:, h // 2, c], start=False, stop=False)
            mm = nc.tensor.matmul(o, C.RK[:, slot_of(h), :], C.Vt[:, h // 2, c], start=False, stop=(h % 2 == 1))
        mm.then_inc(f["y"].sem, 1)

    def prepare_act(act, t, d):
        k, own = d + 1, slice(1 - d, 1 - d + P)
        act.wait_ge(f["decay_arg"].sem, f["decay_arg"].at(t, k))
        if later(t, k):
            act.wait_ge(f["summed"].sem, f["summed"].front(t, k))
        for p in range(NP):
            ins = nc.scalar.activation(C.SW[:, p, :], bank[6][:, p * P:(p + 1) * P], ACT.Tanh,
                                       bias=C.half_w0[:, d * NP + p:d * NP + p + 1], scale=0.5)
        ins.then_inc(f["tanh"].sem, 1)
        act.wait_ge(f["tanh"].sem, f["tanh"].at(t, k))
        nc.scalar.activation(C.SW, C.SW, ACT.Identity, bias=S.eps[:, 3:4], scale=0.5).then_inc(f["sw"].sem, 1)
        act.wait_ge(f["middle"].sem, f["middle"].at(t, k))
        if later(t, k):
            for x in ("b_rows", "k_rows", "moved"):
                act.wait_ge(f[x].sem, f[x].front(t, k))
        if later(t):
            act.wait_ge(f["r_rows"].sem, f["r_rows"].last(t, k))
            act.wait_ge(f["new_state"].sem, f["new_state"].last(t, k))
        for p in range(NP):
            nc.scalar.activation(C.EP[d][:, p, :], C.cs[:, p, :], ACT.Exp, scale=-DECAY, bias=C.mid[:, 0, p:p + 1])
            nc.scalar.activation(C.EM[:, p, :], C.cs[:, p, own], ACT.Exp, scale=DECAY, bias=C.mid[:, 1, p:p + 1])
        nc.scalar.activation(C.mid[:, 2, :], C.mid[:, 1, :], ACT.Exp).then_inc(f["exped"].sem, 1)

    def step_act(act, t, d, more=True):
        k = d + 1
        act.wait_ge(f["turned"].sem, f["turned"].at(t, k))
        if later(t, k):
            act.wait_ge(f["y"].sem, f["y"].front(t, k))
        for i, x in enumerate((C.Bt, C.Kt, C.Vt)):
            ins = nc.scalar.copy(x, b3[4 + i])
        ins.then_inc(f["copied"].sem, 1)
        if more:
            prepare_act(act, *following(act, t, d))
        act.wait_ge(f["q"].sem, f["q"].at(t, k))
        nc.scalar.copy(C.Q, b3[6]).then_inc(f["q_copied"].sem, 1)
        act.wait_ge(f["u"].sem, f["u"].at(t, k))
        nc.scalar.copy(C.U, b3[7]).then_inc(f["u_copied"].sem, 1)

    def sum_dve(dve, t, d):
        k, own = d + 1, slice(1 - d, 1 - d + P)
        dve.wait_ge(f["sw"].sem, f["sw"].at(t, k))
        if later(t, k):
            dve.wait_ge(f["exped"].sem, f["exped"].front(t, k))
            dve.wait_ge(f["moved"].sem, f["moved"].front(t, k))
        zero = C.cs[:, :, 0:1] if d == 0 else C.cs[:, :, P:P + 1]
        nc.vector.memset(zero, 0.0)
        for p in range(NP):
            o, x = C.cs[:, p, own], C.SW[:, p, :]
            if d:
                o, x = o[:, ::-1], x[:, ::-1]
            ins = nc.vector.tensor_tensor_scan(o, S.ones[:, :], x, 0.0, ALU.mult, ALU.add)
        ins.then_inc(f["summed"].sem, 1)
        dve.wait_ge(f["summed"].sem, f["summed"].at(t, k))
        nc.vector.tensor_scalar(C.mid[:, 0, :], C.cs[:, :, P // 2], DECAY, None, ALU.mult)
        nc.vector.tensor_scalar(C.mid[:, 1, :], C.cs[:, :, P // 2], -DECAY, None, ALU.mult).then_inc(f["middle"].sem, 1)

    def rows_dve(dve, t, d):
        k, past, A_ = d + 1, slice(d, d + P), A_of[d]
        at = ds(direction_tiles(dve, t)[0][d], P)
        if later(t, k):
            dve.wait_ge(f["k_rows"].sem, f["k_rows"].front(t, k))
        for p in range(NP):
            ins = nc.vector.tensor_scalar(C.t2[:, p, :], C.A[:, d, p, at], S.PT[:, ka_at + p:ka_at + p + 1],
                                          C.one_ka[:, p:p + 1], ALU.mult, ALU.add)
        ins.then_inc(f["ka"].sem, 1)
        dve.wait_ge(f["exped"].sem, f["exped"].at(t, k))
        nc.vector.tensor_tensor(C.t1, C.A[:, d, :, at], C.EM, ALU.mult).then_inc(f["a_em"].sem, 1)
        dve.wait_ge(f["ka"].sem, f["ka"].at(t, k))
        nc.vector.tensor_tensor(C.t2, C.t2, S.Z[:, 3:6, at], ALU.mult).then_inc(f["k_dir"].sem, 1)
        if later(t, k):
            dve.wait_ge(f["turned"].sem, f["turned"].front(t, k))
        dve.wait_ge(f["a_em"].sem, f["a_em"].at(t, k))
        nc.vector.scalar_tensor_tensor(out=C.BT, in0=C.nkk[:, :, at], scalar=-1.0, in1=C.t1,
                                       op0=ALU.mult, op1=ALU.mult).then_inc(f["b_rows"].sem, 1)
        dve.wait_ge(f["k_dir"].sem, f["k_dir"].at(t, k))
        nc.vector.tensor_tensor(C.KT, C.t2, C.EM, ALU.mult).then_inc(f["k_rows"].sem, 1)
        if later(t):
            dve.wait_ge(f["q"].sem, f["q"].last(t, k))
        nc.vector.tensor_tensor(A_, C.nkk[:, :, at], C.EP[d][:, :, past], ALU.mult).then_inc(f["a_rows"].sem, 1)

    def step_dve(dve, t, d, more=True):
        k = d + 1
        tile = direction_tiles(dve, t)[1][d]
        if later(t, k):
            dve.wait_ge(f["new_state"].sem, f["new_state"].front(t, k))
        nc.vector.tensor_tensor(
            C.Sc, C.S[d], C.mid[:, 2, :].unsqueeze(2).to_broadcast([P, NP, P]), ALU.mult).then_inc(f["moved"].sem, 1)
        for i, (name, _, _, mask, dst) in enumerate(products(d)):
            for half in range(2):
                n = 2 * i + half
                dve.wait_ge(gram.sem, gram.at(t, 10 * d + n + 1))
                m = S.level[:, d, 0, :] if mask is None else mask[:, :]
                nc.vector.tensor_tensor(dst[:, 3 * half:3 * half + 3, :], b3[n % 4],
                                        m.unsqueeze(1).to_broadcast([P, 3, P]), ALU.mult).then_inc(masked.sem, 1)
            if name == "L":
                dve.wait_ge(masked.sem, masked.at(t, 10 * d + 4))
                nc.vector.tensor_tensor(
                    C.TI, C.TI, S.ident[:, :].unsqueeze(1).to_broadcast([P, H, P]), ALU.add).then_inc(f["level0"].sem, 1)
        dve.wait_ge(f["seeded"].sem, f["seeded"].at(t, k))
        for i in range(n_lv):
            m = 2 * n_lv * d + 2 * i
            for half in range(2):
                dve.wait_ge(lt.sem, lt.at(t, m + half + 1))
                if i:
                    dve.wait_ge(tz.sem, tz.at(t, m - 2 + half + 1))
                nc.vector.tensor_tensor(
                    C.Zm[:, 3 * half:3 * half + 3, :], b3[half],
                    S.level[:, d, i + 1, :].unsqueeze(1).to_broadcast([P, 3, P]), ALU.mult).then_inc(zm.sem, 1)
            for half in range(2):
                dve.wait_ge(tz.sem, tz.at(t, m + half + 1))
                x = slice(3 * half, 3 * half + 3)
                if i < n_lv - 1:
                    nc.vector.tensor_tensor(C.TI[:, x, :], C.TI[:, x, :], b3[2 + half], ALU.add)
                nc.vector.tensor_tensor(C.TT[:, x, :], C.TT[:, x, :], b3[4 + half], ALU.add).then_inc(grown.sem, 1)
            if i == 2 and more:
                sum_dve(dve, *following(dve, t, d))
        if more:
            rows_dve(dve, *following(dve, t, d))
        dve.wait_ge(f["state"].sem, f["state"].at(t, k))
        dve.wait_ge(f["y"].sem, f["y"].at(t, k))
        nc.vector.tensor_tensor(C.Sc, C.Sc, b3[6], ALU.add).then_inc(f["added"].sem, 1)
        dve.wait_ge(f["added"].sem, f["added"].at(t, k))
        end = P if d == 0 else 0
        for p in range(NP):
            ins = nc.vector.scalar_tensor_tensor(out=C.S[d][:, p, :], in0=C.Sc[:, p, :], scalar=C.EP[d][:, p, end:end + 1],
                                                 in1=S.halves[:, :], op0=ALU.mult, op1=ALU.mult)
        ins.then_inc(f["new_state"].sem, 1)
        y = C.Y[:, ds(tile, 1), :].rearrange("p a c -> p (a c)")
        if later(t, k):
            dve.wait_ge(f["y_added"].sem, f["y_added"].front(t, k))
        nc.vector.tensor_tensor(y, y, bank[7], ALU.add).then_inc(f["y_added"].sem, 1)

    def rounds(eng, step, between=None):
        for d in range(2):
            step(eng, 0, d)
        if between:
            between(eng)
        with eng.Fori(1, NT - 1) as t:
            for d in range(2):
                step(eng, t, d)
        step(eng, NT - 1, 0)
        step(eng, NT - 1, 1, more=False)

    staging = [C.Q, C.U]

    with nc.Block() as block:
        @block.sync
        def _(sp):
            for store in (True, False):
                if store:
                    sp.wait_ge(s_copied.sem, s_copied.at(0, 2))
                else:
                    sp.wait_ge(s_out.sem, s_out.at())
                    sp.wait_ge(s_cleared.sem, s_cleared.at())
                dram = S.out[5] if store else io["state_rwkv_S"]
                for d in range(2):
                    for h in range(H):
                        on_chip = staging[d][rows_of(h), h // 2, N * (h % 2):N * (h % 2) + N]
                        a, b = (dram[0, 0, d, h], on_chip) if store else (on_chip, dram[0, 0, d, h])
                        sp.dma_start(a, b).then_inc((s_out if store else s_in).sem, 16)

        @block.gpsimd
        def _(pool):
            pool.wait_ge(ready.sem, ready.at())
            prepare_pool(pool, 0, 0)
            rounds(pool, step_pool)

        @block.tensor
        def _(pe):
            def states(pe):
                pe.wait_ge(f["new_state"].sem, f["new_state"].at(0))
                pe.wait_ge(f["y_added"].sem, f["y_added"].at(0))
                for d in range(2):
                    for p in range(NP):
                        tr = nc.tensor.transpose(bank[4 + d][:, p * P:(p + 1) * P], C.S[d][:, p, :], S.ident[:, :])
                tr.then_inc(s_turned.sem, 1)
                pe.wait_ge(s_in.sem, s_in.at())
                for d in range(2):
                    for p in range(NP):
                        tr = nc.tensor.transpose(bank[4 + d][:, p * P:(p + 1) * P], staging[d][:, p, :], S.ident[:, :])
                tr.then_inc(s_turned.sem, 1)
                pe.wait_ge(s_copied.sem, s_copied.at())
            pe.wait_ge(ready.sem, ready.at())
            prepare_pe(pe, 0, 0)
            rounds(pe, step_pe, states)

        @block.scalar
        def _(act):
            act.preload_act_table_set(EXP_TANH)
            act.wait_ge(ready.sem, ready.at())
            prepare_act(act, 0, 0)
            rounds(act, step_act)

        @block.vector
        def _(dve):
            def states(dve):
                dve.wait_ge(s_turned.sem, s_turned.at(0, 1))
                for d in range(2):
                    nc.vector.tensor_copy(staging[d], b3[4 + d]).then_inc(s_copied.sem, 1)
                dve.wait_ge(s_out.sem, s_out.at())
                nc.vector.memset(staging[0], 0.0)
                nc.vector.memset(staging[1], 0.0).then_inc(s_cleared.sem, 1)
                dve.wait_ge(s_turned.sem, s_turned.at(0, 2))
                for d in range(2):
                    nc.vector.tensor_copy(C.S[d], b3[4 + d]).then_inc(s_copied.sem, 1)
                dve.wait_ge(s_copied.sem, s_copied.at())
            nc.vector.memset(S.eps[:, 3:4], 0.5)
            nc.vector.memset(C.Y, 0.0)
            for d in range(2):
                nc.vector.memset(C.S[d], 0.0).then_inc(ready.sem, 1)
            nc.vector.tensor_scalar(C.half_w0, S.PT[:, w0_at:w0_at + 2 * NP], 0.5, None, ALU.mult)
            nc.vector.memset(C.mid[:, :, :], 0.0).then_inc(ready.sem, 1)
            dve.wait_ge(ready.sem, ready.at())
            sum_dve(dve, 0, 0)
            rows_dve(dve, 0, 0)
            rounds(dve, step_dve, states)


def finish_c(S, C):
    nc, io = S.nc, S.io
    DEV, SQ, YN = C.TI[:, 0:3, :], C.TI[:, 3:6, :], C.TT[:, 0:3, :]
    as_heads = lambda x: x.rearrange("p a b -> p (a b)").rearrange("p (h c) -> p h c", h=H)
    DEV, SQ, YN = as_heads(DEV), as_heads(SQ), as_heads(YN)
    KS, M, BV, OUT = C.LT[:, 0:3, :], C.LT[:, 3:6, :], C.RB[:, 0:3, :], C.RB[:, 3:6, :]
    G2 = Area(S.PAD[0][:, :]).cut(C_W)
    coef = C.mid
    norm = HeadNorm(S, "cn", H, DEV)
    names = ("a_sum", "k_scale", "k_both", "r_k", "bonus", "bonus_v", "gate", "turned", "normed_v", "stored")
    f = {k: S.flag("cf_" + k) for k in names}
    loaded, ready = S.flag("cf_g2", 16), S.flag("cf_coef")
    ka, rk, lng = (PROWS[x][0] for x in ("rwkv_k_a", "rwkv_r_k", "rwkv_ln_g"))

    def round_pe(pe, t):
        tok = 0 if isinstance(t, int) else pe.snap(t * P, min_val=0, max_val=T - P)
        if later(t):
            pe.wait_ge(f["stored"].sem, f["stored"].last(t))
        for p in range(NP):
            mm = nc.tensor.matmul(S.PS[0][:, p * P:(p + 1) * P], G2[:, p * P:(p + 1) * P], S.Z[:, 11, ds(tok, P)],
                                  start=True, stop=True)
        mm.then_inc(f["gate"].sem, 1)
        pe.wait_ge(f["r_k"].sem, f["r_k"].at(t))
        nc.tensor.matmul(S.PS[1][:, 0:3 * P], S.halves[:, :], M, start=True, stop=True).then_inc(f["bonus"].sem, 1)
        pe.wait_ge(norm.normed.sem, norm.normed.at(t))
        for p in range(NP):
            tr = nc.tensor.transpose(S.PS[2][:, p * P:(p + 1) * P], YN[:, 2 * p:2 * p + 2, :], S.ident[:, :])
        tr.then_inc(f["turned"].sem, 1)

    def round_dve(dve, t):
        tok = 0 if isinstance(t, int) else dve.snap(t * P, min_val=0, max_val=T - P)
        at = ds(tok, P)
        if later(t):
            dve.wait_ge(f["bonus"].sem, f["bonus"].last(t))
        nc.vector.tensor_tensor(KS, C.A[:, 0, :, at], C.A[:, 1, :, at], ALU.add).then_inc(f["a_sum"].sem, 1)
        dve.wait_ge(f["a_sum"].sem, f["a_sum"].at(t))
        for p in range(NP):
            ins = nc.vector.tensor_scalar(KS[:, p, :], KS[:, p, :], S.PT[:, ka + p:ka + p + 1], coef[:, 0, p:p + 1],
                                          ALU.mult, ALU.add)
        ins.then_inc(f["k_scale"].sem, 1)
        dve.wait_ge(f["k_scale"].sem, f["k_scale"].at(t))
        nc.vector.tensor_tensor(KS, KS, S.Z[:, 3:6, at], ALU.mult).then_inc(f["k_both"].sem, 1)
        dve.wait_ge(f["k_both"].sem, f["k_both"].at(t))
        for p in range(NP):
            ins = nc.vector.scalar_tensor_tensor(out=M[:, p, :], in0=KS[:, p, :], scalar=S.PT[:, rk + p:rk + p + 1],
                                                 in1=S.Z[:, p, at], op0=ALU.mult, op1=ALU.mult)
        ins.then_inc(f["r_k"].sem, 1)
        if later(t):
            dve.wait_ge(f["turned"].sem, f["turned"].last(t))
        S.apart(dve)
        norm.vector(dve, t, C.Y[:, ds(t, 1), :].rearrange("p a (h c) -> p (a h) c", h=H), SQ, YN)
        dve.wait_ge(f["bonus"].sem, f["bonus"].at(t))
        nc.vector.tensor_tensor(BV, S.Z[:, 6:9, at], S.PS[1][:, 0:3 * P].rearrange("p (h t) -> p h t", h=3),
                                                 ALU.mult).then_inc(f["bonus_v"].sem, 1)
        dve.wait_ge(f["bonus_v"].sem, f["bonus_v"].at(t))
        dve.wait_ge(f["turned"].sem, f["turned"].at(t))
        for p in range(NP):
            ins = nc.vector.scalar_tensor_tensor(out=OUT[:, p, :], in0=S.PS[2][:, p * P:(p + 1) * P],
                                                 scalar=S.PT[:, lng + p:lng + p + 1], in1=BV[:, p, :],
                                                 op0=ALU.mult, op1=ALU.add)
        ins.then_inc(f["normed_v"].sem, 1)
        dve.wait_ge(f["normed_v"].sem, f["normed_v"].at(t))
        dve.wait_ge(f["gate"].sem, f["gate"].at(t))
        nc.vector.tensor_tensor(S.YT[:, 5:8, at], OUT,
                                                S.PS[0][:, 0:3 * P].rearrange("p (h t) -> p h t", h=3), ALU.mult).then_inc(f["stored"].sem, 1)

    with nc.Block() as block:
        @block.sync
        def _(sp):
            sp.dma_start(G2, io["rwkv_g2"][0]).then_inc(loaded.sem, 16)

        @block.tensor
        def _(pe):
            pe.wait_ge(loaded.sem, loaded.at())
            round_pe(pe, 0)
            with pe.Fori(1, NT) as t:
                round_pe(pe, t)

        @block.scalar
        def _(act):
            act.preload_act_table_set(EXP_LN)
            norm.scalar(act, 0)
            with act.Fori(1, NT) as t:
                norm.scalar(act, t)

        @block.vector
        def _(dve):
            nc.vector.tensor_scalar(coef[:, 0, :], C.one_ka[:, :], 2.0, None, ALU.mult).then_inc(ready.sem, 1)
            dve.wait_ge(ready.sem, ready.at())
            round_dve(dve, 0)
            with dve.Fori(1, NT) as t:
                round_dve(dve, t)


def residual(S, dve, dense, r, slot, blk, col):
    nc = S.nc
    for g in range(NG):
        dve.wait_ge(dense.summed.sem, dense.filled(r, slot, g))
        parts = ((0, N_CTX, 0), (N_CTX, GRP, 1)) if g == 0 else ((0, GRP, 1),)
        for a, b, c in parts:
            x = S.XT[:, ds(blk, 1), g * GRP + a:g * GRP + b].rearrange("p a n -> p (a n)")
            ins = nc.vector.scalar_tensor_tensor(
                out=x, in0=S.PS[3 * slot + g][:, a:b], scalar=S.MOD[:, ds(col, 1), c:c + 1].rearrange("p a b -> p (a b)"),
                in1=x, op0=ALU.mult, op1=ALU.add)
        ins.then_inc(dense.drained[g].sem, 1)


def project_out(S):
    nc, io = S.nc, S.io
    dense, restored = Dense(S, "o", slabs([lambda x: x[:, 8, :], lambda x: x[:, 9, :]], (S.Z, S.Zr))), S.flag("residual_restored", 16)
    split, left = S.flag("branches_rounded", KB), S.flag("branches_left", KB)
    w = io["w_out"][0].rearrange("(k p) n -> p k n", p=P)
    with nc.Block() as block:
        @block.gpsimd
        def _(pool):
            dense.start(pool)
            with pool.Fori(0, 4) as i:
                for slot in range(2):
                    dense.divide(pool, i, slot)

        @block.scalar
        def _(act):
            for k in range(KB):
                nc.scalar.copy(S.HTr[:, k, :], S.YT[:, k, :]).then_inc(split.sem, 1)

        @block.sync
        def _(sp):
            for slot in range(2):
                dense.load(sp, 0, slot, w[:, :, slot * P:(slot + 1) * P])
            sp.dma_start(S.XT[:, :, :], S.x_dram).then_inc(restored.sem, 16)
            with sp.Fori(1, 4) as i:
                for slot in range(2):
                    dense.load(sp, i, slot, w[:, :, ds(i * 256 + slot * P, P)])

        @block.tensor
        def _(pe):
            pe.wait_ge(left.sem, left.at())
            with pe.Fori(0, 4) as i:
                for slot in range(2):
                    dense.multiply(pe, i, slot, group(S.HTr), group(S.YTr))

        @block.vector
        def _(dve):
            for k in range(KB):
                dve.wait_ge(split.sem, split.at(0, k + 1))
                nc.vector.tensor_tensor(S.YTr[:, k, :], S.YT[:, k, :], plain(S.HTr[:, k, :]), ALU.subtract).then_inc(left.sem, 1)
            dve.wait_ge(restored.sem, restored.at())
            with dve.Fori(0, 4) as i:
                for slot in range(2):
                    blk = dve.snap(i * 2 + slot, min_val=0, max_val=KB - 1)
                    col = dve.snap(i * 2 + (slot + 2 * KB), min_val=0, max_val=N_MOD * KB - 1)
                    residual(S, dve, dense, i, slot, blk, col)


def mlp(S):
    nc, io = S.nc, S.io
    HB = 4
    n_q = D_FF // (HB * P)
    UP, DOWN = HB // 2, KB // 2
    up = Dense(S, "up", slabs([lambda x: x[:, 8, :], lambda x: x[:, 9, :]], (S.Z, S.Zr)))
    rows = [lambda x: x[:, 10, :], lambda x: x[:, 11, :]]
    down = Dense(S, "down", slabs(rows, (S.Z, S.Zr), HB), slabs(rows, (S.Zr,), HB, HB * P)[0], HB)
    w1 = io["mlp_w1"][0].rearrange("(k p) n -> p k n", p=P)
    w2 = io["mlp_w2"][0].rearrange("(q k p) n -> p q k n", p=P, k=HB)
    R = [x[:, 0:T] for x in S.PAD[0:2]]
    squared, kept = S.flag("relu_squared", 2 * NG), S.flag("hidden_rounded", 2 * NG)
    hidden = S.flag("hidden_left", 2 * NG, in_hand=2 * NG)

    def blocks(eng, i, slot):
        return (eng.snap(i * 2 + slot, min_val=0, max_val=HB - 1),
                eng.snap(i * 2 + (slot + HB), min_val=HB, max_val=2 * HB - 1))

    def part(x, blk, g):
        return x[:, ds(blk, 1), g * GRP:(g + 1) * GRP].rearrange("p a n -> p (a n)")

    with nc.Block() as block:
        @block.sync
        def _(sp):
            up.start(sp)
            down.start(sp)
            sp.sem_inc(hidden.sem, hidden.in_hand)
            with sp.Fori(0, n_q) as q:
                with sp.Fori(0, UP) as i:
                    r = sp.snap(q * UP + i, min_val=0, max_val=UP * n_q - 1)
                    for slot in range(2):
                        up.load(sp, r, slot, w1[:, :, ds(q * (HB * P) + i * 256 + slot * P, P)])
                with sp.Fori(0, DOWN) as i:
                    r = sp.snap(q * DOWN + i, min_val=0, max_val=DOWN * n_q - 1)
                    for slot in range(2):
                        down.load(sp, r, slot,
                                  w2[:, ds(q, 1), :, ds(i * 256 + slot * P, P)].rearrange("p q k n -> p (q k) n"))

        @block.gpsimd
        def _(pool):
            with pool.Fori(0, n_q) as q:
                with pool.Fori(0, UP) as i:
                    r = pool.snap(q * UP + i, min_val=0, max_val=UP * n_q - 1)
                    for slot in range(2):
                        up.divide(pool, r, slot)
                with pool.Fori(0, DOWN) as i:
                    r = pool.snap(q * DOWN + i, min_val=0, max_val=DOWN * n_q - 1)
                    for slot in range(2):
                        down.divide(pool, r, slot)

        @block.tensor
        def _(pe):
            with pe.Fori(0, n_q) as q:
                with pe.Fori(0, UP) as i:
                    r = pe.snap(q * UP + i, min_val=0, max_val=UP * n_q - 1)
                    for d in down.drained:
                        pe.wait_ge(d.sem, d.at(q * DOWN, 0))
                    for slot in range(2):
                        up.multiply(pe, r, slot, group(S.HTr), group(S.Zr))
                with pe.Fori(0, DOWN) as i:
                    r = pe.snap(q * DOWN + i, min_val=0, max_val=DOWN * n_q - 1)
                    for d in up.drained:
                        pe.wait_ge(d.sem, d.at(q * UP + (UP - 1)))
                    pe.wait_ge(hidden.sem, hidden.at(q * UP + (UP - 1)))
                    for slot in range(2):
                        down.multiply(pe, r, slot, group(S.YTr), group(S.YTr, HB))

        @block.scalar
        def _(act):
            with act.Fori(0, n_q) as q:
                with act.Fori(0, UP) as i:
                    r = act.snap(q * UP + i, min_val=0, max_val=UP * n_q - 1)
                    for slot in range(2):
                        blk, _ = blocks(act, i, slot)
                        for g in range(NG):
                            n = NG * slot + g + 1
                            act.wait_ge(hidden.sem, hidden.last(r, n))
                            act.wait_ge(up.summed.sem, up.filled(r, slot, g))
                            nc.scalar.activation(R[slot][:, g * GRP:(g + 1) * GRP], up.bank(slot, g),
                                                 ACT.Relu).then_inc(up.drained[g].sem, 1)
                            for d in down.drained:
                                act.wait_ge(d.sem, d.at(q * DOWN, 0))
                            act.wait_ge(squared.sem, squared.at(r, n))
                            S.apart(act)
                            nc.scalar.copy(part(S.YTr, blk, g), R[slot][:, g * GRP:(g + 1) * GRP]).then_inc(kept.sem, 1)

        @block.vector
        def _(dve):
            with dve.Fori(0, n_q) as q:
                with dve.Fori(0, UP) as i:
                    r = dve.snap(q * UP + i, min_val=0, max_val=UP * n_q - 1)
                    for slot in range(2):
                        blk, low = blocks(dve, i, slot)
                        for g in range(NG):
                            n = NG * slot + g + 1
                            x = R[slot][:, g * GRP:(g + 1) * GRP]
                            dve.wait_ge(up.drained[g].sem, up.drained[g].at(r, slot + 1))
                            nc.vector.tensor_tensor(x, x, x, ALU.mult).then_inc(squared.sem, 1)
                            dve.wait_ge(kept.sem, kept.at(r, n))
                            S.apart(dve)
                            nc.vector.tensor_tensor(part(S.YTr, low, g), x, plain(part(S.YTr, blk, g)),
                                                    ALU.subtract).then_inc(hidden.sem, 1)
                with dve.Fori(0, DOWN) as i:
                    r = dve.snap(q * DOWN + i, min_val=0, max_val=DOWN * n_q - 1)
                    for slot in range(2):
                        blk = dve.snap(i * 2 + slot, min_val=0, max_val=KB - 1)
                        col = dve.snap(i * 2 + (slot + 5 * KB), min_val=0, max_val=N_MOD * KB - 1)
                        residual(S, dve, down, r, slot, blk, col)


def leave(S):
    nc = S.nc
    ST = [S.HT[:, i, 0:KB * P].rearrange("p (k n) -> p k n", k=KB) for i in range(2)]
    OUT = [S.HT[:, 2 + i, 0:D] for i in range(2)]
    scaled = [S.flag(f"leave_scaled{i}") for i in range(2)]
    turned = [S.flag(f"leave_turned{i}", 1, in_hand=1) for i in range(2)]
    copied = [S.flag(f"leave_copied{i}", 1, in_hand=1) for i in range(2)]
    stored = [S.flag(f"leave_stored{i}", 16, in_hand=16) for i in range(2)]

    def over_tiles(eng, body):
        body(0, 0, 0)
        with eng.Fori(1, NT // 2 + 1) as i:
            body(eng.snap(i * 2 - 1, min_val=1, max_val=NT - 1), 1, eng.snap(i - 1, min_val=0, max_val=NT))
            body(eng.snap(i * 2, min_val=1, max_val=NT - 1), 0, i)

    with nc.Block() as block:
        @block.gpsimd
        def _(pool):
            for fl in (turned, copied, stored):
                for x in fl:
                    pool.sem_inc(x.sem, x.in_hand)

        @block.vector
        def _(dve):
            def body(t, s, j):
                tok = 0 if isinstance(t, int) else dve.snap(t * P, min_val=0, max_val=T - P)
                dve.wait_ge(turned[s].sem, turned[s].last(j))
                for k in range(KB):
                    ins = nc.vector.scalar_tensor_tensor(out=ST[s][:, k, :], in0=S.XT[:, k, ds(tok, P)],
                                                         scalar=S.param("final_g", k, 1), in1=S.RS[:, ds(tok, P)],
                                                         op0=ALU.mult, op1=ALU.mult)
                ins.then_inc(scaled[s].sem, 1)
            over_tiles(dve, body)

        @block.tensor
        def _(pe):
            def body(t, s, j):
                pe.wait_ge(scaled[s].sem, scaled[s].at(j))
                pe.wait_ge(copied[s].sem, copied[s].last(j))
                for k in range(KB):
                    tr = nc.tensor.transpose(S.PS[2 * s + k // 4][:, (k % 4) * P:(k % 4 + 1) * P], ST[s][:, k, :],
                                             S.ident[:, :])
                tr.then_inc(turned[s].sem, 1)
            over_tiles(pe, body)

        @block.scalar
        def _(act):
            def body(t, s, j):
                act.wait_ge(turned[s].sem, turned[s].at(j))
                act.wait_ge(stored[s].sem, stored[s].last(j))
                for b in range(2):
                    ins = nc.scalar.copy(OUT[s][:, b * 512:(b + 1) * 512], S.PS[2 * s + b][:, :])
                ins.then_inc(copied[s].sem, 1)
            over_tiles(act, body)

        @block.sync
        def _(sp):
            def body(t, s, j):
                sp.wait_ge(copied[s].sem, copied[s].at(j))
                if isinstance(t, int):
                    dst = S.out[0][0]
                else:
                    dst = S.out[1][0, ds(t * P - P, P), :]
                sp.dma_start(dst, OUT[s]).then_inc(stored[s].sem, 16)
            over_tiles(sp, body)
            sp.wait_ge(stored[0].sem, stored[0].at(NT // 2))
            sp.wait_ge(stored[1].sem, stored[1].at(NT // 2 - 1))


def program(nc, io, out):
    with ExitStack() as ctx:
        S = Store(nc, ctx, io, out)
        allocate(S)
        S.always = ctx.enter_context(nc.semaphore("always"))
        S.x_dram = nc.dram_tensor("residual", (P, KB, T), F32, kind="Internal").ap()
        S.low_dram = nc.dram_tensor("low_part", (P, KB, T), F32, kind="Internal").ap()
        S.RS, S.RSr = S.sb2("RS", P, T)
        nc.scalar.preload_act_table_set(EXP_LN)
        setup(S)
        enter(S)
        square_sums(S, "n1")
        S.low_saved = S.flag("low_part_saved", 16)
        modulate(S, "n1", 0, S.XT, S.XTr)
        project_a(S)
        branch_a(S)
        S.release()
        project_b(S)
        B = StoreB(S)
        gates_b(S, B)
        recur_b(S, B)
        finish_b(S, B)
        S.release()
        project_c(S)
        C = StoreC(S)
        prepare_c(S, C)
        recur_c(S, C)
        S.release()
        finish_c(S, C)
        project_out(S)
        square_sums(S, "n2")
        modulate(S, "n2", 1, S.Z, S.Zr)
        S.release()
        mlp(S)
        square_sums(S, "fin")
        leave(S)


def kernel(**inputs):
    import numpy as _np
    import concourse.bacc as _bacc
    from concourse import mybir as _mybir
    from concourse.bass_utils import run_bass_kernel_spmd as _run

    nc = _bacc.Bacc("TRN2", target_bir_lowering=False, num_devices=1)
    arrays, io = {}, {}
    for name, (shape, _) in SHAPES.items():
        a = _np.ascontiguousarray(inputs[name])
        arrays["in_" + name] = a
        io[name] = nc.dram_tensor("in_" + name, shape, _mybir.dt.from_np(a.dtype), kind="ExternalInput").ap()
    out = [nc.dram_tensor(f"out_{i}", s, _mybir.dt.float32, kind="ExternalOutput").ap() for i, s in enumerate(OUTS)]
    program(nc, io, out)
    r = _run(nc, [arrays], core_ids=[0])
    return tuple(r.results[0][f"out_{i}"] for i in range(len(OUTS)))
```

```python
import concourse.bass as bass
from concourse import mybir
from contextlib import ExitStack
import math

F32 = mybir.dt.float32
F32R = mybir.dt.float32r
ALU = mybir.AluOpType
ACT = mybir.ActivationFunctionType
AX = mybir.AxisListType
ds = bass.ds

P = 128
D = 1024
KB = D // P
N_CTX, N_LAT = 128, 1024
T = N_CTX + N_LAT
NT = T // P
GRP = 384
NG = T // GRP
H, N = 6, 64
NP = H // 2
A_W, A_G = 256, 4
B_W = C_W = H * N
OFF_QK, OFF_V, OFF_O, OFF_G = 512, 1280, 1664, 2048
OFF_C = OFF_G + 24
IN_COLS = OFF_C + 3 * C_W + 384
D_FF = 4 * D
N_MOD = 6
EPS, HEAD_EPS = 1e-6, 1e-5
LEVELS = 7
DECAY = math.exp(-0.5)
GELU = 2.0 * math.sqrt(2.0 / math.pi)
NEG = -1e30
CTX0, LAT0, PADW = 1, N_CTX + 2, T + 4

PROWS = {}
_at = 0
for _name, _n in (("b_mod", 48), ("norm1_g", 8), ("norm2_g", 8), ("final_g", 8), ("mlstm_conv", 18),
                  ("rwkv_mu", 12), ("rwkv_w0", 6), ("rwkv_a0", 6), ("rwkv_k_k", 3), ("rwkv_k_a", 3),
                  ("rwkv_r_k", 3), ("rwkv_ln_g", 3), ("gmlp_ln_g", 2), ("mlstm_out_g", 3),
                  ("c", 8), ("c_ctx", 8)):
    PROWS[_name] = (_at, _n)
    _at += _n
N_PROWS = _at


class Flag:

    def __init__(self, sem, q=1, in_hand=0):
        self.sem, self.q, self.in_hand = sem, q, in_hand

    def at(self, j=0, k=None):
        return j * self.q + (self.q if k is None else k) + self.in_hand

    def last(self, j, k=None):
        return j * self.q - self.q + (self.q if k is None else k) + self.in_hand

    def front(self, j, k):
        return j * self.q + k - 1 + self.in_hand


def later(j, k=1):
    return not isinstance(j, int) or j > 0 or k > 1


def plain(x):
    return x.bitcast(F32)


class Store:

    def __init__(self, nc, ctx, io, out):
        self.nc, self.ctx, self.io, self.out = nc, ctx, io, out
        self.sems = []

    def sb(self, name, *shape):
        return self.ctx.enter_context(self.nc.sbuf_tensor(name, list(shape), F32))

    def sb2(self, name, *shape):
        with self.nc.sbuf_tensor(name + "_r", list(shape), F32R) as r:
            pass
        x = self.sb(name, *shape)
        return x, r

    def half(self, name, *shape):
        return self.ctx.enter_context(self.nc.sbuf_tensor(name, list(shape), mybir.dt.bfloat16))

    def sem(self, name):
        self.sems.append(self.nc.alloc_semaphore(name=name))
        return self.sems[-1]

    def release(self):
        self.nc.clear_and_free_semaphores(self.sems)
        self.nc.all_engine_barrier()
        self.sems = []

    def apart(self, eng):
        eng.wait_ge(self.always, 1)

    def flag(self, name, q=1, in_hand=0):
        return Flag(self.sem(name), q, in_hand)

    def param(self, name, i=0, n=None):
        at, count = PROWS[name]
        return self.PT[:, at + i:at + i + (count - i if n is None else n)]


def allocate(S):
    S.XT, S.XTr = S.sb2("XT", P, KB, T)
    S.HT, S.HTr = S.sb2("HT", P, KB, T)
    S.YT, S.YTr = S.sb2("YT", P, KB, T)
    S.Z, S.Zr = S.sb2("Z", P, 12, T)
    slabs = [S.sb2(f"W{i}", P, KB, P) for i in range(2)]
    S.W, S.Wr = [x[0] for x in slabs], [x[1] for x in slabs]
    S.PAD = [S.sb(f"PAD{i}", P, PADW) for i in range(4)]
    S.PT = S.sb("PT", P, N_PROWS)
    S.MOD = S.sb("MOD", P, 48, 2)
    S.GS = S.sb("GSC", P, 2, KB, 2)
    S.ident = S.sb("ident", P, P)
    S.ones = S.sb("ones", P, P)
    S.halves = S.sb("halves", P, P)
    S.tri = {k: S.sb(f"tri_{k}", P, P) for k in ("UPS", "UPI", "LOS", "LOI")}
    S.level = S.half("level", P, 2, LEVELS, P)
    S.neg = [S.sb(f"neg{d}", P, P) for d in range(2)]
    S.eps = S.sb("eps", P, 4)
    S.PS = [S.ctx.enter_context(S.nc.psum_tensor(f"bank{i}", [P, 512], F32)) for i in range(8)]


def setup(S):
    nc, io = S.nc, S.io
    rows = [S.Z[:, 0, 0:P], S.Z[:, 0, P:2 * P]]
    loaded, turned, done = S.flag("params_loaded"), S.flag("params_turned"), S.flag("params_done")
    made, copied = S.flag("constants_made"), S.flag("constants_copied")
    lead = S.flag("rows_cleared")

    with nc.Block() as block:
        @block.vector
        def _(dve):
            dve.sem_inc(S.always, 1)
            nc.vector.memset(S.Z[:, 0, 0:2 * P], 0.0).then_inc(lead.sem, 1)
            nc.vector.memset(S.ones[:, :], 1.0)
            nc.vector.memset(S.eps[:, 0:1], EPS)
            nc.vector.memset(S.eps[:, 1:2], HEAD_EPS)
            nc.vector.memset(S.eps[:, 2:3], 1.0)
            nc.vector.memset(S.halves[0:N, 0:N], 1.0)
            nc.vector.memset(S.halves[N:P, N:P], 1.0)
            nc.vector.memset(S.halves[0:N, N:P], 0.0)
            nc.vector.memset(S.halves[N:P, 0:N], 0.0)
            dve.wait_ge(turned.sem, turned.at())
            nc.vector.tensor_copy(S.PT[:, 0:P], S.PS[0][:, 0:P])
            nc.vector.tensor_copy(S.PT[:, P:N_PROWS], S.PS[0][:, P:N_PROWS])

        @block.sync
        def _(sp):
            sp.wait_ge(lead.sem, lead.at())
            n = 0
            for name, (at, count) in PROWS.items():
                src = io[name].rearrange(SHAPES[name][1], p=P)
                for r in (0, 1):
                    a, b = max(at, r * P), min(at + count, r * P + P)
                    if a < b:
                        sp.dma_start(rows[r][a - r * P:b - r * P, :], src[a - at:b - at, :]).then_inc(loaded.sem, 16)
                        n += 1
            S.n_param_loads = n

        @block.gpsimd
        def _(pool):
            n = 0

            def done_one(ins):
                nonlocal n
                ins.then_inc(made.sem, 1)
                n += 1
                pool.wait_ge(made.sem, made.at(0, n))

            def keep(view, pattern, base, mult, op=ALU.is_ge, fill=0.0):
                done_one(nc.gpsimd.affine_select(out=view, in_=view, compare_op=op, fill=fill, base=base,
                                                 pattern=pattern, channel_multiplier=mult))

            done_one(nc.gpsimd.memset(S.ident[:, :], 0.0))
            keep(S.ident[:, :], [[-1, P]], 0, 1, ALU.not_equal, 1.0)
            for k, (base, mult, step) in {"UPS": (-1, -1, 1), "UPI": (0, -1, 1),
                                          "LOS": (-1, 1, -1), "LOI": (0, 1, -1)}.items():
                done_one(nc.gpsimd.memset(S.tri[k][:, :], 1.0))
                keep(S.tri[k][:, :], [[step, P]], base, mult)
            for d, (mult, step) in enumerate(((-1, 1), (1, -1))):
                done_one(nc.gpsimd.memset(S.neg[d][:, :], 0.0))
                keep(S.neg[d][:, :], [[step, P]], 0, mult, fill=NEG)

        @block.tensor
        def _(pe):
            pe.wait_ge(loaded.sem, loaded.at(0, 16 * S.n_param_loads))
            pe.wait_ge(made.sem, made.at(0, 2))
            nc.tensor.transpose(S.PS[0][:, 0:P], rows[0], S.ident[:, :])
            nc.tensor.transpose(S.PS[0][:, P:2 * P], rows[1], S.ident[:, :]).then_inc(turned.sem, 1)


SHAPES = {
    "x_prompt": ((1, N_CTX, D), None), "x_sample": ((1, N_LAT, D), None), "c": ((1, D), "a (k p) -> (a k) p"),
    "state_mlstm_C": ((1, 1, 2, H, N, N), None), "state_mlstm_n": ((1, 1, 2, H, N), None),
    "state_mlstm_m": ((1, 1, 2, H), None), "state_rwkv_S": ((1, 1, 2, H, N, N), None),
    "c_ctx": ((D,), "(k p) -> k p"), "norm1_g": ((1, D), "a (k p) -> (a k) p"),
    "norm2_g": ((1, D), "a (k p) -> (a k) p"), "w_mod": ((1, D, N_MOD * D), None),
    "b_mod": ((1, N_MOD * D), "a (k p) -> (a k) p"), "w_in": ((1, D, IN_COLS), None), "w_out": ((1, D, D), None),
    "gmlp_ln_g": ((1, A_W), "a (k p) -> (a k) p"), "gmlp_w_s": ((1, A_G, P, P), None),
    "gmlp_b_s": ((1, A_G, P), None), "mlstm_conv": ((1, 3, 2 * B_W), "a c (k p) -> (a c k) p"),
    "mlstm_gate_b": ((1, 2, 2, H), None), "mlstm_out_g": ((1, B_W), "a (k p) -> (a k) p"),
    "rwkv_mu": ((1, 3 * C_W + 384), "a (k p) -> (a k) p"), "rwkv_w0": ((1, 2, C_W), "a r (k p) -> (a r k) p"),
    "rwkv_w2": ((1, 2, 64, C_W), None), "rwkv_a0": ((1, 2, C_W), "a r (k p) -> (a r k) p"),
    "rwkv_a2": ((1, 2, 64, C_W), None), "rwkv_g2": ((1, 128, C_W), None),
    "rwkv_k_k": ((1, C_W), "a (k p) -> (a k) p"), "rwkv_k_a": ((1, C_W), "a (k p) -> (a k) p"),
    "rwkv_r_k": ((1, C_W), "a (k p) -> (a k) p"), "rwkv_ln_g": ((1, C_W), "a (k p) -> (a k) p"),
    "mlp_w1": ((1, D, D_FF), None), "mlp_w2": ((1, D_FF, D), None), "final_g": ((D,), "(k p) -> k p"),
}
OUTS = [(1, N_CTX, D), (1, N_LAT, D), (1, 1, 2, H, N, N), (1, 1, 2, H, N), (1, 1, 2, H), (1, 1, 2, H, N, N)]


EXP_LN, EXP_TANH = "natural_log_exp_and_others", "exp_and_others"


class Area:

    def __init__(self, flat):
        self.flat, self.at = flat, 0

    def cut(self, *shape, rows=P):
        n = math.prod(shape)
        a = self.flat[0:rows, self.at:self.at + n]
        self.at += n
        assert self.at <= self.flat.shape[1], "the region is full"
        if len(shape) > 1:
            names = "abcde"[:len(shape)]
            a = a.rearrange(f"p ({' '.join(names)}) -> p {' '.join(names)}", **dict(zip(names, shape)))
        return a


class SquareSums:

    def __init__(self, S, tag):
        self.S = S
        self.squared, self.added = S.flag(f"{tag}_squared", KB), S.flag(f"{tag}_added", KB)
        self.summed, self.logged = S.flag(f"{tag}_summed"), S.flag(f"{tag}_logged", NG)
        self.SQ, self.total = [S.YT[:, 3 + i, :] for i in range(2)], S.YT[:, 2, :]

    def square(self, act):
        nc, S = self.S.nc, self.S
        for k in range(KB):
            if k >= 2:
                act.wait_ge(self.added.sem, self.added.at(0, k - 1))
            nc.scalar.activation(self.SQ[k % 2], S.XT[:, k, :], ACT.Square).then_inc(self.squared.sem, 1)

    def add(self, dve):
        nc = self.S.nc
        for k in range(KB):
            dve.wait_ge(self.squared.sem, self.squared.at(0, k + 1))
            if k == 0:
                nc.vector.tensor_copy(self.total, self.SQ[0]).then_inc(self.added.sem, 1)
            else:
                dve.wait_ge(self.added.sem, self.added.at(0, k))
                nc.vector.tensor_tensor(self.total, self.total, self.SQ[k % 2], ALU.add).then_inc(self.added.sem, 1)

    def sum(self, pe):
        nc, S = self.S.nc, self.S
        pe.wait_ge(self.added.sem, self.added.at())
        for g in range(NG):
            mm = nc.tensor.matmul(S.PS[g][:, 0:GRP], S.ones[:, :], self.total[:, g * GRP:(g + 1) * GRP],
                                  start=True, stop=True)
        mm.then_inc(self.summed.sem, 1)

    def invert(self, act):
        nc, S = self.S.nc, self.S
        act.wait_ge(self.summed.sem, self.summed.at())
        for g in range(NG):
            nc.scalar.activation(S.RS[:, g * GRP:(g + 1) * GRP], S.PS[g][:, 0:GRP], ACT.Ln,
                                 bias=S.eps[:, 0:1], scale=1.0 / D).then_inc(self.logged.sem, 1)
        act.wait_ge(self.logged.sem, self.logged.at())
        nc.scalar.activation(S.RS[:, :], S.RS[:, :], ACT.Exp, scale=-0.5)


def square_sums(S, tag):
    sums = SquareSums(S, tag)
    with S.nc.Block() as block:
        @block.scalar
        def _(act):
            sums.square(act)
            sums.invert(act)

        @block.vector
        def _(dve):
            sums.add(dve)

        @block.tensor
        def _(pe):
            sums.sum(pe)


def modulate(S, tag, which, low, low_r):
    nc = S.nc
    scaled, gained = S.flag(f"{tag}_scaled", KB), S.flag(f"{tag}_gained")
    shifted, split = S.flag(f"{tag}_shifted", KB), S.flag(f"{tag}_rounded", KB)
    left = S.flag(f"{tag}_left", KB)
    with nc.Block() as block:
        @block.vector
        def _(dve):
            sc = S.MOD[:, (3 * which + 1) * KB:(3 * which + 2) * KB, :]
            g = S.param("norm1_g" if which == 0 else "norm2_g")
            for c in range(2):
                ins = nc.vector.scalar_tensor_tensor(out=S.GS[:, which, :, c], in0=sc[:, :, c], scalar=1.0, in1=g,
                                                     op0=ALU.add, op1=ALU.mult)
            ins.then_inc(gained.sem, 1)
            for k in range(KB):
                nc.vector.tensor_tensor(S.HT[:, k, :], S.XT[:, k, :], S.RS[:, :], ALU.mult).then_inc(scaled.sem, 1)
            for k in range(KB):
                dve.wait_ge(split.sem, split.at(0, k + 1))
                nc.vector.tensor_tensor(low_r[:, k, :], low[:, k, :], plain(S.HTr[:, k, :]), ALU.subtract).then_inc(
                    left.sem, 1)

        @block.scalar
        def _(act):
            act.wait_ge(gained.sem, gained.at())
            if which == 0:
                act.wait_ge(S.saved.sem, S.saved.at())
            for k in range(KB):
                act.wait_ge(scaled.sem, scaled.at(0, k + 1))
                for c, (a, b) in enumerate(((0, N_CTX), (N_CTX, T))):
                    ins = nc.scalar.activation(low[:, k, a:b], S.HT[:, k, a:b], ACT.Identity,
                                               bias=S.MOD[:, 3 * which * KB + k, c:c + 1], scale=S.GS[:, which, k, c:c + 1])
                ins.then_inc(shifted.sem, 1)
                if k:
                    act.wait_ge(shifted.sem, shifted.at(0, k))
                    nc.scalar.copy(S.HTr[:, k - 1, :], low[:, k - 1, :]).then_inc(split.sem, 1)
            act.wait_ge(shifted.sem, shifted.at())
            nc.scalar.copy(S.HTr[:, KB - 1, :], low[:, KB - 1, :]).then_inc(split.sem, 1)


def enter(S):
    nc, io = S.nc, S.io
    x_in = [S.YT[:, i, 0:D] for i in range(2)]
    WM = [S.Z[:, 4 * i:4 * i + 4, :].rearrange("p a b -> p (a b)")[:, 0:KB * 512].rearrange("p (k n) -> p k n", k=KB)
          for i in range(3)]
    SC = S.HT[:, 0, 0:16].rearrange("p (k c) -> p k c", c=2)
    SE = S.HT[:, 1, 0:16].rearrange("p (k c) -> p k c", c=2)
    x_loaded = [S.flag(f"x_loaded{i}") for i in range(2)]
    x_turned, x_stored = S.flag("x_turned", 2), S.flag("x_stored", 2)
    S.saved = S.flag("residual_saved", 16)
    mod_loaded = [S.flag(f"w_mod_loaded{i}") for i in range(3)]
    mod_used, mod_turned = S.flag("w_mod_used", 3), S.flag("mod_turned")
    mod_rows = S.flag("mod_rows", 3, in_hand=3)
    MR = S.HT[0:2, 2:8, :].rearrange("p a b -> p (a b)")
    expd, cond = S.flag("cond_exp"), S.flag("cond_ready", 4)
    w_mod = io["w_mod"][0].rearrange("(k p) n -> p k n", p=P)
    n_mod = N_MOD * D // 512 // 3
    sums = SquareSums(S, "n1")

    with nc.Block() as block:
        @block.sync
        def _(sp):
            sp.dma_start(x_in[0], io["x_prompt"][0]).then_inc(x_loaded[0].sem, 16)
            for i in range(3):
                sp.dma_start(WM[i], w_mod[:, :, i * 512:(i + 1) * 512]).then_inc(mod_loaded[i].sem, 16)
            for t in range(1, NT):
                if t >= 2:
                    sp.wait_ge(x_turned.sem, x_turned.at(0, t - 1))
                sp.dma_start(x_in[t % 2], io["x_sample"][0, (t - 1) * P:t * P, :]).then_inc(x_loaded[t % 2].sem, 16)
            with sp.Fori(1, n_mod) as j:
                for i in range(3):
                    sp.wait_ge(mod_used.sem, mod_used.at(j - 1, i + 1))
                    sp.dma_start(WM[i], w_mod[:, :, ds(j * 1536 + i * 512, 512)]).then_inc(mod_loaded[i].sem, 16)
            sp.wait_ge(x_stored.sem, x_stored.at(0, NT))
            sp.dma_start(S.x_dram, S.XT[:, :, :]).then_inc(S.saved.sem, 16)

        @block.tensor
        def _(pe):
            for t in range(NT):
                pe.wait_ge(x_loaded[t % 2].sem, x_loaded[t % 2].at(0, 16 * (t // 2 + 1)))
                if t >= 2:
                    pe.wait_ge(x_stored.sem, x_stored.at(0, t - 1))
                for k in range(KB):
                    tr = nc.tensor.transpose(S.PS[2 * (t % 2) + k // 4][:, (k % 4) * P:(k % 4 + 1) * P],
                                             x_in[t % 2][:, k * P:(k + 1) * P], S.ident[:, :])
                tr.then_inc(x_turned.sem, 1)
            pe.wait_ge(cond.sem, cond.at())
            with pe.Fori(0, n_mod) as j:
                for i in range(3):
                    pe.wait_ge(mod_loaded[i].sem, mod_loaded[i].at(16 * j, 16))
                    pe.wait_ge(mod_rows.sem, mod_rows.last(j, i + 1))
                    for k in range(KB):
                        mm = nc.tensor.matmul(S.PS[4 + i][0:2, :], SC[:, k, :], WM[i][:, k, :],
                                              start=(k == 0), stop=(k == KB - 1))
                    mm.then_inc(mod_used.sem, 1)
            pe.wait_ge(mod_rows.sem, mod_rows.at(n_mod - 1))
            for b in range(N_MOD * KB):
                tr = nc.tensor.transpose(S.PS[7][:, 2 * b:2 * b + 2], MR[:, b * P:(b + 1) * P], S.ident[0:2, 0:2])
            tr.then_inc(mod_turned.sem, 1)
            sums.sum(pe)

        @block.scalar
        def _(act):
            for c, name in enumerate(("c_ctx", "c")):
                ins = nc.scalar.activation(SE[:, :, c], S.param(name), ACT.Exp, scale=-1.0)
            ins.then_inc(expd.sem, 1)
            for t in range(NT):
                act.wait_ge(x_turned.sem, x_turned.at(0, t + 1))
                for i in range(2):
                    ins = nc.scalar.copy(S.XT[:, 4 * i:4 * i + 4, t * P:(t + 1) * P],
                                         S.PS[2 * (t % 2) + i][:, :].rearrange("p (k n) -> p k n", k=4))
                ins.then_inc(x_stored.sem, 1)
            act.wait_ge(x_stored.sem, x_stored.at(0, NT))
            sums.square(act)
            with act.Fori(0, n_mod) as j:
                for i in range(3):
                    act.wait_ge(mod_used.sem, mod_used.at(j, i + 1))
                    S.apart(act)
                    nc.scalar.copy(MR[:, ds(j * 1536 + i * 512, 512)], S.PS[4 + i][0:2, :]).then_inc(mod_rows.sem, 1)
            sums.invert(act)

        @block.gpsimd
        def _(pool):
            pool.sem_inc(mod_rows.sem, mod_rows.in_hand)

        @block.vector
        def _(dve):
            dve.wait_ge(expd.sem, expd.at())
            nc.vector.tensor_scalar(SE, SE, 1.0, None, ALU.add).then_inc(cond.sem, 1)
            dve.wait_ge(cond.sem, cond.at(0, 1))
            nc.vector.reciprocal(SE, SE).then_inc(cond.sem, 1)
            dve.wait_ge(cond.sem, cond.at(0, 2))
            for c, name in enumerate(("c_ctx", "c")):
                nc.vector.tensor_tensor(SC[:, :, c], SE[:, :, c], S.param(name), ALU.mult).then_inc(cond.sem, 1)
            sums.add(dve)
            dve.wait_ge(mod_turned.sem, mod_turned.at())
            for c in range(2):
                nc.vector.tensor_tensor(S.MOD[:, :, c], S.PS[7][:, 0:96].rearrange("p (b c) -> p b c", c=2)[:, :, c],
                                        S.param("b_mod"), ALU.add)


class Dense:

    def __init__(self, S, tag, low, high=None, blocks=KB):
        self.S, self.blocks = S, blocks
        self.high_r = high or [w[:, :, :] for w in S.Wr]
        self.low, self.low_r = low
        self.loaded = [S.flag(f"{tag}_weights_loaded{i}", 16) for i in range(2)]
        self.rounded = S.flag(f"{tag}_weights_rounded", 2)
        self.split = S.flag(f"{tag}_weights_split", 2)
        self.summed = S.flag(f"{tag}_summed", 2 * NG, in_hand=2 * NG)
        self.drained = [S.flag(f"{tag}_drained{g}", 2, in_hand=2) for g in range(NG)]

    def start(self, eng):
        eng.sem_inc(self.summed.sem, self.summed.in_hand)
        for d in self.drained:
            eng.sem_inc(d.sem, d.in_hand)

    def load(self, sp, i, slot, src):
        sp.wait_ge(self.summed.sem, self.summed.last(i, NG * (slot + 1)))
        sp.dma_start(self.low[slot], src).then_inc(self.loaded[slot].sem, 16)

    def divide(self, pool, i, slot):
        nc = self.S.nc
        pool.wait_ge(self.loaded[slot].sem, self.loaded[slot].at(i))
        ones = self.S.ones[:, :].unsqueeze(1).to_broadcast([P, self.blocks, P])
        nc.gpsimd.tensor_tensor(self.high_r[slot], self.low[slot], ones,
                                ALU.mult).then_inc(self.rounded.sem, 1)
        pool.wait_ge(self.rounded.sem, self.rounded.at(i, slot + 1))
        nc.gpsimd.tensor_tensor(self.low_r[slot], self.low[slot], plain(self.high_r[slot]),
                                ALU.subtract).then_inc(self.split.sem, 1)

    def multiply(self, pe, i, slot, high, low, before=None):
        nc, S = self.S.nc, self.S
        pe.wait_ge(self.split.sem, self.split.at(i, slot + 1))
        products = ((self.high_r, high), (self.low_r, high), (self.high_r, low))
        for g in range(NG):
            pe.wait_ge(self.drained[g].sem, self.drained[g].last(i, slot + 1))
            if before:
                before(g)
            for n, (w, x) in enumerate(products):
                for k in range(self.blocks):
                    mm = nc.tensor.matmul(self.bank(slot, g), w[slot][:, k, :], x(k, g),
                                          start=(n == 0 and k == 0), stop=(n == 2 and k == self.blocks - 1))
            mm.then_inc(self.summed.sem, 1)

    def bank(self, slot, g):
        return self.S.PS[3 * slot + g][:, 0:GRP]

    def filled(self, i, slot, g):
        return self.summed.at(i, NG * slot + g + 1)


def slabs(places, views, blocks=KB, skip=0):
    return [[place(x)[:, skip:skip + blocks * P].rearrange("p (k n) -> p k n", k=blocks) for place in places]
            for x in views]


def group(buf, first=0):
    return lambda k, g: buf[:, first + k, g * GRP:(g + 1) * GRP]


def to_padded(S, dense, act, i, slot, ZP):
    nc = S.nc
    for g in range(NG):
        act.wait_ge(dense.summed.sem, dense.filled(i, slot, g))
        a = LAT0 + g * GRP - N_CTX
        if g == 0:
            nc.scalar.copy(ZP[:, CTX0:CTX0 + N_CTX], S.PS[3 * slot][:, 0:N_CTX])
            ins = nc.scalar.copy(ZP[:, LAT0:LAT0 + GRP - N_CTX], S.PS[3 * slot][:, N_CTX:GRP])
        else:
            ins = nc.scalar.copy(ZP[:, a:a + GRP], dense.bank(slot, g))
        ins.then_inc(dense.drained[g].sem, 1)


SEQS = ((0, N_CTX, CTX0), (N_CTX, N_LAT, LAT0))


class HeadNorm:

    def __init__(self, S, tag, heads, dev, q=1):
        self.S, self.heads, self.q, self.dev = S, heads, q, dev
        self.summed = S.flag(f"{tag}_mean", q)
        self.centred = S.flag(f"{tag}_centred", q)
        self.squared = S.flag(f"{tag}_squared_dev", q)
        self.varied = S.flag(f"{tag}_variance", q)
        self.logged = S.flag(f"{tag}_log", q)
        self.rooted = S.flag(f"{tag}_rstd", q)
        self.normed = S.flag(f"{tag}_normed", q)
        self.stat = S.sb(f"{tag}_stat", P, 3, heads)

    def spread(self, dve, j, x, sq):
        nc, S, st, dev, h = self.S.nc, self.S, self.stat, self.dev, self.heads
        nc.vector.tensor_reduce(st[:, 0, :], x, AX.X, ALU.add).then_inc(self.summed.sem, 1)
        dve.wait_ge(self.summed.sem, self.summed.at(j))
        if later(j):
            dve.wait_ge(self.normed.sem, self.normed.last(j))
        S.apart(dve)
        nc.vector.scalar_tensor_tensor(
            out=dev, in0=st[:, 0, :].unsqueeze(2).to_broadcast([P, h, N]), scalar=-1.0 / N, in1=x,
            op0=ALU.mult, op1=ALU.add).then_inc(self.centred.sem, 1)
        dve.wait_ge(self.centred.sem, self.centred.at(j))
        nc.vector.tensor_tensor(sq, dev, dev, ALU.mult).then_inc(self.squared.sem, 1)
        dve.wait_ge(self.squared.sem, self.squared.at(j))
        nc.vector.tensor_reduce(st[:, 1, :], sq, AX.X, ALU.add).then_inc(self.varied.sem, 1)

    def divide(self, dve, j, out):
        nc, st, dev, h = self.S.nc, self.stat, self.dev, self.heads
        dve.wait_ge(self.rooted.sem, self.rooted.at(j))
        nc.vector.tensor_tensor(out, dev, st[:, 2, :].unsqueeze(2).to_broadcast([P, h, N]),
                                ALU.mult).then_inc(self.normed.sem, 1)

    def scalar(self, act, j):
        nc, S, st = self.S.nc, self.S, self.stat
        act.wait_ge(self.varied.sem, self.varied.at(j))
        nc.scalar.activation(st[:, 2, :], st[:, 1, :], ACT.Ln, bias=S.eps[:, 1:2], scale=1.0 / N).then_inc(
            self.logged.sem, 1)
        act.wait_ge(self.logged.sem, self.logged.at(j))
        nc.scalar.activation(st[:, 2, :], st[:, 2, :], ACT.Exp, scale=-0.5).then_inc(self.rooted.sem, 1)


def tiles_ahead(eng, step):
    step(eng, 0, 1)
    with eng.Fori(1, NT - 1) as t:
        step(eng, t, eng.snap(t + 1, min_val=1, max_val=NT - 1))
    step(eng, NT - 1, None)


def tokens_of(eng, t):
    return t * P if isinstance(t, int) else eng.snap(t * P, min_val=0, max_val=T - P)


def project_a(S):
    nc, io = S.nc, S.io
    w_in = io["w_in"][0].rearrange("(k p) n -> p k n", p=P)
    dense = Dense(S, "a", slabs([lambda x: x[:, 5, :], lambda x: x[:, 6, :]], (S.YT, S.YTr)))
    with nc.Block() as block:
        @block.gpsimd
        def _(pool):
            dense.start(pool)
            with pool.Fori(0, 2) as i:
                for slot in range(2):
                    dense.divide(pool, i, slot)

        @block.sync
        def _(sp):
            for slot in range(2):
                dense.load(sp, 0, slot, w_in[:, :, slot * P:(slot + 1) * P])
            sp.dma_start(S.low_dram, plain(S.XTr[:, :, :])).then_inc(S.low_saved.sem, 16)
            for slot in range(2):
                dense.load(sp, 1, slot, w_in[:, :, (2 + slot) * P:(3 + slot) * P])
            sp.wait_ge(S.low_saved.sem, S.low_saved.at())

        @block.tensor
        def _(pe):
            with pe.Fori(0, 2) as i:
                for slot in range(2):
                    dense.multiply(pe, i, slot, group(S.HTr), group(S.XTr))

        @block.scalar
        def _(act):
            with act.Fori(0, 2) as i:
                for slot in range(2):
                    blk = act.snap(i * 2 + slot, min_val=0, max_val=3)
                    for g in range(NG):
                        act.wait_ge(dense.summed.sem, dense.filled(i, slot, g))
                        S.apart(act)
                        nc.scalar.activation(
                            S.Z[:, ds(blk, 1), g * GRP:(g + 1) * GRP], dense.bank(slot, g), ACT.Gelu_apprx_tanh).then_inc(
                                dense.drained[g].sem, 1)


def branch_a(S):
    nc, io = S.nc, S.io
    WS = S.Z[:, 4, 0:4 * P].rearrange("p (g s) -> p g s", g=4)
    WT = S.Z[:, 5, 0:4 * P].rearrange("p (g t) -> p g t", g=4)
    BS = S.Z[0:A_G, 6, 0:P]
    SEL = S.Z[0:A_G, 7, 0:2 * P].rearrange("g (b c) -> g b c", b=2)
    BB = S.Z[:, 8, 0:2 * P].rearrange("p (b t) -> p b t", b=2)
    VT = S.Z[:, 6, 512:512 + 2 * P].rearrange("p (b t) -> p b t", b=2)
    VN = S.Z[:, 9, 0:A_W].rearrange("p (g c) -> p g c", g=A_G)
    SQ = S.Z[:, 9, A_W:2 * A_W].rearrange("p (g c) -> p g c", g=A_G)
    SV = S.Z[:, 10, 0:2 * P].rearrange("p (b t) -> p b t", b=2)
    loaded, sel, made = S.flag("ws_loaded", 16 * 5), S.flag("a_selector", 2), S.flag("a_constants")
    turned, copied = S.flag("ws_turned"), S.flag("ws_copied", 2)
    staged, v_turned = S.flag("v_staged"), S.flag("v_turned")
    norm = HeadNorm(S, "an", A_G, S.Z[:, 11, 0:A_W].rearrange("p (g c) -> p g c", g=A_G))
    mixed, biased, stored = S.flag("v_mixed"), S.flag("v_biased", 2), S.flag("a_stored")

    def turn_pe(pe, t):
        pe.wait_ge(staged.sem, staged.at(t))
        if later(t):
            pe.wait_ge(norm.centred.sem, norm.centred.last(t))
        for b in range(2):
            tr = nc.tensor.transpose(S.PS[1][:, b * P:(b + 1) * P], VT[:, b, :], S.ident[:, :])
        tr.then_inc(v_turned.sem, 1)

    def step_pe(pe, t, after):
        if after is not None:
            turn_pe(pe, after)
        pe.wait_ge(norm.normed.sem, norm.normed.at(t))
        if later(t):
            pe.wait_ge(biased.sem, biased.last(t))
        for b in range(2):
            mm = nc.tensor.matmul(S.PS[2][:, b * 256:(b + 1) * 256], VN[:, 2 * b:2 * b + 2, :],
                                  WT[:, 2 * b:2 * b + 2, :], start=True, stop=True)
        mm.then_inc(mixed.sem, 1)

    def stage_act(act, t):
        if later(t):
            act.wait_ge(v_turned.sem, v_turned.last(t))
        S.apart(act)
        nc.scalar.copy(VT[:, :, :], S.Z[:, 2:4, ds(tokens_of(act, t), P)]).then_inc(staged.sem, 1)

    def step_act(act, t, after):
        if after is not None:
            stage_act(act, after)
        norm.scalar(act, t)

    def spread_dve(dve, t):
        dve.wait_ge(v_turned.sem, v_turned.at(t))
        norm.spread(dve, t, S.PS[1][:, 0:A_W].rearrange("p (g c) -> p g c", g=A_G), SQ)

    def step_dve(dve, t, after):
        tok = tokens_of(dve, t)
        norm.divide(dve, t, VN)
        if after is not None:
            spread_dve(dve, after)
        dve.wait_ge(mixed.sem, mixed.at(t))
        if later(t):
            dve.wait_ge(stored.sem, stored.last(t))
        for b in range(2):
            for half in range(2):
                rows = slice(N * half, N * half + N)
                ins = nc.vector.scalar_tensor_tensor(
                    out=SV[rows, b, :], in0=S.PS[2][rows, b * 256 + half * P:b * 256 + half * P + P],
                    scalar=S.param("gmlp_ln_g", b, 1)[rows, :], in1=BB[rows, b, :], op0=ALU.mult, op1=ALU.add)
            ins.then_inc(biased.sem, 1)
        dve.wait_ge(biased.sem, biased.at(t))
        nc.vector.tensor_tensor(S.YT[:, 0:2, ds(tok, P)], SV[:, :, :], S.Z[:, 0:2, ds(tok, P)], ALU.mult).then_inc(
            stored.sem, 1)

    with nc.Block() as block:
        @block.sync
        def _(sp):
            for g in range(A_G):
                sp.dma_start(WS[:, g, :], io["gmlp_w_s"][0, g]).then_inc(loaded.sem, 16)
            sp.dma_start(BS, io["gmlp_b_s"][0]).then_inc(loaded.sem, 16)

        @block.gpsimd
        def _(pool):
            nc.gpsimd.memset(SEL, 0.0).then_inc(sel.sem, 1)
            pool.wait_ge(sel.sem, sel.at(0, 1))
            nc.gpsimd.affine_select(out=SEL.rearrange("g b (h c) -> g b h c", h=2),
                                            in_=SEL.rearrange("g b (h c) -> g b h c", h=2),
                                            compare_op=ALU.not_equal, fill=1.0, base=0,
                                            pattern=[[-2, 2], [-1, 2], [0, N]], channel_multiplier=1).then_inc(sel.sem, 1)

        @block.tensor
        def _(pe):
            pe.wait_ge(loaded.sem, loaded.at())
            pe.wait_ge(sel.sem, sel.at())
            for g in range(A_G):
                nc.tensor.transpose(S.PS[0][:, g * P:(g + 1) * P], WS[:, g, :], S.ident[:, :])
            for b in range(2):
                mm = nc.tensor.matmul(S.PS[3][:, b * P:(b + 1) * P], SEL[:, b, :], BS, start=True, stop=True)
            mm.then_inc(turned.sem, 1)
            pe.wait_ge(copied.sem, copied.at())
            turn_pe(pe, 0)
            tiles_ahead(pe, step_pe)

        @block.scalar
        def _(act):
            act.preload_act_table_set(EXP_LN)
            stage_act(act, 0)
            tiles_ahead(act, step_act)

        @block.vector
        def _(dve):
            dve.wait_ge(turned.sem, turned.at())
            nc.vector.tensor_copy(WT, S.PS[0][:, :].rearrange("p (g t) -> p g t", g=4)).then_inc(copied.sem, 1)
            nc.vector.tensor_copy(BB, S.PS[3][:, 0:2 * P].rearrange("p (b t) -> p b t", b=2)).then_inc(copied.sem, 1)
            dve.wait_ge(copied.sem, copied.at())
            spread_dve(dve, 0)
            tiles_ahead(dve, step_dve)


def project_b(S):
    nc, io = S.nc, S.io
    w_in = io["w_in"][0].rearrange("(k p) n -> p k n", p=P)
    dense = Dense(S, "b", slabs([lambda x: x[:, 6, :], lambda x: x[:, 7, :]], (S.YT, S.YTr)))
    ZP, CV = S.PAD[0:2], S.PAD[2:4]
    cleared = S.flag("b_pads_cleared", 2)
    centre, left, right = S.flag("conv_centre", 2), S.flag("conv_left", 2), S.flag("conv_right", 2, in_hand=2)
    silued = S.flag("qk_silued", 2, in_hand=2)
    WG = S.YT[:, 3, 0:D].rearrange("p (k n) -> p k n", k=KB)
    WH_r, WG_r = (S.YTr[:, r, 0:D].rearrange("p (k n) -> p k n", k=KB) for r in (4, 3))
    S.gate_high, S.gate_low = WH_r, WG_r
    gate_cleared, gate_loaded = S.flag("gate_weights_cleared"), S.flag("gate_weights_loaded", 16 * 4)
    gate_high = S.flag("gate_weights_rounded")
    at = PROWS["mlstm_conv"][0]
    with nc.Block() as block:
        @block.gpsimd
        def _(pool):
            dense.start(pool)
            nc.gpsimd.memset(WG, 0.0).then_inc(gate_cleared.sem, 1)
            pool.sem_inc(right.sem, right.in_hand)
            pool.sem_inc(silued.sem, silued.in_hand)
            for z in ZP:
                nc.gpsimd.memset(z[:, :], 0.0).then_inc(cleared.sem, 1)
            with pool.Fori(0, 6) as i:
                for slot in range(2):
                    dense.divide(pool, i, slot)
            pool.wait_ge(gate_loaded.sem, gate_loaded.at())
            nc.gpsimd.tensor_copy(WH_r, WG).then_inc(gate_high.sem, 1)
            pool.wait_ge(gate_high.sem, gate_high.at())
            nc.gpsimd.tensor_tensor(WG_r, WG, plain(WH_r), ALU.subtract)

        @block.sync
        def _(sp):
            with sp.Fori(0, 6) as i:
                for slot in range(2):
                    dense.load(sp, i, slot, w_in[:, :, ds(i * 256 + OFF_QK + slot * P, P)])
            sp.wait_ge(gate_cleared.sem, gate_cleared.at())
            for d in range(2):
                for f in range(2):
                    o, c = OFF_G + 2 * H * d + H * f, 2 * DIR_ROW * f + DIR_ROW * d
                    sp.dma_start(WG[:, :, c:c + H], w_in[:, :, o:o + H]).then_inc(gate_loaded.sem, 16)

        @block.tensor
        def _(pe):
            with pe.Fori(0, 6) as i:
                for slot in range(2):
                    dense.multiply(pe, i, slot, group(S.HTr), group(S.XTr))

        @block.scalar
        def _(act):
            act.wait_ge(cleared.sem, cleared.at())
            with act.Fori(0, 3) as i:
                for slot in range(2):
                    blk = act.snap(i * 2 + slot, min_val=0, max_val=5)
                    act.wait_ge(right.sem, right.last(i, slot + 1))
                    to_padded(S, dense, act, i, slot, ZP[slot])
                    act.wait_ge(right.sem, right.at(i, slot + 1))
                    S.apart(act)
                    for a, n, p in SEQS:
                        ins = nc.scalar.activation(S.Z[:, ds(blk, 1), a:a + n], CV[slot][:, p:p + n], ACT.Silu)
                    ins.then_inc(silued.sem, 1)
            with act.Fori(3, 6) as i:
                for slot in range(2):
                    blk = act.snap(i * 2 + slot, min_val=6, max_val=11)
                    for g in range(NG):
                        act.wait_ge(dense.summed.sem, dense.filled(i, slot, g))
                        S.apart(act)
                        nc.scalar.copy(S.Z[:, ds(blk, 1), g * GRP:(g + 1) * GRP], dense.bank(slot, g)).then_inc(
                            dense.drained[g].sem, 1)
            act.wait_ge(dense.drained[NG - 1].sem, dense.drained[NG - 1].at(5))
            nc.scalar.activation(S.Z[:, 9:12, :], S.Z[:, 9:12, :], ACT.Sigmoid)

        @block.vector
        def _(dve):
            with dve.Fori(0, 3) as i:
                for slot in range(2):
                    tap = [dve.snap(i * 2 + (at + 6 * c + slot), min_val=0, max_val=N_PROWS - 1) for c in range(3)]
                    tap = [S.PT[:, ds(c, 1)] for c in tap]
                    z, cv = ZP[slot], CV[slot]
                    dve.wait_ge(dense.drained[NG - 1].sem, dense.drained[NG - 1].at(i, slot + 1))
                    dve.wait_ge(silued.sem, silued.last(i, slot + 1))
                    nc.vector.tensor_scalar(cv[:, 1:LAT0 + N_LAT], z[:, 1:LAT0 + N_LAT], tap[1], None, ALU.mult).then_inc(
                        centre.sem, 1)
                    dve.wait_ge(centre.sem, centre.at(i, slot + 1))
                    nc.vector.scalar_tensor_tensor(
                        out=cv[:, 1:LAT0 + N_LAT], in0=z[:, 0:LAT0 + N_LAT - 1], scalar=tap[0],
                        in1=cv[:, 1:LAT0 + N_LAT], op0=ALU.mult, op1=ALU.add).then_inc(left.sem, 1)
                    dve.wait_ge(left.sem, left.at(i, slot + 1))
                    nc.vector.scalar_tensor_tensor(
                        out=cv[:, 1:LAT0 + N_LAT], in0=z[:, 2:LAT0 + N_LAT + 1], scalar=tap[2],
                        in1=cv[:, 1:LAT0 + N_LAT], op0=ALU.mult, op1=ALU.add).then_inc(right.sem, 1)


DIR_ROW = 32
ROWS = DIR_ROW + H


def last_in_time(x, d):
    return x[:, P - 1::P] if d == 0 else x[:, 0::P]


def gates_b(S, B):
    nc, io = S.nc, S.io
    I, F = B.I, B.F
    loaded, cleared = S.flag("gate_loads", 16 * 6), S.flag("gate_cleared", 9)
    summed, biased = S.flag("gates_summed", NG), S.flag("gates_biased", 2 * NG)
    folded, soft = S.flag("gates_folded"), S.flag("gates_soft", 2)
    rows, turned, spread = S.flag("gate_rows", 40), S.flag("gates_turned"), S.flag("gates_spread")
    prepared, out_m = S.flag("gates_prepared", 40), S.flag("m_out", 32)
    n_rows = [0]

    with nc.Block() as block:
        @block.gpsimd
        def _(pool):
            for x in (B.VAL[:, :, :], B.gate_bias[:, :], B.m0[:, :]):
                nc.gpsimd.memset(x, 0.0).then_inc(cleared.sem, 1)
            nc.gpsimd.memset(B.reset[:, :], 1.0).then_inc(cleared.sem, 1)
            nc.gpsimd.memset(B.SEL[:, :, :], 0.0).then_inc(cleared.sem, 1)
            pool.wait_ge(cleared.sem, cleared.at(0, 5))
            nc.gpsimd.memset(B.reset[0:DIR_ROW, 0::P], 0.0).then_inc(cleared.sem, 1)
            pool.wait_ge(cleared.sem, cleared.at(0, 6))
            nc.gpsimd.memset(B.reset[DIR_ROW:2 * DIR_ROW, P - 1::P], 0.0).then_inc(cleared.sem, 1)
            pool.wait_ge(cleared.sem, cleared.at(0, 7))
            for d in range(2):
                v = B.SEL[:, d * H:(d + 1) * H, :]
                ins = nc.gpsimd.affine_select(out=v, in_=v, compare_op=ALU.not_equal, fill=1.0, base=-DIR_ROW * d,
                                              pattern=[[-1, H], [0, P]], channel_multiplier=1)
            pool.wait_ge(summed.sem, summed.at())
            nc.gpsimd.memset(B.M[:, :], 0.0).then_inc(cleared.sem, 1)
            nc.gpsimd.memset(B.C[:, :], 0.0).then_inc(cleared.sem, 1)

        @block.sync
        def _(sp):
            sp.wait_ge(cleared.sem, cleared.at(0, 3))
            for d in range(2):
                for f in range(2):
                    sp.dma_start(B.gate_bias[DIR_ROW * d:DIR_ROW * d + H, f:f + 1],
                                 io["mlstm_gate_b"][0, d, f].unsqueeze(1)).then_inc(loaded.sem, 16)
                sp.dma_start(B.m0[DIR_ROW * d:DIR_ROW * d + H, :],
                             io["state_mlstm_m"][0, 0, d].unsqueeze(1)).then_inc(loaded.sem, 16)
            sp.wait_ge(rows.sem, rows.at(0, B.scans_done))
            for d in range(2):
                c = P - 1 if d == 0 else 0
                sp.dma_start(S.out[4][0, 0, d].unsqueeze(1), B.M[DIR_ROW * d:DIR_ROW * d + H, c:c + 1]).then_inc(
                    out_m.sem, 16)
            sp.wait_ge(out_m.sem, out_m.at())

        @block.tensor
        def _(pe):
            for g in range(NG):
                for n, (w, x) in enumerate(((S.gate_high, S.HTr), (S.gate_low, S.HTr), (S.gate_high, S.XTr))):
                    for k in range(KB):
                        mm = nc.tensor.matmul(S.PS[g][:, 0:GRP], w[:, k, :], x[:, k, g * GRP:(g + 1) * GRP],
                                              start=(n == 0 and k == 0), stop=(n == 2 and k == KB - 1))
                mm.then_inc(summed.sem, 1)
            pe.wait_ge(rows.sem, rows.at(0, B.rows_done))
            for q, x in enumerate((B.I, B.X2, B.M)):
                for t in range(NT):
                    c = t * ROWS
                    tr = nc.tensor.transpose(S.PS[3 + q][:, c:c + ROWS], x[0:ROWS, t * P:(t + 1) * P],
                                             S.ident[0:ROWS, 0:ROWS])
            tr.then_inc(turned.sem, 1)
            for d in range(2):
                r = slice(DIR_ROW * d, DIR_ROW * d + H)
                mm = nc.tensor.matmul(S.PS[6 + d][:, 0:3 * NT * H], S.ones[r, :],
                                      B.diag[r, :, :, :], start=True, stop=True)
            mm.then_inc(spread.sem, 1)

        @block.scalar
        def _(act):
            act.preload_act_table_set(EXP_LN)
            act.wait_ge(loaded.sem, loaded.at())
            act.wait_ge(summed.sem, summed.at())
            for g in range(NG):
                for f, x in enumerate((I, F)):
                    nc.scalar.activation(x[0:2 * DIR_ROW, g * GRP:(g + 1) * GRP],
                                                    S.PS[g][2 * DIR_ROW * f:2 * DIR_ROW * (f + 1), 0:GRP],
                                                    ACT.Identity, bias=B.gate_bias[:, f:f + 1]).then_inc(biased.sem, 1)
            act.wait_ge(folded.sem, folded.at())
            nc.scalar.activation(B.X2[:, :], B.X2[:, :], ACT.Exp).then_inc(soft.sem, 1)
            act.wait_ge(soft.sem, soft.at(0, 1))
            nc.scalar.activation(B.X2[:, :], B.X2[:, :], ACT.Ln, bias=S.eps[0:2 * DIR_ROW, 2:3]).then_inc(soft.sem, 1)
            act.wait_ge(prepared.sem, prepared.at(0, B.logs_done))
            nc.scalar.activation(B.tok[:, :, :, 0:3, :], B.tok[:, :, :, 0:3, :], ACT.Exp)
            for half in range(2):
                r = slice(N * half, N * half + N)
                for d in range(2):
                    nc.scalar.activation(B.decay[r, d, :, :], B.spread[r, d, 2, :, half::2], ACT.Exp)

        @block.vector
        def _(dve):
            def row_op(ins):
                ins.then_inc(rows.sem, 1)
                n_rows[0] += 1
                dve.wait_ge(rows.sem, rows.at(0, n_rows[0]))

            dve.wait_ge(biased.sem, biased.at())
            dve.wait_ge(cleared.sem, cleared.at())
            nc.vector.scalar_tensor_tensor(out=B.X2[:, :], in0=F[:, :], scalar=-1.0, in1=F[:, :],
                                                      op0=ALU.mult, op1=ALU.min).then_inc(folded.sem, 1)
            dve.wait_ge(soft.sem, soft.at())
            row_op(nc.vector.scalar_tensor_tensor(out=F[:, :], in0=F[:, :], scalar=0.0, in1=B.X2[:, :],
                                                  op0=ALU.min, op1=ALU.subtract))
            for d in range(2):
                r = slice(DIR_ROW * d, DIR_ROW * d + H)

                def time(x, a, b, d=d, r=r):
                    return x[r, a:b] if d == 0 else x[r, a:b][:, ::-1]
                row_op(nc.vector.tensor_tensor_scan(time(B.C, 0, T), time(B.reset, 0, T), time(F, 0, T), 0.0,
                                                    ALU.mult, ALU.add))
                for a, b, first in ((0, N_CTX, 0.0), (N_CTX, T, B.m0[r, :])):
                    row_op(nc.vector.tensor_tensor_scan(time(B.M, a, b), time(F, a, b), time(I, a, b), first,
                                                        ALU.add, ALU.max))
            B_scans = n_rows[0]
            assert B_scans == B.scans_done
            row_op(nc.vector.tensor_tensor(I[:, :], I[:, :], B.C[:, :], ALU.subtract))
            row_op(nc.vector.tensor_tensor(B.X2[:, :], B.C[:, :], B.M[:, :], ALU.subtract))
            for d in range(2):
                r = slice(DIR_ROW * d, DIR_ROW * d + H)
                V, M, C = B.VAL[r, :, :], B.M[r, :], B.C[r, :]
                if d == 0:
                    nc.vector.tensor_copy(V[:, 0, 1:2], B.m0[r, :])
                    nc.vector.tensor_copy(V[:, 0, 2:NT], M[:, 2 * P - 1:T - P:P])
                else:
                    nc.vector.tensor_copy(V[:, 0, NT - 1:NT], B.m0[r, :])
                    nc.vector.tensor_copy(V[:, 0, 1:NT - 1], M[:, 2 * P::P])
                row_op(nc.vector.tensor_tensor(V[:, 1, :], last_in_time(C, d), last_in_time(M, d), ALU.subtract))
                row_op(nc.vector.tensor_tensor(V[:, 2, :], V[:, 1, :], V[:, 0, :], ALU.add))
                for h in range(H):
                    row_op(nc.vector.tensor_scalar(B.diag[r, :, :, h], V, S.ident[r, DIR_ROW * d + h:DIR_ROW * d + h + 1],
                                                   None, ALU.mult))
            assert n_rows[0] == B.rows_done
            dve.wait_ge(turned.sem, turned.at())
            dve.wait_ge(spread.sem, spread.at())
            n = 0

            def prepare(ins):
                nonlocal n
                ins.then_inc(prepared.sem, 1)
                n += 1

            def per_token(q, d):
                return S.PS[3 + q][:, 0:NT * ROWS].rearrange("p (t r) -> p t r", r=ROWS)[:, :, DIR_ROW * d:DIR_ROW * d + H]
            for d in range(2):
                prepare(nc.vector.tensor_copy(B.spread[:, d, :, :, :],
                                              S.PS[6 + d][:, 0:3 * NT * H].rearrange("p (q t h) -> p q t h", q=3, t=NT)))
            dve.wait_ge(prepared.sem, prepared.at(0, n))
            for d in range(2):
                tok = B.tok[:, d, :, :, :]
                prepare(nc.vector.tensor_tensor(tok[:, :, 0, :], per_token(1, d), B.spread[:, d, 0, :, :], ALU.add))
                prepare(nc.vector.tensor_tensor(tok[:, :, 1, :], per_token(0, d), B.spread[:, d, 1, :, :], ALU.add))
                prepare(nc.vector.tensor_scalar(tok[:, :, 2, :], per_token(2, d), -1.0, None, ALU.mult))
                prepare(nc.vector.tensor_copy(tok[:, :, 3, :], per_token(0, d)))
            assert n == B.logs_done


class StoreB:
    scans_done = 1 + 2 * 3
    rows_done = scans_done + 2 + 2 * (2 + H)
    logs_done = 2 + 2 * 4

    def __init__(self, S):
        area = Area(S.XT[:, :, :].rearrange("p k t -> p (k t)"))
        self.Hs = area.cut(NT, B_W)
        R = 2 * DIR_ROW
        self.I, self.F = area.cut(T, rows=R), area.cut(T, rows=R)
        self.C, self.M = area.cut(T, rows=R), area.cut(T, rows=R)
        self.X2 = S.RS[0:R, :]
        self.reset = S.PAD[0][0:R, 0:T]
        self.tok = area.cut(2, NT, 4, H)
        pads = Area(S.PAD[1][:, :])
        self.spread = pads.cut(2, 3, NT, H)
        self.VAL = pads.cut(3, NT, rows=R)
        self.diag = pads.cut(3, NT, H, rows=R)
        self.gate_bias = S.sb("gate_bias", R, 2)
        self.m0 = S.sb("m0", R, 1)
        self.decay = area.cut(2, NT, NP)
        self.SEL = Area(S.YT[:, 5:8, :].rearrange("p k t -> p (k t)")).cut(2 * H, P, rows=R)

def slot_of(h):
    return NP * (h % 2) + h // 2


def direction_tiles(eng, t):
    if isinstance(t, int):
        f, b = t, (NT - t) % NT
        return [f * P, b * P], [f, b]
    f = eng.snap(t * P, min_val=0, max_val=T - P)
    b = eng.snap(t * (-P) + T, min_val=0, max_val=T - P)
    return [f, b], [t, eng.snap(t * (-1) + NT, min_val=0, max_val=NT - 1)]


def following(eng, t, d):
    if d == 0:
        return t, 1
    return (t + 1 if isinstance(t, int) else eng.snap(t + 1, min_val=1, max_val=NT)), 0


def over_rounds(eng, step, between=None):
    for d in range(2):
        step(eng, 0, d)
    if between:
        between(eng)
    with eng.Fori(1, NT - 1) as t:
        for d in range(2):
            step(eng, t, d)
    step(eng, NT - 1, 0)
    step(eng, NT - 1, 1, more=False)


def recur_b(S, B):
    nc, io = S.nc, S.io
    pads = Area(S.PAD[2][:, :])
    QS, KS = pads.cut(NP, P), pads.cut(NP, P)
    VS = pads.cut(NP, P)
    pads = Area(S.PAD[3][:, :])
    KW, V1 = pads.cut(H, N), pads.cut(H, N + 1)
    DEN = pads.cut(2, H)
    yt = Area(S.YT[:, 2:5, :].rearrange("p k t -> p (k t)"))
    X2S, CURS = yt.cut(P, rows=2 * DIR_ROW), [yt.cut(4, H) for _ in range(2)]
    E, PM = yt.cut(H, P), yt.cut(H, P)
    HN, HH = yt.cut(H, N + 1), yt.cut(H, N)
    CS = [yt.cut(NP, 2 * (N + 1)) for _ in range(2)]
    MASK = yt.cut(2 * (N + 1))
    W2 = 2 * (N + 1)

    f = {k: S.flag("mlstm_" + k, 2) for k in (
        "staged_q", "staged_k", "staged_v", "staged_rows", "turned", "weighted_k", "copied_v", "scored",
        "exponents", "exped", "weighted_scores", "numerator", "inter", "update", "decayed", "updated",
        "gated", "summed", "den_abs", "den_max", "den_inv", "quotient", "h_added")}
    ready, loads, stores = S.flag("b_ready", 4), S.flag("b_state_loads", 16 * 24), S.flag("b_state_stores", 16 * 24)
    zeroed, kept, replaced = S.flag("b_states_zeroed", 2), S.flag("b_states_kept", 2), S.flag("b_states_replaced", 2)
    cached, final = ([w.cut(NP, W2) for _ in range(2)]
                     for w in (Area(w[:, :, :].rearrange("p k n -> p (k n)")) for w in S.W))
    bK, bV, bS, bE, bN, bI = S.PS[0], S.PS[1], S.PS[2:4], S.PS[4:6], S.PS[6], S.PS[7]

    def head_rows(h):
        return slice(N * (h % 2), N * (h % 2) + N)

    def state_io(sp, flag, C, n, store):
        for d in range(2):
            for h in range(H):
                c = (N + 1) * (h % 2)
                x = final if store else cached
                for on_chip, dram in ((x[d][head_rows(h), h // 2, c:c + N], C[0, 0, d, h]),
                                      (x[d][head_rows(h), h // 2, c + N:c + N + 1], n[0, 0, d, h].unsqueeze(1))):
                    a, b = (dram, on_chip) if store else (on_chip, dram)
                    sp.dma_start(a, b).then_inc(flag.sem, 16)


    def front_pool(pool, t, d):
        tok, k = direction_tiles(pool, t)[0][d], d + 1
        if later(t, k):
            pool.wait_ge(f["inter"].sem, f["inter"].front(t, k))
        S.apart(pool)
        nc.gpsimd.tensor_copy(QS, S.Z[:, 0:3, ds(tok, P)]).then_inc(f["staged_q"].sem, 1)
        if later(t, k):
            pool.wait_ge(f["turned"].sem, f["turned"].front(t, k))
        S.apart(pool)
        nc.gpsimd.tensor_copy(VS, S.Z[:, 6:9, ds(tok, P)]).then_inc(f["staged_v"].sem, 1)

    def step_pool(pool, t, d, more=True):
        if more:
            front_pool(pool, *following(pool, t, d))

    def exponents_pe(pe, t, d):
        k = d + 1
        pe.wait_ge(f["staged_rows"].sem, f["staged_rows"].at(t, k))
        if later(t, k):
            pe.wait_ge(f["exped"].sem, f["exped"].front(t, k))
        for b in range(2):
            for i in range(3):
                h, o = 2 * i + b, bE[b][:, i * P:(i + 1) * P]
                nc.tensor.matmul(o, S.ident[:, :], S.neg[d][:, :], start=True, stop=False)
                mm = nc.tensor.matmul(o, B.SEL[:, d * H + h, :], X2S, start=False, stop=True)
        mm.then_inc(f["exponents"].sem, 1)

    def scores_pe(pe, t, d):
        k = d + 1
        pe.wait_ge(f["staged_k"].sem, f["staged_k"].at(t, k))
        pe.wait_ge(f["staged_q"].sem, f["staged_q"].at(t, k))
        if later(t, k):
            pe.wait_ge(f["weighted_scores"].sem, f["weighted_scores"].front(t, k))
        for h in range(H):
            mm = nc.tensor.matmul(bS[h % 2][:, (h // 2) * P:(h // 2 + 1) * P], KS[head_rows(h), h // 2, :],
                                  QS[head_rows(h), h // 2, :], start=True, stop=True)
        mm.then_inc(f["scored"].sem, 1)
        pe.wait_ge(f["staged_v"].sem, f["staged_v"].at(t, k))
        if later(t, k):
            pe.wait_ge(f["updated"].sem, f["updated"].front(t, k))
            pe.wait_ge(f["copied_v"].sem, f["copied_v"].front(t, k))
        for p in range(NP):
            nc.tensor.transpose(bK[:, p * P:(p + 1) * P], KS[:, p, :], S.ident[:, :])
        for p in range(NP):
            tr = nc.tensor.transpose(bV[:, p * P:(p + 1) * P], VS[:, p, :], S.ident[:, :])
        tr.then_inc(f["turned"].sem, 1)

    def step_pe(pe, t, d, more=True):
        k = d + 1
        if later(t, k):
            pe.wait_ge(f["gated"].sem, f["gated"].front(t, k))
        if later(t):
            pe.wait_ge(f["updated"].sem, f["updated"].last(t, k))
        for p in range(NP):
            mm = nc.tensor.matmul(bI[:, p * W2:(p + 1) * W2], QS[:, p, :], CS[d][:, p, :], start=True, stop=True)
        mm.then_inc(f["inter"].sem, 1)
        pe.wait_ge(f["weighted_k"].sem, f["weighted_k"].at(t, k))
        pe.wait_ge(f["copied_v"].sem, f["copied_v"].at(t, k))
        for p in range(NP):
            mm = nc.tensor.matmul(bK[:, p * W2:(p + 1) * W2], KW[:, 2 * p:2 * p + 2, :],
                                  V1[:, 2 * p:2 * p + 2, :], start=True, stop=True)
        mm.then_inc(f["update"].sem, 1)
        if more:
            exponents_pe(pe, *following(pe, t, d))
        pe.wait_ge(f["weighted_scores"].sem, f["weighted_scores"].at(t, k))
        if later(t, k):
            pe.wait_ge(f["summed"].sem, f["summed"].front(t, k))
        for h in range(H):
            mm = nc.tensor.matmul(bN[:, h * (N + 1):(h + 1) * (N + 1)], PM[:, slot_of(h), :], V1[:, h, :],
                                  start=True, stop=True)
        mm.then_inc(f["numerator"].sem, 1)
        if more:
            scores_pe(pe, *following(pe, t, d))

    def front_act(act, t, d):
        k = d + 1
        act.wait_ge(f["exponents"].sem, f["exponents"].at(t, k))
        act.wait_ge(f["staged_rows"].sem, f["staged_rows"].at(t, k))
        if later(t, k):
            act.wait_ge(f["weighted_scores"].sem, f["weighted_scores"].front(t, k))
        for h in range(H):
            ins = nc.scalar.activation(E[:, slot_of(h), :], bE[h % 2][:, (h // 2) * P:(h // 2 + 1) * P], ACT.Exp,
                                       bias=CURS[d][:, 3, h:h + 1])
        ins.then_inc(f["exped"].sem, 1)

    def step_act(act, t, d, more=True):
        k = d + 1
        act.wait_ge(f["turned"].sem, f["turned"].at(t, k))
        if later(t, k):
            act.wait_ge(f["numerator"].sem, f["numerator"].front(t, k))
        nc.scalar.copy(V1[:, :, 0:N], bV[:, 0:B_W].rearrange("p (h c) -> p h c", h=H)).then_inc(f["copied_v"].sem, 1)
        if more:
            front_act(act, *following(act, t, d))

    def front_dve(dve, t, d):
        tok, tile = direction_tiles(dve, t)
        k = d + 1
        if later(t, k):
            dve.wait_ge(f["turned"].sem, f["turned"].front(t, k))
            dve.wait_ge(f["exponents"].sem, f["exponents"].front(t, k))
        if later(t):
            dve.wait_ge(f["exped"].sem, f["exped"].last(t, k))
            dve.wait_ge(f["quotient"].sem, f["quotient"].last(t, k))
        S.apart(dve)
        nc.vector.tensor_copy(CURS[d], B.tok[:, d, ds(tile[d], 1), :, :])
        nc.vector.tensor_copy(X2S, B.X2[:, ds(tok[d], P)]).then_inc(f["staged_rows"].sem, 1)
        nc.vector.tensor_scalar(KS, S.Z[:, 3:6, ds(tok[d], P)], N ** -0.5, None, ALU.mult).then_inc(f["staged_k"].sem, 1)

    def step_dve(dve, t, d, more=True):
        k, CUR = d + 1, CURS[d]
        tile = direction_tiles(dve, t)[1][d]
        dve.wait_ge(f["turned"].sem, f["turned"].at(t, k))
        dve.wait_ge(f["staged_rows"].sem, f["staged_rows"].at(t, k))
        if later(t, k):
            dve.wait_ge(f["update"].sem, f["update"].front(t, k))
        nc.vector.tensor_tensor(
            KW, bK[:, 0:B_W].rearrange("p (h c) -> p h c", h=H),
            CUR[:, 1, :].unsqueeze(2).to_broadcast([P, H, N]), ALU.mult).then_inc(f["weighted_k"].sem, 1)
        if more:
            front_dve(dve, *following(dve, t, d))
        dve.wait_ge(f["scored"].sem, f["scored"].at(t, k))
        dve.wait_ge(f["exped"].sem, f["exped"].at(t, k))
        if later(t, k):
            dve.wait_ge(f["numerator"].sem, f["numerator"].front(t, k))
        for b in range(2):
            ins = nc.vector.tensor_tensor(PM[:, 3 * b:3 * b + 3, :], E[:, 3 * b:3 * b + 3, :],
                                          bS[b][:, 0:3 * P].rearrange("p (h t) -> p h t", h=3), ALU.mult)
        ins.then_inc(f["weighted_scores"].sem, 1)
        dve.wait_ge(f["update"].sem, f["update"].at(t, k))
        dve.wait_ge(f["inter"].sem, f["inter"].at(t, k))
        for p in range(NP):
            ins = nc.vector.scalar_tensor_tensor(
                out=CS[d][:, p, :], in0=CS[d][:, p, :], scalar=B.decay[:, d, ds(tile, 1), p:p + 1].rearrange("p a b -> p (a b)"),
                in1=bK[:, p * W2:(p + 1) * W2], op0=ALU.mult, op1=ALU.add)
        ins.then_inc(f["decayed"].sem, 1)
        dve.wait_ge(f["decayed"].sem, f["decayed"].at(t, k))
        nc.vector.tensor_tensor(CS[d], CS[d], MASK.unsqueeze(1).to_broadcast([P, NP, W2]), ALU.mult).then_inc(
            f["updated"].sem, 1)
        nc.vector.tensor_tensor(
            HN, bI[:, 0:NP * W2].rearrange("p (h c) -> p h c", h=H),
            CUR[:, 0, :].unsqueeze(2).to_broadcast([P, H, N + 1]), ALU.mult).then_inc(f["gated"].sem, 1)
        dve.wait_ge(f["numerator"].sem, f["numerator"].at(t, k))
        dve.wait_ge(f["gated"].sem, f["gated"].at(t, k))
        nc.vector.tensor_tensor(
            HN, HN, bN[:, 0:NP * W2].rearrange("p (h c) -> p h c", h=H), ALU.add).then_inc(f["summed"].sem, 1)
        dve.wait_ge(f["summed"].sem, f["summed"].at(t, k))
        den = HN[:, :, N]
        nc.vector.scalar_tensor_tensor(out=DEN[:, 0, :], in0=den, scalar=-1.0, in1=den,
                                       op0=ALU.mult, op1=ALU.max).then_inc(f["den_abs"].sem, 1)
        dve.wait_ge(f["den_abs"].sem, f["den_abs"].at(t, k))
        nc.vector.tensor_tensor(DEN[:, 1, :], DEN[:, 0, :], CUR[:, 2, :], ALU.max).then_inc(f["den_max"].sem, 1)
        dve.wait_ge(f["den_max"].sem, f["den_max"].at(t, k))
        nc.vector.reciprocal(DEN[:, 0, :], DEN[:, 1, :]).then_inc(f["den_inv"].sem, 1)
        dve.wait_ge(f["den_inv"].sem, f["den_inv"].at(t, k))
        nc.vector.tensor_tensor(
            HH, HN[:, :, 0:N], DEN[:, 0, :].unsqueeze(2).to_broadcast([P, H, N]), ALU.mult).then_inc(f["quotient"].sem, 1)
        dve.wait_ge(f["quotient"].sem, f["quotient"].at(t, k))
        hs = B.Hs[:, ds(tile, 1), :].rearrange("p a (h c) -> p (a h) c", h=H)
        nc.vector.tensor_tensor(hs, hs, HH, ALU.add).then_inc(f["h_added"].sem, 1)
        dve.wait_ge(f["h_added"].sem, f["h_added"].at(t, k))

    with nc.Block() as block:
        @block.sync
        def _(sp):
            sp.wait_ge(zeroed.sem, zeroed.at(0, 1))
            state_io(sp, loads, io["state_mlstm_C"], io["state_mlstm_n"], False)
            sp.wait_ge(kept.sem, kept.at())
            state_io(sp, stores, S.out[2], S.out[3], True)
            sp.wait_ge(stores.sem, stores.at())

        @block.gpsimd
        def _(pool):
            front_pool(pool, 0, 0)
            over_rounds(pool, step_pool)

        @block.tensor
        def _(pe):
            pe.wait_ge(ready.sem, ready.at())
            exponents_pe(pe, 0, 0)
            scores_pe(pe, 0, 0)
            over_rounds(pe, step_pe, lambda pe: pe.wait_ge(replaced.sem, replaced.at()))

        @block.scalar
        def _(act):
            act.preload_act_table_set(EXP_LN)
            act.wait_ge(ready.sem, ready.at())
            front_act(act, 0, 0)
            over_rounds(act, step_act)

        @block.vector
        def _(dve):
            def states(dve):
                dve.wait_ge(f["updated"].sem, f["updated"].at(0))
                for d in range(2):
                    nc.vector.tensor_copy(final[d], CS[d]).then_inc(kept.sem, 1)
                dve.wait_ge(loads.sem, loads.at())
                dve.wait_ge(kept.sem, kept.at())
                for d in range(2):
                    nc.vector.tensor_copy(CS[d], cached[d]).then_inc(replaced.sem, 1)
                dve.wait_ge(replaced.sem, replaced.at())
            nc.vector.memset(cached[0], 0.0)
            nc.vector.memset(cached[1], 0.0).then_inc(zeroed.sem, 1)
            nc.vector.memset(B.Hs[:, :, :], 0.0)
            for d in range(2):
                nc.vector.memset(CS[d], 0.0).then_inc(ready.sem, 1)
            nc.vector.memset(V1, 1.0).then_inc(ready.sem, 1)
            nc.vector.memset(MASK, 0.0)
            nc.vector.memset(DEN, 0.0).then_inc(ready.sem, 1)
            dve.wait_ge(ready.sem, ready.at())
            nc.vector.memset(MASK[0:N, 0:N + 1], 1.0)
            nc.vector.memset(MASK[N:P, N + 1:W2], 1.0).then_inc(zeroed.sem, 1)
            dve.wait_ge(zeroed.sem, zeroed.at())
            front_dve(dve, 0, 0)
            over_rounds(dve, step_dve, states)


def finish_b(S, B):
    nc = S.nc
    pads = Area(S.PAD[2][:, :])
    HN, SQ, DEV = pads.cut(H, N), pads.cut(H, N), pads.cut(H, N)
    norm = HeadNorm(S, "bn", H, DEV)
    turned, stored, low_loaded = S.flag("bf_turned"), S.flag("bf_stored"), S.flag("bf_low_loaded", 16)
    at = PROWS["mlstm_out_g"][0]

    def round_pe(pe, t):
        pe.wait_ge(norm.normed.sem, norm.normed.at(t))
        if later(t):
            pe.wait_ge(stored.sem, stored.last(t))
        for p in range(NP):
            tr = nc.tensor.transpose(S.PS[0][:, p * P:(p + 1) * P], HN[:, 2 * p:2 * p + 2, :], S.ident[:, :])
        tr.then_inc(turned.sem, 1)

    def spread_dve(dve, t):
        S.apart(dve)
        norm.spread(dve, t, B.Hs[:, ds(t, 1), :].rearrange("p a (h c) -> p (a h) c", h=H), SQ)

    def step_dve(dve, t, after):
        tok = tokens_of(dve, t)
        norm.divide(dve, t, HN)
        if after is not None:
            spread_dve(dve, after)
        dve.wait_ge(turned.sem, turned.at(t))
        for p in range(NP):
            ins = nc.vector.scalar_tensor_tensor(
                out=S.YT[:, 2 + p, ds(tok, P)], in0=S.PS[0][:, p * P:(p + 1) * P], scalar=S.PT[:, at + p:at + p + 1],
                in1=S.Z[:, 9 + p, ds(tok, P)], op0=ALU.mult, op1=ALU.mult)
        ins.then_inc(stored.sem, 1)

    with nc.Block() as block:
        @block.tensor
        def _(pe):
            round_pe(pe, 0)
            with pe.Fori(1, NT) as t:
                round_pe(pe, t)

        @block.scalar
        def _(act):
            act.preload_act_table_set(EXP_LN)
            norm.scalar(act, 0)
            with act.Fori(1, NT) as t:
                norm.scalar(act, t)

        @block.vector
        def _(dve):
            spread_dve(dve, 0)
            tiles_ahead(dve, step_dve)

        @block.sync
        def _(sp):
            sp.dma_start(S.XT[:, 3:7, :], S.low_dram[:, 3:7, :]).then_inc(low_loaded.sem, 16)

        @block.gpsimd
        def _(pool):
            pool.wait_ge(low_loaded.sem, low_loaded.at())
            for k in range(3, 7):
                nc.gpsimd.tensor_copy(S.XTr[:, k, :], S.XT[:, k, :])


def project_c(S):
    nc, io = S.nc, S.io
    w_in = io["w_in"][0].rearrange("(k p) n -> p k n", p=P)
    dense = Dense(S, "c", [[Area(yt[:, 5:8, :].rearrange("p k t -> p (k t)")[:, 2 * PADW:]).cut(KB, P),
                            Area(rs[:, 24:]).cut(KB, P)] for yt, rs in ((S.YT, S.RS), (S.YTr, S.RSr))])
    low_loaded, low_back = S.flag("low_part_loaded", 32), S.flag("low_part_back", 4)
    ZP = S.PAD[0:2]
    SM = S.PAD[2:4]
    yt = Area(S.YT[:, 5:8, :].rearrange("p k t -> p (k t)"))
    CV = [yt.cut(PADW) for i in range(2)]
    half_mu, one_mu = S.RS[:, 0:12], S.RS[:, 12:24]
    cleared, coeffs = S.flag("c_pads_cleared", 2), S.flag("c_mu", 2)
    neighbours, own = S.flag("c_neighbours", 2), S.flag("c_own", 2)
    mixed = S.flag("c_mixed", 2, in_hand=2)
    with nc.Block() as block:
        @block.gpsimd
        def _(pool):
            dense.start(pool)
            pool.sem_inc(mixed.sem, mixed.in_hand)
            for z in ZP:
                nc.gpsimd.memset(z[:, :], 0.0).then_inc(cleared.sem, 1)
            with pool.Fori(0, 6) as i:
                for slot in range(2):
                    dense.divide(pool, i, slot)

        @block.sync
        def _(sp):
            for slot in range(2):
                dense.load(sp, 0, slot, w_in[:, :, OFF_C + slot * P:OFF_C + (slot + 1) * P])
            for a, b in ((0, 3), (7, 8)):
                sp.dma_start(S.XT[:, a:b, :], S.low_dram[:, a:b, :]).then_inc(low_loaded.sem, 16)
            with sp.Fori(1, 6) as i:
                for slot in range(2):
                    dense.load(sp, i, slot, w_in[:, :, ds(i * 256 + OFF_C + slot * P, P)])

        @block.tensor
        def _(pe):
            pe.wait_ge(low_back.sem, low_back.at())
            with pe.Fori(0, 6) as i:
                for slot in range(2):
                    dense.multiply(pe, i, slot, group(S.HTr), group(S.XTr))

        @block.scalar
        def _(act):
            act.wait_ge(low_loaded.sem, low_loaded.at())
            for k in (0, 1, 2, 7):
                nc.scalar.copy(S.XTr[:, k, :], S.XT[:, k, :]).then_inc(low_back.sem, 1)
            act.wait_ge(cleared.sem, cleared.at())
            with act.Fori(0, 6) as i:
                for slot in range(2):
                    act.wait_ge(mixed.sem, mixed.last(i, slot + 1))
                    to_padded(S, dense, act, i, slot, ZP[slot])
            act.wait_ge(mixed.sem, mixed.at(5))
            nc.scalar.activation(S.Z[:, 9, :], S.Z[:, 9, :], ACT.Tanh)
            nc.scalar.activation(S.Z[:, 11, :], S.Z[:, 11, :], ACT.Sigmoid)

        @block.vector
        def _(dve):
            nc.vector.tensor_scalar(half_mu, S.param("rwkv_mu"), 0.5, None, ALU.mult).then_inc(coeffs.sem, 1)
            nc.vector.tensor_scalar(one_mu, S.param("rwkv_mu"), -1.0, 1.0, ALU.mult, ALU.add).then_inc(coeffs.sem, 1)
            dve.wait_ge(coeffs.sem, coeffs.at())
            with dve.Fori(0, 6) as i:
                for slot in range(2):
                    blk = dve.snap(i * 2 + slot, min_val=0, max_val=11)
                    dve.wait_ge(dense.drained[NG - 1].sem, dense.drained[NG - 1].at(i, slot + 1))
                    dve.wait_ge(mixed.sem, mixed.last(i, slot + 1))
                    nc.vector.tensor_tensor(SM[slot][:, 1:LAT0 + N_LAT], ZP[slot][:, 0:LAT0 + N_LAT - 1],
                                            ZP[slot][:, 2:LAT0 + N_LAT + 1], ALU.add).then_inc(neighbours.sem, 1)
                    nc.vector.tensor_scalar(CV[slot][:, 1:LAT0 + N_LAT], ZP[slot][:, 1:LAT0 + N_LAT],
                                                    one_mu[:, ds(blk, 1)], None, ALU.mult).then_inc(own.sem, 1)
                    dve.wait_ge(own.sem, own.at(i, slot + 1))
                    dve.wait_ge(neighbours.sem, neighbours.at(i, slot + 1))
                    for a, n, p in SEQS:
                        ins = nc.vector.scalar_tensor_tensor(
                            out=S.Z[:, ds(blk, 1), a:a + n].rearrange("p a n -> p (a n)"), in0=SM[slot][:, p:p + n],
                            scalar=half_mu[:, ds(blk, 1)], in1=CV[slot][:, p:p + n], op0=ALU.mult, op1=ALU.add)
                    ins.then_inc(mixed.sem, 1)


class StoreC:

    def __init__(self, S):
        X = Area(S.XT[:, :, :].rearrange("p k t -> p (k t)"))
        HA = Area(S.HT[:, :, :].rearrange("p k t -> p (k t)"))
        PD = [Area(p[:, :]) for p in S.PAD]
        W = [Area(w[:, :, :].rearrange("p k n -> p (k n)")) for w in S.W]
        self.A = X.cut(2, NP, T)
        self.nkk, self.Y = HA.cut(NP, T), HA.cut(NT, C_W)
        self.TI, self.TT, self.Zm = X.cut(H, P), X.cut(H, P), X.cut(H, P)
        self.LT, self.RB, self.AK = HA.cut(H, P), HA.cut(H, P), HA.cut(H, P)
        self.RK, self.BT = PD[0].cut(H, P), PD[0].cut(NP, P)
        yt = Area(S.YT[:, 5:8, :].rearrange("p k t -> p (k t)"))
        self.AR = [PD[1].cut(2, NP, P), yt.cut(2, NP, P)]
        self.KT = PD[1].cut(NP, P)
        self.Bt, self.Kt, self.Vt = (PD[2].cut(NP, P) for _ in range(3))
        self.U, self.Q, self.Sc = (PD[3].cut(NP, P) for _ in range(3))
        self.W2 = W[0].cut(2, C_W)
        rs = Area(S.RS[:, :])
        self.S = [rs.cut(NP, P) for _ in range(2)]
        self.VS = rs.cut(NP, P)
        self.A2 = W[1].cut(2, C_W)
        z = Area(S.Z[:, 10, :])
        self.EM, self.t1, self.t2 = z.cut(NP, P), z.cut(NP, P), z.cut(NP, P)
        w1 = Area(S.W[1][:, :, :].rearrange("p k n -> p (k n)"))
        self.SW = w1.cut(NP, P)
        self.cs = S.sb("c_sums", P, NP, P + 1)
        self.EP = [S.sb("c_decays", P, NP, P + 1), yt.cut(NP, P + 1)]
        self.half_w0 = yt.cut(2 * NP)
        self.cached, self.final = ([yt.cut(NP, P) for _ in range(2)] for _ in range(2))
        self.mid = S.sb("c_mid", P, 3, NP)
        self.one_ka = S.sb("c_one_ka", P, NP)


def prepare_c(S, C):
    nc, io = S.nc, S.io
    kkr = [S.YT[:, 5 + p, :] for p in range(NP)]
    sq = [S.PAD[p][:, 0:T] for p in range(NP)]
    loaded, cleared = S.flag("cp_loads", 16 * 4), S.flag("cp_cleared", 2)
    squared, summed, rooted = S.flag("cp_squared", NP), S.flag("cp_summed", NP), S.flag("cp_rooted", NP)
    scaled, clipped, inverted = S.flag("cp_scaled", NP), S.flag("cp_clipped", NP), S.flag("cp_inverted", NP)
    lora, a_done, made = S.flag("cp_lora", 6), S.flag("cp_a", 6), S.flag("cp_levels")
    with nc.Block() as block:
        @block.gpsimd
        def _(pool):
            n = 0

            def one(ins):
                nonlocal n
                ins.then_inc(made.sem, 1)
                n += 1
                pool.wait_ge(made.sem, made.at(0, n))

            for w in (C.W2, C.A2):
                nc.gpsimd.memset(w, 0.0).then_inc(cleared.sem, 1)
            pool.wait_ge(cleared.sem, cleared.at())
            for d in range(2):
                for i in range(LEVELS):
                    b = 1 << i
                    m = S.level[:, d, i, :].rearrange("p (n h x) -> p n h x", h=2, x=b)
                    src = m[:, :, d, :]
                    one(nc.gpsimd.memset(S.level[:, d, i, :], 0.0))
                    one(nc.gpsimd.memset(src, 1.0))
                    first = b if d == 0 else 0
                    for base, mult, step in ((-first, 1, -2 * b), (first + b - 1, -1, 2 * b)):
                        one(nc.gpsimd.affine_select(out=src, in_=src, compare_op=ALU.is_ge, fill=0.0, base=base,
                                                    pattern=[[step, P // (2 * b)], [0, b]], channel_multiplier=mult))

        @block.sync
        def _(sp):
            sp.wait_ge(cleared.sem, cleared.at())
            for d in range(2):
                r = slice(N * d, N * d + N)
                sp.dma_start(C.W2[r, d, :], io["rwkv_w2"][0, d]).then_inc(loaded.sem, 16)
                sp.dma_start(C.A2[r, d, :], io["rwkv_a2"][0, d]).then_inc(loaded.sem, 16)

        @block.tensor
        def _(pe):
            for p in range(NP):
                pe.wait_ge(squared.sem, squared.at(0, p + 1))
                if p:
                    pe.wait_ge(rooted.sem, rooted.at(0, p))
                for g in range(NG):
                    mm = nc.tensor.matmul(S.PS[g][:, 0:GRP], S.halves[:, :], sq[p][:, g * GRP:(g + 1) * GRP],
                                          start=True, stop=True)
                mm.then_inc(summed.sem, 1)
            pe.wait_ge(loaded.sem, loaded.at())
            for d in range(2):
                for p in range(NP):
                    n = d * NP + p
                    if n:
                        pe.wait_ge(a_done.sem, a_done.at(0, n))
                    for g in range(NG):
                        mm = nc.tensor.matmul(S.PS[3 + g][:, 0:GRP], C.A2[:, d, p * P:(p + 1) * P],
                                              S.Z[:, 10, g * GRP:(g + 1) * GRP], start=True, stop=True)
                    mm.then_inc(lora.sem, 1)

        @block.scalar
        def _(act):
            for p in range(NP):
                act.wait_ge(scaled.sem, scaled.at(0, p + 1))
                nc.scalar.activation(sq[p], kkr[p], ACT.Square).then_inc(squared.sem, 1)
            for p in range(NP):
                act.wait_ge(summed.sem, summed.at(0, p + 1))
                for g in range(NG):
                    ins = nc.scalar.activation(sq[p][:, g * GRP:(g + 1) * GRP], S.PS[g][:, 0:GRP], ACT.Sqrt)
                ins.then_inc(rooted.sem, 1)
            for d in range(2):
                for p in range(NP):
                    act.wait_ge(lora.sem, lora.at(0, d * NP + p + 1))
                    for g in range(NG):
                        ins = nc.scalar.activation(C.A[:, d, p, g * GRP:(g + 1) * GRP], S.PS[3 + g][:, 0:GRP],
                                                   ACT.Sigmoid, bias=S.param("rwkv_a0", d * NP + p, 1))
                    ins.then_inc(a_done.sem, 1)

        @block.vector
        def _(dve):
            for p in range(NP):
                nc.vector.tensor_scalar(kkr[p], S.Z[:, 3 + p, :], S.param("rwkv_k_k", p, 1), None, ALU.mult).then_inc(
                    scaled.sem, 1)
            nc.vector.tensor_scalar(C.one_ka[:, :], S.param("rwkv_k_a"), -1.0, 1.0, ALU.mult, ALU.add)
            for p in range(NP):
                dve.wait_ge(rooted.sem, rooted.at(0, p + 1))
                nc.vector.tensor_scalar(sq[p], sq[p], 1e-12, None, ALU.max).then_inc(clipped.sem, 1)
                dve.wait_ge(clipped.sem, clipped.at(0, p + 1))
                nc.vector.reciprocal(sq[p], sq[p]).then_inc(inverted.sem, 1)
                dve.wait_ge(inverted.sem, inverted.at(0, p + 1))
                nc.vector.scalar_tensor_tensor(out=C.nkk[:, p, :], in0=kkr[p], scalar=-1.0, in1=sq[p],
                                               op0=ALU.mult, op1=ALU.mult)


def recur_c(S, C):
    nc, io = S.nc, S.io
    names = ("decay_arg", "tanh", "sw", "summed", "middle", "exped", "staged_v", "a_rows", "r_rows", "b_rows", "k_rows",
             "k_dir", "a_em", "ka", "turned", "copied", "level0", "t_first", "seeded", "moved", "q", "q_copied",
             "u", "u_copied", "state", "y", "added", "new_state", "y_added")
    f = {k: S.flag("rwkv_" + k, 2) for k in names}
    gram, masked = S.flag("rwkv_gram", 2 * 10), S.flag("rwkv_masked", 2 * 10)
    n_lv = LEVELS - 1
    lt, zm = S.flag("rwkv_lt", 4 * n_lv), S.flag("rwkv_zm", 4 * n_lv)
    tz, grown = S.flag("rwkv_tz", 4 * n_lv), S.flag("rwkv_grown", 4 * n_lv)
    t_grown = S.flag("rwkv_t_grown", 4 * (n_lv - 1))
    ready = S.flag("rwkv_ready", 3)
    s_out, s_in = S.flag("rwkv_state_stores", 16 * 12), S.flag("rwkv_state_loads", 16 * 12)
    s_turned, s_copied, s_cleared = S.flag("rwkv_state_turned", 2), S.flag("rwkv_state_copied", 4), S.flag("rwkv_cleared")
    bank = [S.PS[i][:, 0:3 * P] for i in range(8)]
    b3 = [b.rearrange("p (h t) -> p h t", h=3) for b in bank]
    A_of, R_ = [ar[:, 0, :, :] for ar in C.AR], [ar[:, 1, :, :] for ar in C.AR]
    w0_at, ka_at = PROWS["rwkv_w0"][0], PROWS["rwkv_k_a"][0]

    def rows_of(h):
        return slice(N * (h % 2), N * (h % 2) + N)

    def strict(d, turned):
        return S.tri["UPS" if (d == 0) == turned else "LOS"]

    def products(d):
        A_, R = A_of[d], R_[d]
        return (("L_turned", C.BT, A_, strict(d, True), C.LT),
                ("L", A_, C.BT, None, C.TI),
                ("AK", C.KT, A_, strict(d, True), C.AK),
                ("RB", C.BT, R, S.tri["UPI" if d == 0 else "LOI"], C.RB),
                ("RK", C.KT, R, S.tri["UPI" if d == 0 else "LOI"], C.RK))


    def prepare_pool(pool, t, d):
        tok, k = direction_tiles(pool, t)[0][d], d + 1
        if later(t, k):
            pool.wait_ge(f["turned"].sem, f["turned"].front(t, k))
        S.apart(pool)
        nc.gpsimd.tensor_copy(C.VS, S.Z[:, 6:9, ds(tok, P)]).then_inc(f["staged_v"].sem, 1)
        pool.wait_ge(f["exped"].sem, f["exped"].at(t, k))
        if later(t):
            pool.wait_ge(f["y"].sem, f["y"].last(t, k))
        S.apart(pool)
        off = 1 - d
        nc.gpsimd.tensor_tensor(R_[d], S.Z[:, 0:3, ds(tok, P)], C.EP[d][:, :, off:off + P],
                                ALU.mult).then_inc(f["r_rows"].sem, 1)

    def step_pool(pool, t, d, more=True):
        k = d + 1
        pool.wait_ge(masked.sem, masked.at(t, 10 * d + 2))
        nc.gpsimd.tensor_tensor(
            C.TT, C.LT, S.level[:, 1 - d, 0, :].unsqueeze(1).to_broadcast([P, H, P]), ALU.mult).then_inc(
                f["t_first"].sem, 1)
        pool.wait_ge(f["t_first"].sem, f["t_first"].at(t, k))
        nc.gpsimd.tensor_tensor(
            C.TT, C.TT, S.ident[:, :].unsqueeze(1).to_broadcast([P, H, P]), ALU.add).then_inc(f["seeded"].sem, 1)
        if more:
            prepare_pool(pool, *following(pool, t, d))

    def prepare_pe(pe, t, d):
        tok = direction_tiles(pe, t)[0][d]
        for p in range(NP):
            mm = nc.tensor.matmul(bank[6][:, p * P:(p + 1) * P], C.W2[:, d, p * P:(p + 1) * P],
                                  S.Z[:, 9, ds(tok, P)], start=True, stop=True)
        mm.then_inc(f["decay_arg"].sem, 1)

    def step_pe(pe, t, d, more=True):
        k, A_, R = d + 1, A_of[d], R_[d]
        for x in ("a_rows", "b_rows", "k_rows", "r_rows", "staged_v"):
            pe.wait_ge(f[x].sem, f[x].at(t, k))
        if later(t, k):
            pe.wait_ge(grown.sem, grown.front(t, 2 * n_lv * d + 1))
        for i, x in enumerate((C.BT, C.KT)):
            for p in range(NP):
                tr = nc.tensor.transpose(bank[4 + i][:, p * P:(p + 1) * P], x[:, p, :], S.ident[:, :])
        for i, (_, source, target, _, _) in enumerate(products(d)):
            for half in range(2):
                n = 2 * i + half
                if n >= 4:
                    pe.wait_ge(masked.sem, masked.at(t, 10 * d + n - 3))
                for j in range(NP):
                    h = 2 * j + half
                    mm = nc.tensor.matmul(bank[n % 4][:, j * P:(j + 1) * P], source[rows_of(h), h // 2, :],
                                          target[rows_of(h), h // 2, :], start=True, stop=True)
                mm.then_inc(gram.sem, 1)
        if later(t, k):
            pe.wait_ge(f["new_state"].sem, f["new_state"].front(t, k))
        for p in range(NP):
            tr = nc.tensor.transpose(bank[6][:, p * P:(p + 1) * P], C.VS[:, p, :], S.ident[:, :])
        tr.then_inc(f["turned"].sem, 1)
        pe.wait_ge(f["seeded"].sem, f["seeded"].at(t, k))
        pe.wait_ge(f["level0"].sem, f["level0"].at(t, k))
        pe.wait_ge(masked.sem, masked.at(t, 10 * d + 10))
        for i in range(n_lv):
            m = 2 * n_lv * d + 2 * i
            if i == 1 and more:
                prepare_pe(pe, *following(pe, t, d))
            for half in range(2):
                if i:
                    pe.wait_ge(t_grown.sem, t_grown.at(t, 2 * (n_lv - 1) * d + 2 * (i - 1) + half + 1))
                for j in range(3):
                    x = 3 * half + j
                    mm = nc.tensor.matmul(bank[half][:, j * P:(j + 1) * P], C.LT[:, x, :], C.TI[:, x, :],
                                          start=True, stop=True)
                mm.then_inc(lt.sem, 1)
            if i == 0:
                pe.wait_ge(f["copied"].sem, f["copied"].at(t, k))
            for half in range(2):
                pe.wait_ge(zm.sem, zm.at(t, m + half + 1))
                if i:
                    pe.wait_ge(grown.sem, grown.at(t, m - 2 + half + 1))
                if i < n_lv - 1:
                    for j in range(3):
                        x = 3 * half + j
                        nc.tensor.matmul(bank[2 + half][:, j * P:(j + 1) * P], C.TT[:, x, :], C.Zm[:, x, :],
                                         start=True, stop=True)
                for j in range(3):
                    x = 3 * half + j
                    mm = nc.tensor.matmul(bank[4 + half][:, j * P:(j + 1) * P], C.Zm[:, x, :], C.TT[:, x, :],
                                          start=True, stop=True)
                mm.then_inc(tz.sem, 1)
        pe.wait_ge(f["moved"].sem, f["moved"].at(t, k))
        if more:
            n, e = following(pe, t, d)
            pe.wait_ge(f["sw"].sem, f["sw"].at(n, e + 1))
        for h in range(H):
            if h % 2 == 0:
                nc.tensor.matmul(bank[6][:, h * N:(h + 2) * N], A_[:, h // 2, :], C.Sc[:, h // 2, :],
                                 start=True, stop=False)
            mm = nc.tensor.matmul(bank[6][:, h * N:(h + 1) * N], C.AK[:, slot_of(h), :],
                                  C.Vt[:, h // 2, N * (h % 2):N * (h % 2) + N], start=False, stop=(h % 2 == 1))
        mm.then_inc(f["q"].sem, 1)
        pe.wait_ge(grown.sem, grown.at(t, 2 * n_lv * (d + 1)))
        pe.wait_ge(f["q_copied"].sem, f["q_copied"].at(t, k))
        if later(t, k):
            pe.wait_ge(f["y_added"].sem, f["y_added"].front(t, k))
        for h in range(H):
            mm = nc.tensor.matmul(bank[7][:, h * N:(h + 1) * N], C.TT[:, slot_of(h), :],
                                  C.Q[:, h // 2, N * (h % 2):N * (h % 2) + N], start=True, stop=True)
        mm.then_inc(f["u"].sem, 1)
        pe.wait_ge(f["u_copied"].sem, f["u_copied"].at(t, k))
        for p in range(NP):
            nc.tensor.matmul(bank[6][:, p * P:(p + 1) * P], C.Bt[:, p, :], C.U[:, p, :], start=True, stop=False)
            mm = nc.tensor.matmul(bank[6][:, p * P:(p + 1) * P], C.Kt[:, p, :], C.Vt[:, p, :], start=False, stop=True)
        mm.then_inc(f["state"].sem, 1)
        for h in range(H):
            o, c = bank[7][:, h * N:(h + 1) * N], slice(N * (h % 2), N * (h % 2) + N)
            if h % 2 == 0:
                nc.tensor.matmul(bank[7][:, h * N:(h + 2) * N], R[:, h // 2, :], C.Sc[:, h // 2, :],
                                 start=True, stop=False)
            nc.tensor.matmul(o, C.RB[:, slot_of(h), :], C.U[:, h // 2, c], start=False, stop=False)
            mm = nc.tensor.matmul(o, C.RK[:, slot_of(h), :], C.Vt[:, h // 2, c], start=False, stop=(h % 2 == 1))
        mm.then_inc(f["y"].sem, 1)

    def prepare_act(act, t, d):
        k, own = d + 1, slice(1 - d, 1 - d + P)
        act.wait_ge(f["decay_arg"].sem, f["decay_arg"].at(t, k))
        if later(t, k):
            act.wait_ge(f["summed"].sem, f["summed"].front(t, k))
        for p in range(NP):
            ins = nc.scalar.activation(C.SW[:, p, :], bank[6][:, p * P:(p + 1) * P], ACT.Tanh,
                                       bias=C.half_w0[:, d * NP + p:d * NP + p + 1], scale=0.5)
        ins.then_inc(f["tanh"].sem, 1)
        act.wait_ge(f["tanh"].sem, f["tanh"].at(t, k))
        nc.scalar.activation(C.SW, C.SW, ACT.Identity, bias=S.eps[:, 3:4], scale=0.5).then_inc(f["sw"].sem, 1)
        act.wait_ge(f["middle"].sem, f["middle"].at(t, k))
        if later(t, k):
            for x in ("b_rows", "k_rows", "moved"):
                act.wait_ge(f[x].sem, f[x].front(t, k))
        if later(t):
            act.wait_ge(f["r_rows"].sem, f["r_rows"].last(t, k))
            act.wait_ge(f["new_state"].sem, f["new_state"].last(t, k))
        for p in range(NP):
            nc.scalar.activation(C.EP[d][:, p, :], C.cs[:, p, :], ACT.Exp, scale=-DECAY, bias=C.mid[:, 0, p:p + 1])
            nc.scalar.activation(C.EM[:, p, :], C.cs[:, p, own], ACT.Exp, scale=DECAY, bias=C.mid[:, 1, p:p + 1])
        nc.scalar.activation(C.mid[:, 2, :], C.mid[:, 1, :], ACT.Exp).then_inc(f["exped"].sem, 1)

    def step_act(act, t, d, more=True):
        k = d + 1
        act.wait_ge(f["turned"].sem, f["turned"].at(t, k))
        if later(t, k):
            act.wait_ge(f["y"].sem, f["y"].front(t, k))
        for i, x in enumerate((C.Bt, C.Kt, C.Vt)):
            ins = nc.scalar.copy(x, b3[4 + i])
        ins.then_inc(f["copied"].sem, 1)
        if more:
            prepare_act(act, *following(act, t, d))
        act.wait_ge(f["q"].sem, f["q"].at(t, k))
        nc.scalar.copy(C.Q, b3[6]).then_inc(f["q_copied"].sem, 1)
        act.wait_ge(f["u"].sem, f["u"].at(t, k))
        nc.scalar.copy(C.U, b3[7]).then_inc(f["u_copied"].sem, 1)

    def sum_dve(dve, t, d):
        k, own = d + 1, slice(1 - d, 1 - d + P)
        dve.wait_ge(f["sw"].sem, f["sw"].at(t, k))
        if later(t, k):
            dve.wait_ge(f["exped"].sem, f["exped"].front(t, k))
            dve.wait_ge(f["moved"].sem, f["moved"].front(t, k))
        zero = C.cs[:, :, 0:1] if d == 0 else C.cs[:, :, P:P + 1]
        nc.vector.memset(zero, 0.0)
        for p in range(NP):
            o, x = C.cs[:, p, own], C.SW[:, p, :]
            if d:
                o, x = o[:, ::-1], x[:, ::-1]
            ins = nc.vector.tensor_tensor_scan(o, S.ones[:, :], x, 0.0, ALU.mult, ALU.add)
        ins.then_inc(f["summed"].sem, 1)
        dve.wait_ge(f["summed"].sem, f["summed"].at(t, k))
        nc.vector.tensor_scalar(C.mid[:, 0, :], C.cs[:, :, P // 2], DECAY, None, ALU.mult)
        nc.vector.tensor_scalar(C.mid[:, 1, :], C.cs[:, :, P // 2], -DECAY, None, ALU.mult).then_inc(f["middle"].sem, 1)

    def rows_dve(dve, t, d):
        k, past, A_ = d + 1, slice(d, d + P), A_of[d]
        at = ds(direction_tiles(dve, t)[0][d], P)
        if later(t, k):
            dve.wait_ge(f["k_rows"].sem, f["k_rows"].front(t, k))
        for p in range(NP):
            ins = nc.vector.tensor_scalar(C.t2[:, p, :], C.A[:, d, p, at], S.PT[:, ka_at + p:ka_at + p + 1],
                                          C.one_ka[:, p:p + 1], ALU.mult, ALU.add)
        ins.then_inc(f["ka"].sem, 1)
        dve.wait_ge(f["exped"].sem, f["exped"].at(t, k))
        nc.vector.tensor_tensor(C.t1, C.A[:, d, :, at], C.EM, ALU.mult).then_inc(f["a_em"].sem, 1)
        dve.wait_ge(f["ka"].sem, f["ka"].at(t, k))
        nc.vector.tensor_tensor(C.t2, C.t2, S.Z[:, 3:6, at], ALU.mult).then_inc(f["k_dir"].sem, 1)
        if later(t, k):
            dve.wait_ge(f["turned"].sem, f["turned"].front(t, k))
        dve.wait_ge(f["a_em"].sem, f["a_em"].at(t, k))
        nc.vector.scalar_tensor_tensor(out=C.BT, in0=C.nkk[:, :, at], scalar=-1.0, in1=C.t1,
                                       op0=ALU.mult, op1=ALU.mult).then_inc(f["b_rows"].sem, 1)
        dve.wait_ge(f["k_dir"].sem, f["k_dir"].at(t, k))
        nc.vector.tensor_tensor(C.KT, C.t2, C.EM, ALU.mult).then_inc(f["k_rows"].sem, 1)
        if later(t):
            dve.wait_ge(f["q"].sem, f["q"].last(t, k))
        nc.vector.tensor_tensor(A_, C.nkk[:, :, at], C.EP[d][:, :, past], ALU.mult).then_inc(f["a_rows"].sem, 1)

    def step_dve(dve, t, d, more=True):
        k = d + 1
        tile = direction_tiles(dve, t)[1][d]
        if later(t, k):
            dve.wait_ge(f["new_state"].sem, f["new_state"].front(t, k))
        nc.vector.tensor_tensor(
            C.Sc, C.S[d], C.mid[:, 2, :].unsqueeze(2).to_broadcast([P, NP, P]), ALU.mult).then_inc(f["moved"].sem, 1)
        for i, (name, _, _, mask, dst) in enumerate(products(d)):
            for half in range(2):
                n = 2 * i + half
                dve.wait_ge(gram.sem, gram.at(t, 10 * d + n + 1))
                m = S.level[:, d, 0, :] if mask is None else mask[:, :]
                nc.vector.tensor_tensor(dst[:, 3 * half:3 * half + 3, :], b3[n % 4],
                                        m.unsqueeze(1).to_broadcast([P, 3, P]), ALU.mult).then_inc(masked.sem, 1)
            if name == "L":
                dve.wait_ge(masked.sem, masked.at(t, 10 * d + 4))
                nc.vector.tensor_tensor(
                    C.TI, C.TI, S.ident[:, :].unsqueeze(1).to_broadcast([P, H, P]), ALU.add).then_inc(f["level0"].sem, 1)
        dve.wait_ge(f["seeded"].sem, f["seeded"].at(t, k))
        def mask_dve(i, half):
            m = 2 * n_lv * d + 2 * i
            dve.wait_ge(lt.sem, lt.at(t, m + half + 1))
            if i:
                dve.wait_ge(tz.sem, tz.at(t, m - 2 + half + 1))
            nc.vector.tensor_tensor(
                C.Zm[:, 3 * half:3 * half + 3, :], b3[half],
                S.level[:, d, i + 1, :].unsqueeze(1).to_broadcast([P, 3, P]), ALU.mult).then_inc(zm.sem, 1)

        for half in range(2):
            mask_dve(0, half)
        for i in range(n_lv):
            m = 2 * n_lv * d + 2 * i
            for half in range(2):
                dve.wait_ge(tz.sem, tz.at(t, m + half + 1))
                x = slice(3 * half, 3 * half + 3)
                if i < n_lv - 1:
                    nc.vector.tensor_tensor(C.TI[:, x, :], C.TI[:, x, :], b3[2 + half], ALU.add).then_inc(t_grown.sem, 1)
                    if half:
                        mask_dve(i + 1, 0)
                nc.vector.tensor_tensor(C.TT[:, x, :], C.TT[:, x, :], b3[4 + half], ALU.add).then_inc(grown.sem, 1)
            if i < n_lv - 1:
                mask_dve(i + 1, 1)
            if i == 2 and more:
                sum_dve(dve, *following(dve, t, d))
        if more:
            rows_dve(dve, *following(dve, t, d))
        dve.wait_ge(f["state"].sem, f["state"].at(t, k))
        dve.wait_ge(f["y"].sem, f["y"].at(t, k))
        nc.vector.tensor_tensor(C.Sc, C.Sc, b3[6], ALU.add).then_inc(f["added"].sem, 1)
        dve.wait_ge(f["added"].sem, f["added"].at(t, k))
        end = P if d == 0 else 0
        for p in range(NP):
            ins = nc.vector.scalar_tensor_tensor(out=C.S[d][:, p, :], in0=C.Sc[:, p, :], scalar=C.EP[d][:, p, end:end + 1],
                                                 in1=S.halves[:, :], op0=ALU.mult, op1=ALU.mult)
        ins.then_inc(f["new_state"].sem, 1)
        y = C.Y[:, ds(tile, 1), :].rearrange("p a c -> p (a c)")
        if later(t, k):
            dve.wait_ge(f["y_added"].sem, f["y_added"].front(t, k))
        nc.vector.tensor_tensor(y, y, bank[7], ALU.add).then_inc(f["y_added"].sem, 1)


    with nc.Block() as block:
        @block.sync
        def _(sp):
            for store in (False, True):
                if store:
                    sp.wait_ge(s_copied.sem, s_copied.at(0, 2))
                else:
                    sp.wait_ge(s_cleared.sem, s_cleared.at())
                dram = S.out[5] if store else io["state_rwkv_S"]
                for d in range(2):
                    for h in range(H):
                        on_chip = (C.final if store else C.cached)[d][rows_of(h), h // 2, N * (h % 2):N * (h % 2) + N]
                        a, b = (dram[0, 0, d, h], on_chip) if store else (on_chip, dram[0, 0, d, h])
                        sp.dma_start(a, b).then_inc((s_out if store else s_in).sem, 16)
            sp.wait_ge(s_out.sem, s_out.at())

        @block.gpsimd
        def _(pool):
            pool.wait_ge(ready.sem, ready.at())
            prepare_pool(pool, 0, 0)
            over_rounds(pool, step_pool)

        @block.tensor
        def _(pe):
            def states(pe):
                pe.wait_ge(f["new_state"].sem, f["new_state"].at(0))
                pe.wait_ge(f["y_added"].sem, f["y_added"].at(0))
                for d in range(2):
                    for p in range(NP):
                        tr = nc.tensor.transpose(bank[4 + d][:, p * P:(p + 1) * P], C.S[d][:, p, :], S.ident[:, :])
                tr.then_inc(s_turned.sem, 1)
                pe.wait_ge(s_in.sem, s_in.at())
                for d in range(2):
                    for p in range(NP):
                        tr = nc.tensor.transpose(bank[d][:, p * P:(p + 1) * P], C.cached[d][:, p, :], S.ident[:, :])
                tr.then_inc(s_turned.sem, 1)
                pe.wait_ge(s_copied.sem, s_copied.at())
            pe.wait_ge(ready.sem, ready.at())
            prepare_pe(pe, 0, 0)
            over_rounds(pe, step_pe, states)

        @block.scalar
        def _(act):
            act.preload_act_table_set(EXP_TANH)
            act.wait_ge(ready.sem, ready.at())
            prepare_act(act, 0, 0)
            over_rounds(act, step_act)

        @block.vector
        def _(dve):
            def states(dve):
                dve.wait_ge(s_turned.sem, s_turned.at(0, 1))
                for d in range(2):
                    nc.vector.tensor_copy(C.final[d], b3[4 + d]).then_inc(s_copied.sem, 1)
                dve.wait_ge(s_turned.sem, s_turned.at(0, 2))
                for d in range(2):
                    nc.vector.tensor_copy(C.S[d], b3[d]).then_inc(s_copied.sem, 1)
                dve.wait_ge(s_copied.sem, s_copied.at())
            nc.vector.memset(C.cached[0], 0.0)
            nc.vector.memset(C.cached[1], 0.0).then_inc(s_cleared.sem, 1)
            nc.vector.memset(S.eps[:, 3:4], 0.5)
            nc.vector.memset(C.Y, 0.0)
            for d in range(2):
                nc.vector.memset(C.S[d], 0.0).then_inc(ready.sem, 1)
            nc.vector.tensor_scalar(C.half_w0, S.PT[:, w0_at:w0_at + 2 * NP], 0.5, None, ALU.mult)
            nc.vector.memset(C.mid[:, :, :], 0.0).then_inc(ready.sem, 1)
            dve.wait_ge(ready.sem, ready.at())
            sum_dve(dve, 0, 0)
            rows_dve(dve, 0, 0)
            over_rounds(dve, step_dve, states)


def finish_c(S, C):
    nc, io = S.nc, S.io
    DEV, SQ, YN = C.TI[:, 0:3, :], C.TI[:, 3:6, :], C.TT[:, 0:3, :]
    as_heads = lambda x: x.rearrange("p a b -> p (a b)").rearrange("p (h c) -> p h c", h=H)
    DEV, SQ, YN = as_heads(DEV), as_heads(SQ), as_heads(YN)
    KS, M, BV, OUT = C.LT[:, 0:3, :], C.LT[:, 3:6, :], C.RB[:, 0:3, :], C.RB[:, 3:6, :]
    G2 = Area(S.PAD[0][:, :]).cut(C_W)
    coef = C.mid
    norm = HeadNorm(S, "cn", H, DEV)
    names = ("a_sum", "k_scale", "k_both", "r_k", "bonus", "bonus_v", "gate", "turned", "normed_v", "stored")
    f = {k: S.flag("cf_" + k) for k in names}
    loaded, ready = S.flag("cf_g2", 16), S.flag("cf_coef")
    ka, rk, lng = (PROWS[x][0] for x in ("rwkv_k_a", "rwkv_r_k", "rwkv_ln_g"))

    def round_pe(pe, t):
        tok = 0 if isinstance(t, int) else pe.snap(t * P, min_val=0, max_val=T - P)
        if later(t):
            pe.wait_ge(f["stored"].sem, f["stored"].last(t))
        for p in range(NP):
            mm = nc.tensor.matmul(S.PS[0][:, p * P:(p + 1) * P], G2[:, p * P:(p + 1) * P], S.Z[:, 11, ds(tok, P)],
                                  start=True, stop=True)
        mm.then_inc(f["gate"].sem, 1)
        pe.wait_ge(f["r_k"].sem, f["r_k"].at(t))
        nc.tensor.matmul(S.PS[1][:, 0:3 * P], S.halves[:, :], M, start=True, stop=True).then_inc(f["bonus"].sem, 1)
        pe.wait_ge(norm.normed.sem, norm.normed.at(t))
        for p in range(NP):
            tr = nc.tensor.transpose(S.PS[2][:, p * P:(p + 1) * P], YN[:, 2 * p:2 * p + 2, :], S.ident[:, :])
        tr.then_inc(f["turned"].sem, 1)

    def front_dve(dve, t):
        at = ds(tokens_of(dve, t), P)
        if later(t):
            dve.wait_ge(f["bonus"].sem, f["bonus"].last(t))
        S.apart(dve)
        nc.vector.tensor_tensor(KS, C.A[:, 0, :, at], C.A[:, 1, :, at], ALU.add).then_inc(f["a_sum"].sem, 1)
        dve.wait_ge(f["a_sum"].sem, f["a_sum"].at(t))
        for p in range(NP):
            ins = nc.vector.tensor_scalar(KS[:, p, :], KS[:, p, :], S.PT[:, ka + p:ka + p + 1], coef[:, 0, p:p + 1],
                                          ALU.mult, ALU.add)
        ins.then_inc(f["k_scale"].sem, 1)
        dve.wait_ge(f["k_scale"].sem, f["k_scale"].at(t))
        nc.vector.tensor_tensor(KS, KS, S.Z[:, 3:6, at], ALU.mult).then_inc(f["k_both"].sem, 1)
        dve.wait_ge(f["k_both"].sem, f["k_both"].at(t))
        for p in range(NP):
            ins = nc.vector.scalar_tensor_tensor(out=M[:, p, :], in0=KS[:, p, :], scalar=S.PT[:, rk + p:rk + p + 1],
                                                 in1=S.Z[:, p, at], op0=ALU.mult, op1=ALU.mult)
        ins.then_inc(f["r_k"].sem, 1)

    def spread_dve(dve, t):
        S.apart(dve)
        norm.spread(dve, t, C.Y[:, ds(t, 1), :].rearrange("p a (h c) -> p (a h) c", h=H), SQ)

    def step_dve(dve, t, after):
        at = ds(tokens_of(dve, t), P)
        norm.divide(dve, t, YN)
        if after is not None:
            spread_dve(dve, after)
        dve.wait_ge(f["bonus"].sem, f["bonus"].at(t))
        if later(t):
            dve.wait_ge(f["normed_v"].sem, f["normed_v"].last(t))
        nc.vector.tensor_tensor(BV, S.Z[:, 6:9, at], S.PS[1][:, 0:3 * P].rearrange("p (h t) -> p h t", h=3),
                                ALU.mult).then_inc(f["bonus_v"].sem, 1)
        dve.wait_ge(f["bonus_v"].sem, f["bonus_v"].at(t))
        dve.wait_ge(f["turned"].sem, f["turned"].at(t))
        for p in range(NP):
            ins = nc.vector.scalar_tensor_tensor(out=OUT[:, p, :], in0=S.PS[2][:, p * P:(p + 1) * P],
                                                 scalar=S.PT[:, lng + p:lng + p + 1], in1=BV[:, p, :],
                                                 op0=ALU.mult, op1=ALU.add)
        ins.then_inc(f["normed_v"].sem, 1)
        if after is not None:
            front_dve(dve, after)
        dve.wait_ge(f["normed_v"].sem, f["normed_v"].at(t))
        dve.wait_ge(f["gate"].sem, f["gate"].at(t))
        nc.vector.tensor_tensor(S.YT[:, 5:8, at], OUT,
                                S.PS[0][:, 0:3 * P].rearrange("p (h t) -> p h t", h=3), ALU.mult).then_inc(
                                    f["stored"].sem, 1)

    with nc.Block() as block:
        @block.sync
        def _(sp):
            sp.dma_start(G2, io["rwkv_g2"][0]).then_inc(loaded.sem, 16)

        @block.tensor
        def _(pe):
            pe.wait_ge(loaded.sem, loaded.at())
            round_pe(pe, 0)
            with pe.Fori(1, NT) as t:
                round_pe(pe, t)

        @block.scalar
        def _(act):
            act.preload_act_table_set(EXP_LN)
            norm.scalar(act, 0)
            with act.Fori(1, NT) as t:
                norm.scalar(act, t)

        @block.vector
        def _(dve):
            nc.vector.tensor_scalar(coef[:, 0, :], C.one_ka[:, :], 2.0, None, ALU.mult).then_inc(ready.sem, 1)
            dve.wait_ge(ready.sem, ready.at())
            front_dve(dve, 0)
            spread_dve(dve, 0)
            tiles_ahead(dve, step_dve)


def residual(S, dve, dense, r, slot, blk, col):
    nc = S.nc
    for g in range(NG):
        dve.wait_ge(dense.summed.sem, dense.filled(r, slot, g))
        parts = ((0, N_CTX, 0), (N_CTX, GRP, 1)) if g == 0 else ((0, GRP, 1),)
        for a, b, c in parts:
            x = S.XT[:, ds(blk, 1), g * GRP + a:g * GRP + b].rearrange("p a n -> p (a n)")
            ins = nc.vector.scalar_tensor_tensor(
                out=x, in0=S.PS[3 * slot + g][:, a:b], scalar=S.MOD[:, ds(col, 1), c:c + 1].rearrange("p a b -> p (a b)"),
                in1=x, op0=ALU.mult, op1=ALU.add)
        ins.then_inc(dense.drained[g].sem, 1)


def project_out(S):
    nc, io = S.nc, S.io
    dense = Dense(S, "o", slabs([lambda x: x[:, 8, :], lambda x: x[:, 9, :]], (S.Z, S.Zr)))
    restored = S.flag("residual_restored", 16)
    split, left = S.flag("branches_rounded", KB), S.flag("branches_left", KB)
    w = io["w_out"][0].rearrange("(k p) n -> p k n", p=P)
    with nc.Block() as block:
        @block.gpsimd
        def _(pool):
            dense.start(pool)
            with pool.Fori(0, 4) as i:
                for slot in range(2):
                    dense.divide(pool, i, slot)

        @block.scalar
        def _(act):
            for k in range(KB):
                nc.scalar.copy(S.HTr[:, k, :], S.YT[:, k, :]).then_inc(split.sem, 1)

        @block.sync
        def _(sp):
            for slot in range(2):
                dense.load(sp, 0, slot, w[:, :, slot * P:(slot + 1) * P])
            sp.dma_start(S.XT[:, :, :], S.x_dram).then_inc(restored.sem, 16)
            with sp.Fori(1, 4) as i:
                for slot in range(2):
                    dense.load(sp, i, slot, w[:, :, ds(i * 256 + slot * P, P)])

        @block.tensor
        def _(pe):
            pe.wait_ge(left.sem, left.at())
            with pe.Fori(0, 4) as i:
                for slot in range(2):
                    dense.multiply(pe, i, slot, group(S.HTr), group(S.YTr))

        @block.vector
        def _(dve):
            for k in range(KB):
                dve.wait_ge(split.sem, split.at(0, k + 1))
                nc.vector.tensor_tensor(S.YTr[:, k, :], S.YT[:, k, :], plain(S.HTr[:, k, :]), ALU.subtract).then_inc(
                    left.sem, 1)
            dve.wait_ge(restored.sem, restored.at())
            with dve.Fori(0, 4) as i:
                for slot in range(2):
                    blk = dve.snap(i * 2 + slot, min_val=0, max_val=KB - 1)
                    col = dve.snap(i * 2 + (slot + 2 * KB), min_val=0, max_val=N_MOD * KB - 1)
                    residual(S, dve, dense, i, slot, blk, col)


def mlp(S):
    nc, io = S.nc, S.io
    HB = 4
    n_q = D_FF // (HB * P)
    UP, DOWN = HB // 2, KB // 2
    up = Dense(S, "up", slabs([lambda x: x[:, 8, :], lambda x: x[:, 9, :]], (S.Z, S.Zr)))
    rows = [lambda x: x[:, 10, :], lambda x: x[:, 11, :]]
    down = Dense(S, "down", slabs(rows, (S.Z, S.Zr), HB), slabs(rows, (S.Zr,), HB, HB * P)[0], HB)
    w1 = io["mlp_w1"][0].rearrange("(k p) n -> p k n", p=P)
    w2 = io["mlp_w2"][0].rearrange("(q k p) n -> p q k n", p=P, k=HB)
    R = [x[:, 0:T] for x in S.PAD[0:2]]
    squared, kept = S.flag("relu_squared", 2 * NG), S.flag("hidden_rounded", 2 * NG)
    hidden = S.flag("hidden_left", 2 * NG, in_hand=2 * NG)

    def blocks(eng, i, slot):
        return (eng.snap(i * 2 + slot, min_val=0, max_val=HB - 1),
                eng.snap(i * 2 + (slot + HB), min_val=HB, max_val=2 * HB - 1))

    def part(x, blk, g):
        return x[:, ds(blk, 1), g * GRP:(g + 1) * GRP].rearrange("p a n -> p (a n)")

    with nc.Block() as block:
        @block.sync
        def _(sp):
            up.start(sp)
            down.start(sp)
            sp.sem_inc(hidden.sem, hidden.in_hand)
            with sp.Fori(0, n_q) as q:
                with sp.Fori(0, UP) as i:
                    r = sp.snap(q * UP + i, min_val=0, max_val=UP * n_q - 1)
                    for slot in range(2):
                        up.load(sp, r, slot, w1[:, :, ds(q * (HB * P) + i * 256 + slot * P, P)])
                with sp.Fori(0, DOWN) as i:
                    r = sp.snap(q * DOWN + i, min_val=0, max_val=DOWN * n_q - 1)
                    for slot in range(2):
                        down.load(sp, r, slot,
                                  w2[:, ds(q, 1), :, ds(i * 256 + slot * P, P)].rearrange("p q k n -> p (q k) n"))

        @block.gpsimd
        def _(pool):
            with pool.Fori(0, n_q) as q:
                with pool.Fori(0, UP) as i:
                    r = pool.snap(q * UP + i, min_val=0, max_val=UP * n_q - 1)
                    for slot in range(2):
                        up.divide(pool, r, slot)
                with pool.Fori(0, DOWN) as i:
                    r = pool.snap(q * DOWN + i, min_val=0, max_val=DOWN * n_q - 1)
                    for slot in range(2):
                        down.divide(pool, r, slot)

        @block.tensor
        def _(pe):
            with pe.Fori(0, n_q) as q:
                with pe.Fori(0, UP) as i:
                    r = pe.snap(q * UP + i, min_val=0, max_val=UP * n_q - 1)

                    def left(g):
                        pe.wait_ge(down.drained[g].sem, down.drained[g].at(q * DOWN, 0))
                    for slot in range(2):
                        up.multiply(pe, r, slot, group(S.HTr), group(S.Zr), left)
                with pe.Fori(0, DOWN) as i:
                    r = pe.snap(q * DOWN + i, min_val=0, max_val=DOWN * n_q - 1)

                    def kept_up(g):
                        pe.wait_ge(up.drained[g].sem, up.drained[g].at(q * UP + (UP - 1)))
                        pe.wait_ge(hidden.sem, hidden.at(q * UP + (UP - 1), NG + g + 1))
                    for slot in range(2):
                        down.multiply(pe, r, slot, group(S.YTr), group(S.YTr, HB), kept_up)

        @block.scalar
        def _(act):
            with act.Fori(0, n_q) as q:
                with act.Fori(0, UP) as i:
                    r = act.snap(q * UP + i, min_val=0, max_val=UP * n_q - 1)
                    for slot in range(2):
                        blk, _ = blocks(act, i, slot)
                        for g in range(NG):
                            n = NG * slot + g + 1
                            act.wait_ge(hidden.sem, hidden.last(r, n))
                            act.wait_ge(up.summed.sem, up.filled(r, slot, g))
                            nc.scalar.activation(R[slot][:, g * GRP:(g + 1) * GRP], up.bank(slot, g),
                                                 ACT.Relu).then_inc(up.drained[g].sem, 1)
                            for d in down.drained:
                                act.wait_ge(d.sem, d.at(q * DOWN, 0))
                            act.wait_ge(squared.sem, squared.at(r, n))
                            S.apart(act)
                            nc.scalar.copy(part(S.YTr, blk, g), R[slot][:, g * GRP:(g + 1) * GRP]).then_inc(kept.sem, 1)

        @block.vector
        def _(dve):
            with dve.Fori(0, n_q) as q:
                with dve.Fori(0, UP) as i:
                    r = dve.snap(q * UP + i, min_val=0, max_val=UP * n_q - 1)
                    for slot in range(2):
                        blk, low = blocks(dve, i, slot)
                        for g in range(NG):
                            n = NG * slot + g + 1
                            x = R[slot][:, g * GRP:(g + 1) * GRP]
                            dve.wait_ge(up.drained[g].sem, up.drained[g].at(r, slot + 1))
                            nc.vector.tensor_tensor(x, x, x, ALU.mult).then_inc(squared.sem, 1)
                            dve.wait_ge(kept.sem, kept.at(r, n))
                            S.apart(dve)
                            nc.vector.tensor_tensor(part(S.YTr, low, g), x, plain(part(S.YTr, blk, g)),
                                                    ALU.subtract).then_inc(hidden.sem, 1)
                with dve.Fori(0, DOWN) as i:
                    r = dve.snap(q * DOWN + i, min_val=0, max_val=DOWN * n_q - 1)
                    for slot in range(2):
                        blk = dve.snap(i * 2 + slot, min_val=0, max_val=KB - 1)
                        col = dve.snap(i * 2 + (slot + 5 * KB), min_val=0, max_val=N_MOD * KB - 1)
                        residual(S, dve, down, r, slot, blk, col)


def leave(S):
    nc = S.nc
    ST = [S.HT[:, i, 0:KB * P].rearrange("p (k n) -> p k n", k=KB) for i in range(2)]
    OUT = [S.HT[:, 2 + i, 0:D] for i in range(2)]
    scaled = [S.flag(f"leave_scaled{i}") for i in range(2)]
    turned = [S.flag(f"leave_turned{i}", 1, in_hand=1) for i in range(2)]
    copied = [S.flag(f"leave_copied{i}", 1, in_hand=1) for i in range(2)]
    stored = [S.flag(f"leave_stored{i}", 16, in_hand=16) for i in range(2)]

    def over_tiles(eng, body):
        body(0, 0, 0)
        with eng.Fori(1, NT // 2 + 1) as i:
            body(eng.snap(i * 2 - 1, min_val=1, max_val=NT - 1), 1, eng.snap(i - 1, min_val=0, max_val=NT))
            body(eng.snap(i * 2, min_val=1, max_val=NT - 1), 0, i)

    with nc.Block() as block:
        @block.gpsimd
        def _(pool):
            for fl in (turned, copied, stored):
                for x in fl:
                    pool.sem_inc(x.sem, x.in_hand)

        @block.vector
        def _(dve):
            def body(t, s, j):
                tok = 0 if isinstance(t, int) else dve.snap(t * P, min_val=0, max_val=T - P)
                dve.wait_ge(turned[s].sem, turned[s].last(j))
                for k in range(KB):
                    ins = nc.vector.scalar_tensor_tensor(out=ST[s][:, k, :], in0=S.XT[:, k, ds(tok, P)],
                                                         scalar=S.param("final_g", k, 1), in1=S.RS[:, ds(tok, P)],
                                                         op0=ALU.mult, op1=ALU.mult)
                ins.then_inc(scaled[s].sem, 1)
            over_tiles(dve, body)

        @block.tensor
        def _(pe):
            def body(t, s, j):
                pe.wait_ge(scaled[s].sem, scaled[s].at(j))
                pe.wait_ge(copied[s].sem, copied[s].last(j))
                for k in range(KB):
                    tr = nc.tensor.transpose(S.PS[2 * s + k // 4][:, (k % 4) * P:(k % 4 + 1) * P], ST[s][:, k, :],
                                             S.ident[:, :])
                tr.then_inc(turned[s].sem, 1)
            over_tiles(pe, body)

        @block.scalar
        def _(act):
            def body(t, s, j):
                act.wait_ge(turned[s].sem, turned[s].at(j))
                act.wait_ge(stored[s].sem, stored[s].last(j))
                for b in range(2):
                    ins = nc.scalar.copy(OUT[s][:, b * 512:(b + 1) * 512], S.PS[2 * s + b][:, :])
                ins.then_inc(copied[s].sem, 1)
            over_tiles(act, body)

        @block.sync
        def _(sp):
            def body(t, s, j):
                sp.wait_ge(copied[s].sem, copied[s].at(j))
                if isinstance(t, int):
                    dst = S.out[0][0]
                else:
                    dst = S.out[1][0, ds(t * P - P, P), :]
                sp.dma_start(dst, OUT[s]).then_inc(stored[s].sem, 16)
            over_tiles(sp, body)
            sp.wait_ge(stored[0].sem, stored[0].at(NT // 2))
            sp.wait_ge(stored[1].sem, stored[1].at(NT // 2 - 1))


def program(nc, io, out):
    with ExitStack() as ctx:
        S = Store(nc, ctx, io, out)
        allocate(S)
        S.always = ctx.enter_context(nc.semaphore("always"))
        S.x_dram = nc.dram_tensor("residual", (P, KB, T), F32, kind="Internal").ap()
        S.low_dram = nc.dram_tensor("low_part", (P, KB, T), F32, kind="Internal").ap()
        S.RS, S.RSr = S.sb2("RS", P, T)
        nc.scalar.preload_act_table_set(EXP_LN)
        setup(S)
        enter(S)
        S.low_saved = S.flag("low_part_saved", 16)
        modulate(S, "n1", 0, S.XT, S.XTr)
        project_a(S)
        branch_a(S)
        S.release()
        project_b(S)
        B = StoreB(S)
        gates_b(S, B)
        recur_b(S, B)
        finish_b(S, B)
        S.release()
        project_c(S)
        C = StoreC(S)
        prepare_c(S, C)
        recur_c(S, C)
        S.release()
        finish_c(S, C)
        project_out(S)
        square_sums(S, "n2")
        modulate(S, "n2", 1, S.Z, S.Zr)
        S.release()
        mlp(S)
        square_sums(S, "fin")
        leave(S)


def kernel(**inputs):
    import numpy as _np
    import concourse.bacc as _bacc
    from concourse import mybir as _mybir
    from concourse.bass_utils import run_bass_kernel_spmd as _run

    nc = _bacc.Bacc("TRN2", target_bir_lowering=False, num_devices=1)
    arrays, io = {}, {}
    for name, (shape, _) in SHAPES.items():
        a = _np.ascontiguousarray(inputs[name])
        arrays["in_" + name] = a
        io[name] = nc.dram_tensor("in_" + name, shape, _mybir.dt.from_np(a.dtype), kind="ExternalInput").ap()
    out = [nc.dram_tensor(f"out_{i}", s, _mybir.dt.float32, kind="ExternalOutput").ap() for i, s in enumerate(OUTS)]
    program(nc, io, out)
    r = _run(nc, [arrays], core_ids=[0])
    return tuple(r.results[0][f"out_{i}"] for i in range(len(OUTS)))
```
